# Optimizing a Trainium2 kernel written in Bass

```python
import functools
import jax, jax.numpy as jnp
from jax import lax
import numpy as np

D_MODEL = 1024
BATCH = 1
SEQ = 512
DEPTH = 1
DEC_BATCH = 8
DEC_SEQ = 1
PAST_LEN = 1024
PAGE_SIZE = 128

H_RET = 8
HD_RET = D_MODEL // 16
RET_CHUNK = 128
RET_THETA = 10000.0
H_NSA = 8
G_NSA = 2
R_NSA = H_NSA // G_NSA
HD_NSA = D_MODEL // 16
CMP_BLK = 64
N_SEL = 16
WINDOW = 512
WIN_QBLK = 128
SEL_QCH = 32
SEL_FORCE = 1.0e4
ROPE_THETA = 500000.0
ROPE_DIMS = HD_NSA // 4
N_MEM = 256
H_MEM = 4
HD_MEM = D_MODEL // 8
PEER_KEYS = 128
PEER_HEADS = 8
PEER_DKEY = 128
PEER_TOPK = 16
PEER_CHUNK = 256
N_EXPERTS = PEER_KEYS * PEER_KEYS
EPS = 1e-6

D_RET = H_RET * HD_RET
D_NSA = H_NSA * HD_NSA
D_MIX = D_RET + D_NSA
D_KV = G_NSA * HD_NSA
D_IN = 4 * D_RET + D_NSA + 6 * D_KV + 3 * H_NSA

kernel_name = 'hymba_retnet_nsa_peer_step'

def rms_norm(x, g):
    xf = x.astype(jnp.float32)
    y = xf * lax.rsqrt(jnp.mean(xf * xf, axis=-1, keepdims=True) + EPS)
    return (y * g.astype(jnp.float32)).astype(x.dtype)

def rotary(x, pos, n_rot, theta):
    half = n_rot // 2
    inv = theta ** (-jnp.arange(half, dtype=jnp.float32) / half)
    ang = pos.astype(jnp.float32)[:, None] * inv[None, :]
    cos = jnp.cos(ang)[None, :, None, :]
    sin = jnp.sin(ang)[None, :, None, :]
    xf = x.astype(jnp.float32)
    x1, x2 = xf[..., :half], xf[..., half:n_rot]
    out = jnp.concatenate([x1 * cos - x2 * sin, x1 * sin + x2 * cos, xf[..., n_rot:]], axis=-1)
    return out.astype(x.dtype)

def masked_softmax(s, mask):
    s = jnp.where(mask, s.astype(jnp.float32), -jnp.inf)
    m = jnp.max(s, axis=-1, keepdims=True)
    m = jnp.where(jnp.isfinite(m), m, 0.0)
    p = jnp.exp(s - m)
    return p / jnp.maximum(jnp.sum(p, axis=-1, keepdims=True), 1e-30)

def mixer_projections(hn, pos, w_in):
    B, L, _ = hn.shape
    sizes = [D_RET] * 4 + [D_NSA] + [D_KV] * 6 + [3 * H_NSA]
    cuts = np.cumsum(sizes)[:-1].tolist()
    rq, rk, rv, rg, nq, ck, cv, sk, sv, wk, wv, ng = jnp.split(hn @ w_in, cuts, axis=-1)
    ret_heads = lambda t: t.reshape(B, L, H_RET, HD_RET)
    rq = rotary(ret_heads(rq), pos, HD_RET, RET_THETA).astype(jnp.float32)
    rk = rotary(ret_heads(rk), pos, HD_RET, RET_THETA).astype(jnp.float32) * (HD_RET ** -0.5)
    rv = ret_heads(rv).astype(jnp.float32)
    nq = rotary(nq.reshape(B, L, H_NSA, HD_NSA), pos, ROPE_DIMS, ROPE_THETA)
    nq = nq.reshape(B, L, G_NSA, R_NSA, HD_NSA)

    def kv_rows(t, rotate):
        t = t.reshape(B, L, G_NSA, HD_NSA)
        if rotate:
            t = rotary(t, pos, ROPE_DIMS, ROPE_THETA)
        return t.transpose(0, 2, 1, 3)

    ck, sk, wk = (kv_rows(t, True) for t in (ck, sk, wk))
    cv, sv, wv = (kv_rows(t, False) for t in (cv, sv, wv))
    gates = jax.nn.sigmoid(ng.astype(jnp.float32)).reshape(B, L, G_NSA, R_NSA, 3)
    return rq, rk, rv, rg, nq, ck, cv, sk, sv, wk, wv, gates

def retention(q, k, v, s0):
    B, L, H, d = q.shape
    C = RET_CHUNK if L % RET_CHUNK == 0 else L
    nC = L // C
    lg = jnp.log(1.0 - 2.0 ** (-5.0 - jnp.arange(H, dtype=jnp.float32)))
    idx = jnp.arange(C, dtype=jnp.float32)
    diff = idx[:, None] - idx[None, :]
    dmat = jnp.where(diff >= 0, jnp.exp(lg[:, None, None] * jnp.maximum(diff, 0.0)), 0.0)
    xi = jnp.exp(lg[None, :] * (idx[:, None] + 1.0))
    zeta = jnp.exp(lg[:, None] * (C - 1.0 - idx[None, :]))
    g_c = jnp.exp(lg * C)
    to_chunks = lambda t: t.reshape(B, nC, C, H, d).transpose(1, 0, 2, 3, 4)

    def step(S, inp):
        qc, kc, vc = inp
        att = jnp.einsum('bihd,bjhd->bhij', qc, kc) * dmat[None]
        inner = jnp.einsum('bhij,bjhe->bihe', att, vc)
        cross = jnp.einsum('bihd,bhde->bihe', qc, S) * xi[None, :, :, None]
        S = S * g_c[None, :, None, None] + jnp.einsum('bjhd,bjhe,hj->bhde', kc, vc, zeta)
        return S, inner + cross

    S, o = lax.scan(step, s0, (to_chunks(q), to_chunks(k), to_chunks(v)))
    return o.transpose(1, 0, 2, 3, 4).reshape(B, L, H, d), S

def head_group_norm(o, g):
    B, L, H, d = o.shape
    mu = jnp.mean(o, axis=-1, keepdims=True)
    var = jnp.mean(jnp.square(o - mu), axis=-1, keepdims=True)
    return ((o - mu) * lax.rsqrt(var + EPS)).reshape(B, L, H * d) * g.astype(jnp.float32)

def compress(rows, w, b):
    return jnp.einsum('...jd,jde->...e', rows, w) + b

def cmp_attend(q, q_pos, ck, cv):
    nb = ck.shape[2]
    s = jnp.einsum('bqgrd,bgnd->bqgrn', q, ck).astype(jnp.float32) * (HD_NSA ** -0.5)
    blk_end = jnp.arange(nb) * CMP_BLK + CMP_BLK - 1
    vis = blk_end[None, :] <= q_pos[:, None]
    p = masked_softmax(s, vis[None, :, None, None, :])
    o = jnp.einsum('bqgrn,bgnd->bqgrd', p.astype(cv.dtype), cv)
    return o, jnp.sum(p, axis=3), vis

def select_blocks(imp, vis, q_pos):
    nb = imp.shape[-1]
    n_sel = min(N_SEL, nb)
    blk = jnp.arange(nb)
    forced = (blk[None, :] == 0) | (blk[None, :] == (q_pos[:, None] // CMP_BLK))
    score = jnp.where(forced[None, :, None, :], SEL_FORCE, jnp.where(vis[None, :, None, :], imp, -1.0))
    top, idx = lax.top_k(score, n_sel)
    return idx, top >= 0.0

def sel_attend(q, q_pos, idx, valid, gather):
    kb, vb = gather(idx)
    kpos = idx[..., None] * CMP_BLK + jnp.arange(CMP_BLK)
    mask = valid[..., None] & (kpos <= q_pos[None, :, None, None, None])
    s = jnp.einsum('bqgrd,bqgnkd->bqgrnk', q, kb).astype(jnp.float32) * (HD_NSA ** -0.5)
    B, Lq, G, R, n, K = s.shape
    p = masked_softmax(s.reshape(B, Lq, G, R, n * K), mask.reshape(B, Lq, G, 1, n * K))
    return jnp.einsum('bqgrm,bqgmd->bqgrd', p.astype(vb.dtype), vb.reshape(B, Lq, G, n * K, HD_NSA))

def win_attend(q, q_pos, k, v, k_pos):
    s = jnp.einsum('bqgrd,bgkd->bqgrk', q, k).astype(jnp.float32) * (HD_NSA ** -0.5)
    dist = q_pos[:, None] - k_pos[None, :]
    mask = (dist >= 0) & (dist < WINDOW) & (k_pos[None, :] >= 0)
    p = masked_softmax(s, mask[None, :, None, None, :])
    return jnp.einsum('bqgrk,bgkd->bqgrd', p.astype(v.dtype), v)

def nsa_prompt(nq, ck, cv, sk, sv, wk, wv, cw, cb, pos):
    B, L = nq.shape[:2]
    nb = L // CMP_BLK
    blocks = lambda t: t.reshape(B, G_NSA, nb, CMP_BLK, HD_NSA)
    cK = compress(blocks(ck), cw[0], cb[0])
    cV = compress(blocks(cv), cw[1], cb[1])
    o_cmp, imp, vis = cmp_attend(nq, pos, cK, cV)
    idx, valid = select_blocks(imp, vis, pos)
    kb, vb = blocks(sk), blocks(sv)
    bi = jnp.arange(B)[:, None, None, None]
    gi = jnp.arange(G_NSA)[None, None, :, None]
    gather = lambda i: (kb[bi, gi, i], vb[bi, gi, i])
    nqc = L // SEL_QCH
    chunk = lambda t: jnp.moveaxis(t.reshape((B, nqc, SEL_QCH) + t.shape[2:]), 1, 0)
    o_slc = lax.map(lambda a: sel_attend(a[0], a[1], a[2], a[3], gather),
                    (chunk(nq), pos.reshape(nqc, SEL_QCH), chunk(idx), chunk(valid)))
    o_slc = jnp.moveaxis(o_slc, 0, 1).reshape(B, L, G_NSA, R_NSA, HD_NSA)
    nqb = L // WIN_QBLK
    span = WINDOW + WIN_QBLK
    lpad = lambda t: jnp.pad(t, ((0, 0), (0, 0), (WINDOW, 0), (0, 0)))
    wkp, wvp = lpad(wk), lpad(wv)
    qb = jnp.moveaxis(nq.reshape(B, nqb, WIN_QBLK, G_NSA, R_NSA, HD_NSA), 1, 0)

    def band(args):
        i, qi = args
        start = i * WIN_QBLK
        kk = lax.dynamic_slice_in_dim(wkp, start, span, axis=2)
        vv = lax.dynamic_slice_in_dim(wvp, start, span, axis=2)
        return win_attend(qi, start + jnp.arange(WIN_QBLK), kk, vv, start - WINDOW + jnp.arange(span))

    o_win = jnp.moveaxis(lax.map(band, (jnp.arange(nqb), qb)), 0, 1).reshape(B, L, G_NSA, R_NSA, HD_NSA)
    to_pages = lambda t: t.reshape(B, G_NSA, L // PAGE_SIZE, PAGE_SIZE, HD_NSA).transpose(0, 2, 1, 3, 4)
    keep = min(WINDOW, L)
    new_state = (to_pages(ck), to_pages(cv), to_pages(sk), to_pages(sv), wk[:, :, L - keep:], wv[:, :, L - keep:])
    return o_cmp, o_slc, o_win, new_state

def nsa_sample(nq, ck, cv, sk, sv, wk, wv, cw, cb, pos, page_table, layer,
               pool_ck, pool_cv, pool_sk, pool_sv, win_k, win_v):
    DB, LS = nq.shape[:2]
    n_pages = page_table.shape[1]
    bpp = PAGE_SIZE // CMP_BLK
    nb_past = n_pages * bpp
    pad_n = (-LS) % CMP_BLK
    nnb = (LS + pad_n) // CMP_BLK

    def new_blocks(t):
        t = jnp.pad(t, ((0, 0), (0, 0), (0, pad_n), (0, 0)))
        return t.reshape(DB, G_NSA, nnb, CMP_BLK, HD_NSA)

    def past_compressed(pool, w, b):
        rows = pool[layer, page_table]
        rows = rows.reshape(DB, n_pages, G_NSA, bpp, CMP_BLK, HD_NSA)
        c = compress(rows, w, b)
        return c.transpose(0, 2, 1, 3, 4).reshape(DB, G_NSA, nb_past, HD_NSA)

    cK = jnp.concatenate([past_compressed(pool_ck, cw[0], cb[0]), compress(new_blocks(ck), cw[0], cb[0])], axis=2)
    cV = jnp.concatenate([past_compressed(pool_cv, cw[1], cb[1]), compress(new_blocks(cv), cw[1], cb[1])], axis=2)
    o_cmp, imp, vis = cmp_attend(nq, pos, cK, cV)
    idx, valid = select_blocks(imp, vis, pos)
    bi = jnp.arange(DB)[:, None, None, None]
    gi = jnp.arange(G_NSA)[None, None, :, None]
    offs = jnp.arange(CMP_BLK)

    def block_source(pool, new):
        nblocks = new_blocks(new)

        def get(i):
            ip = jnp.minimum(i, nb_past - 1)
            page = page_table[bi, ip // bpp]
            row = ((ip % bpp) * CMP_BLK)[..., None] + offs
            past_rows = pool[layer, page[..., None], gi[..., None], row]
            new_rows = nblocks[bi, gi, jnp.clip(i - nb_past, 0, nnb - 1)]
            return jnp.where((i < nb_past)[..., None, None], past_rows, new_rows)
        return get

    get_k, get_v = block_source(pool_sk, sk), block_source(pool_sv, sv)
    o_slc = sel_attend(nq, pos, idx, valid, lambda i: (get_k(i), get_v(i)))
    wb = win_k.shape[2]
    kw = jnp.concatenate([win_k, wk], axis=2)
    vw = jnp.concatenate([win_v, wv], axis=2)
    o_win = win_attend(nq, pos, kw, vw, PAST_LEN - wb + jnp.arange(wb + LS))
    keep = min(WINDOW, wb + LS)
    new_state = (ck, cv, sk, sv, kw[:, :, wb + LS - keep:], vw[:, :, wb + LS - keep:])
    return o_cmp, o_slc, o_win, new_state

def mixer_output(o_ret, rg, gn_g, o_cmp, o_slc, o_win, gates, w_out):
    B, L = rg.shape[:2]
    y_ret = jax.nn.silu(rg.astype(jnp.float32)) * head_group_norm(o_ret, gn_g)
    o_nsa = gates[..., 0:1] * o_cmp + gates[..., 1:2] * o_slc + gates[..., 2:3] * o_win
    cat = jnp.concatenate([y_ret, o_nsa.reshape(B, L, D_NSA)], axis=-1)
    return cat.astype(w_out.dtype) @ w_out

def mem_kv(mem, g, w_mk, w_mv):
    Bm, M, _ = mem.shape
    m = rms_norm(mem, g)
    return (m @ w_mk).reshape(Bm, M, H_MEM, HD_MEM), (m @ w_mv).reshape(Bm, M, H_MEM, HD_MEM)

def mem_attend(hn, mk, mv, w_mq, w_mo):
    B, L, _ = hn.shape
    q = (hn @ w_mq).reshape(B, L, H_MEM, HD_MEM)
    s = jnp.einsum('blhd,bmhd->bhlm', q, mk).astype(jnp.float32) * (HD_MEM ** -0.5)
    p = jax.nn.softmax(s, axis=-1).astype(mv.dtype)
    o = jnp.einsum('bhlm,bmhd->blhd', p, mv).reshape(B, L, H_MEM * HD_MEM)
    return o @ w_mo

def peer_ffn(hn, wq, subkeys, u, v):
    B, L, D = hn.shape
    n = B * L
    pad = (-n) % PEER_CHUNK
    t = jnp.pad(hn.reshape(n, D), ((0, pad), (0, 0))).reshape(-1, PEER_CHUNK, D)

    def chunk(xc):
        q = (xc @ wq).reshape(PEER_CHUNK, PEER_HEADS, 2, PEER_DKEY // 2)
        s = jnp.einsum('chpd,hpkd->chpk', q, subkeys).astype(jnp.float32)
        s1, i1 = lax.top_k(s[:, :, 0], PEER_TOPK)
        s2, i2 = lax.top_k(s[:, :, 1], PEER_TOPK)
        cand = (s1[..., :, None] + s2[..., None, :]).reshape(PEER_CHUNK, PEER_HEADS, PEER_TOPK * PEER_TOPK)
        cidx = (i1[..., :, None] * PEER_KEYS + i2[..., None, :]).reshape(PEER_CHUNK, PEER_HEADS, PEER_TOPK * PEER_TOPK)
        top, sel = lax.top_k(cand, PEER_TOPK)
        expert = jnp.take_along_axis(cidx, sel, axis=-1)
        g = jax.nn.softmax(top, axis=-1)
        act = jax.nn.gelu(jnp.einsum('cd,chkd->chk', xc, u[expert]).astype(jnp.float32))
        return jnp.einsum('chk,chkd->cd', (g * act).astype(v.dtype), v[expert])

    out = lax.map(chunk, t).reshape(-1, D)[:n]
    return out.reshape(B, L, D)

def trunk_layer(h, pos, s0, nsa_fn, mk, mv, lw):
    g_mix, w_in, gn_g, w_out, g_mem, w_mq, w_mo, g_ffn, p_wq, p_keys, p_u, p_v = lw
    hn = rms_norm(h, g_mix)
    rq, rk, rv, rg, nq, ck, cv, sk, sv, wk, wv, gates = mixer_projections(hn, pos, w_in)
    o_ret, s_new = retention(rq, rk, rv, s0)
    o_cmp, o_slc, o_win, nsa_state = nsa_fn(nq, ck, cv, sk, sv, wk, wv)
    h = h + mixer_output(o_ret, rg, gn_g, o_cmp, o_slc, o_win, gates, w_out).astype(h.dtype)
    h = h + mem_attend(rms_norm(h, g_mem), mk, mv, w_mq, w_mo).astype(h.dtype)
    h = h + peer_ffn(rms_norm(h, g_ffn), p_wq, p_keys, p_u, p_v).astype(h.dtype)
    return h, s_new, nsa_state

def setup_inputs(seed: int = 0) -> dict:
    key = jax.random.key(seed)
    keys = jax.random.split(key, 40)
    f32 = jnp.float32
    n_pages = PAST_LEN // PAGE_SIZE
    n_used = DEC_BATCH * n_pages
    n_phys = n_used + n_used // 4
    win_buf = min(WINDOW, PAST_LEN)
    nrm = lambda i, shape, scale: jax.random.normal(keys[i], shape, f32) * scale
    gain = lambda i, shape: 1.0 + 0.05 * jax.random.normal(keys[i], shape, f32)
    page_table = jax.random.permutation(keys[0], n_phys)[:n_used].reshape(DEC_BATCH, n_pages).astype(jnp.int32)
    pool = (DEPTH, n_phys, G_NSA, PAGE_SIZE, HD_NSA)
    return {
        'x_prompt': nrm(1, (BATCH, SEQ, D_MODEL), 1.0),
        'x_sample': nrm(2, (DEC_BATCH, DEC_SEQ, D_MODEL), 1.0),
        'mem_prompt': nrm(3, (BATCH, N_MEM, D_MODEL), 1.0),
        'state_ret': nrm(4, (DEPTH, DEC_BATCH, H_RET, HD_RET, HD_RET), 1.0),
        'cache_cmp_k': nrm(5, pool, 1.0),
        'cache_cmp_v': nrm(6, pool, 1.0),
        'cache_slc_k': nrm(7, pool, 1.0),
        'cache_slc_v': nrm(8, pool, 1.0),
        'cache_win_k': nrm(9, (DEPTH, DEC_BATCH, G_NSA, win_buf, HD_NSA), 1.0),
        'cache_win_v': nrm(10, (DEPTH, DEC_BATCH, G_NSA, win_buf, HD_NSA), 1.0),
        'cache_mem_k': nrm(11, (DEPTH, DEC_BATCH, N_MEM, H_MEM, HD_MEM), 1.0),
        'cache_mem_v': nrm(12, (DEPTH, DEC_BATCH, N_MEM, H_MEM, HD_MEM), 1.0),
        'page_table': page_table,
        'norm_mix_g': gain(13, (DEPTH, D_MODEL)),
        'w_in': nrm(14, (DEPTH, D_MODEL, D_IN), D_MODEL ** -0.5),
        'ret_gn_g': gain(15, (DEPTH, D_RET)),
        'cmp_w': nrm(16, (DEPTH, 2, CMP_BLK, HD_NSA, HD_NSA), (CMP_BLK * HD_NSA) ** -0.5),
        'cmp_b': nrm(17, (DEPTH, 2, HD_NSA), 0.02),
        'w_out': nrm(18, (DEPTH, D_MIX, D_MODEL), D_MIX ** -0.5),
        'norm_mem_g': gain(19, (DEPTH, D_MODEL)),
        'mem_norm_g': gain(20, (DEPTH, D_MODEL)),
        'w_mq': nrm(21, (DEPTH, D_MODEL, H_MEM * HD_MEM), D_MODEL ** -0.5),
        'w_mk': nrm(22, (DEPTH, D_MODEL, H_MEM * HD_MEM), D_MODEL ** -0.5),
        'w_mv': nrm(23, (DEPTH, D_MODEL, H_MEM * HD_MEM), D_MODEL ** -0.5),
        'w_mo': nrm(24, (DEPTH, H_MEM * HD_MEM, D_MODEL), (H_MEM * HD_MEM) ** -0.5),
        'norm_ffn_g': gain(25, (DEPTH, D_MODEL)),
        'peer_wq': nrm(26, (DEPTH, D_MODEL, PEER_HEADS * PEER_DKEY), D_MODEL ** -0.5),
        'peer_subkeys': nrm(27, (DEPTH, PEER_HEADS, 2, PEER_KEYS, PEER_DKEY // 2), (PEER_DKEY // 2) ** -0.5),
        'peer_u': nrm(28, (DEPTH, N_EXPERTS, D_MODEL), D_MODEL ** -0.5),
        'peer_v': nrm(29, (DEPTH, N_EXPERTS, D_MODEL), 0.5),
        'norm_final_g': gain(30, (D_MODEL,)),
    }

def reference(x_prompt, x_sample, mem_prompt, state_ret, cache_cmp_k, cache_cmp_v, cache_slc_k, cache_slc_v,
              cache_win_k, cache_win_v, cache_mem_k, cache_mem_v, page_table, norm_mix_g, w_in, ret_gn_g,
              cmp_w, cmp_b, w_out, norm_mem_g, mem_norm_g, w_mq, w_mk, w_mv, w_mo, norm_ffn_g,
              peer_wq, peer_subkeys, peer_u, peer_v, norm_final_g):
    B, L, _ = x_prompt.shape
    DB, LS, _ = x_sample.shape
    pos_p = jnp.arange(L, dtype=jnp.int32)
    pos_s = PAST_LEN + jnp.arange(LS, dtype=jnp.int32)
    hp, hs = x_prompt, x_sample
    p_ret, p_ck, p_cv, p_sk, p_sv, p_wk, p_wv, p_mk, p_mv = [], [], [], [], [], [], [], [], []
    s_ret, s_ck, s_cv, s_sk, s_sv, s_wk, s_wv = [], [], [], [], [], [], []
    for l in range(DEPTH):
        lw = (norm_mix_g[l], w_in[l], ret_gn_g[l], w_out[l], norm_mem_g[l], w_mq[l], w_mo[l],
              norm_ffn_g[l], peer_wq[l], peer_subkeys[l], peer_u[l], peer_v[l])
        mk, mv = mem_kv(mem_prompt, mem_norm_g[l], w_mk[l], w_mv[l])
        nsa_p = functools.partial(nsa_prompt, cw=cmp_w[l], cb=cmp_b[l], pos=pos_p)
        s0 = jnp.zeros((B, H_RET, HD_RET, HD_RET), jnp.float32)
        hp, sr, st = trunk_layer(hp, pos_p, s0, nsa_p, mk, mv, lw)
        p_ret.append(sr)
        p_mk.append(mk)
        p_mv.append(mv)
        for lst, a in zip((p_ck, p_cv, p_sk, p_sv, p_wk, p_wv), st):
            lst.append(a)
        nsa_s = functools.partial(nsa_sample, cw=cmp_w[l], cb=cmp_b[l], pos=pos_s, page_table=page_table,
                                  layer=l, pool_ck=cache_cmp_k, pool_cv=cache_cmp_v, pool_sk=cache_slc_k,
                                  pool_sv=cache_slc_v, win_k=cache_win_k[l], win_v=cache_win_v[l])
        hs, sr, st = trunk_layer(hs, pos_s, state_ret[l].astype(jnp.float32), nsa_s,
                                 cache_mem_k[l], cache_mem_v[l], lw)
        s_ret.append(sr)
        for lst, a in zip((s_ck, s_cv, s_sk, s_sv, s_wk, s_wv), st):
            lst.append(a)
    y_prompt = rms_norm(hp, norm_final_g)
    y_sample = rms_norm(hs, norm_final_g)
    stk = lambda xs: jnp.stack(xs, axis=0)
    return (y_prompt, y_sample, stk(p_ret), stk(p_ck), stk(p_cv), stk(p_sk), stk(p_sv), stk(p_wk), stk(p_wv),
            stk(p_mk), stk(p_mv), stk(s_ret), stk(s_ck), stk(s_cv), stk(s_sk), stk(s_sv), stk(s_wk), stk(s_wv))


_drawn_inputs = setup_inputs


def setup_inputs(seed=0):
    import zlib

    import numpy as np

    out = dict(_drawn_inputs(seed))
    spreads = {}
    factors = {'cmp_b': 2.94, 'norm_mem_g': 3.214}
    for name, (base, spread) in spreads.items():
        noise = np.random.default_rng([zlib.crc32(name.encode()), seed]).standard_normal(out[name].shape)
        drawn = base * np.exp(spread * noise) if base else spread * noise
        out[name] = __import__('jax').numpy.asarray(drawn.astype(out[name].dtype))
    for name, factor in factors.items():
        out[name] = (out[name] * factor).astype(out[name].dtype)
    return out
```

```python
from contextlib import ExitStack

import concourse.bass as bass
from concourse import mybir

ALU = mybir.AluOpType
ACT = mybir.ActivationFunctionType
AX = mybir.AxisListType
F32 = mybir.dt.float32
U32 = mybir.dt.uint32

P = 128
D = 1024
KC = D // P
SEQ = 512
PT = SEQ // P
DB = 8
NT = PT + 1
SAMPLE = PT
H = 8
HD = 64
G = 2
R4 = H // G
CMP = 64
PAST = 1024
PAGES = PAST // P
BG = DB * G
NMEM = 256
HM = 4
HDM = 128
NKEY = 128
TOPK = 16
SLOTS = H * TOPK
D_IN = 4 * 512 + 512 + 6 * P + 3 * H
C_RQ, C_RK, C_RV, C_RG, C_NQ, C_CK, C_CV, C_SK, C_SV, C_WK, C_WV, C_NG = (
    0, 512, 1024, 1536, 2048, 2560, 2688, 2816, 2944, 3072, 3200, 3328)
CHUNKS = [(c, min(512, D_IN - c)) for c in range(0, D_IN, 512)]
EPS = 1e-6
NEG = -1.0e30
RING = 16
TURNS = SLOTS // RING
GELU_A = 0.044715
GELU_B = 0.7978845608028654


def rows_of(t):
    return P if t < PT else DB


class Arena:

    def __init__(self, tensor, at, end):
        self.tensor, self.at, self.end = tensor, at, end

    def take(self, *shape):
        n = 1
        for s in shape:
            n *= s
        a = self.at
        self.at += n
        assert self.at <= self.end, (self.at, self.end)
        v = self.tensor[:, a:a + n]
        names = "abcd"[:len(shape)]
        if len(shape) > 1:
            v = v.rearrange(f"p ({' '.join(names)}) -> p {' '.join(names)}", **dict(zip(names, shape)))
        return v

    def part(self, off, size):
        return Arena(self.tensor, self.at + off, self.at + off + size)


def trunk_kernel(nc, a, c, out):
    with ExitStack() as ctx:
        def sb(name, shape, dt=F32):
            return ctx.enter_context(nc.sbuf_tensor(name, shape, dt))

        def sem(name):
            return ctx.enter_context(nc.semaphore(name))

        def scratch(name, shape):
            return nc.dram_tensor(name, shape, F32, kind="Internal").ap()

        banks = [ctx.enter_context(nc.psum_tensor(f"bank{i}", [P, 512], F32)) for i in range(8)]

        sc_heads = scratch("sc_heads", (5, DB, 512))
        sc_gates = scratch("sc_gates", (DB, 3 * H))
        sc_cv = scratch("sc_cv", (BG, HD))
        sc_cat = scratch("sc_cat", (2, DB, 512))
        sc_hn = scratch("sc_hn", (DB, D))

        words = 51900
        arena = sb("arena", [P, words])
        base = Arena(arena, 0, words)
        h = base.take(NT, D)
        gain = base.take(5, D)
        MIX, MEM, MEMN, FFN, FIN = range(5)
        gn_gain = base.take(512)
        gn_rows = base.take(HD)
        cmp_bv = base.take(HD)
        cmp_bk = base.take(1)
        ident = base.take(P)
        tri = base.take(P)
        decay = base.take(H, P)
        xi = base.take(H)
        zeta = base.take(H)
        g_chunk = base.take(H)
        gamma1 = base.take(1)
        cmp_vis = base.take(PT, H)
        cmp_neg = base.take(PT, H)
        rot_ret = base.take(NT, 2, 2, 32)
        rot_nsa = base.take(NT, 2, 8)
        own_neg = base.take(256)
        group = base.take(64)
        blk_excl = base.take(16)
        blk_rank = base.take(16)
        page_f = base.take(10)
        row_add = base.take(3)
        iota16 = base.take(16)
        eye8 = base.take(DB, DB)
        mean_sq = base.take(16)
        rstd = base.take(16)
        half_neg = base.take(H)
        gn_v = base.take(H)
        gn_r = base.take(H)
        neg_max = base.take(16)
        exp_sum = base.take(2, H)
        gate = base.take(3 * H)
        gate_w = base.take(H)
        drop_neg = base.take(16)
        c_kT = base.take(272)
        c_v = base.take(2, HD)
        c_vblk = base.take(512)
        col = base.take(160)
        blk_idx = sb("blk_idx", [P, 2], U32)
        row_idx = sb("row_idx", [P, BG], U32)
        page_i = sb("page_i", [P, 10], mybir.dt.int32)
        x0 = base.at
        XW = words - x0

        proj = [base.part(t * D_IN, D_IN).take(D_IN) for t in range(NT)]
        cat = base.part(NT * D_IN, NT * D).take(NT, D)
        r2 = NT * D_IN + NT * D
        R2W = XW - r2
        ar = base.part(r2, R2W)
        hnT = ar.take(KC, 520)
        hn_buf = ar.take(2, D)
        w_buf = ar.take(2, KC, 512)
        sq_junk = cat[:, 0, :]
        ar = base.part(r2, R2W)
        blk_buf = ar.take(2, CMP * HD)
        cmp_w = ar.take(2, 32, HD)
        blkT = ar.take(2, 4, P)
        cv_out = ar.take(HD)
        ar = base.part(r2, R2W)
        rqT = ar.take(H, P)
        rkT = ar.take(H, P)
        nqT = ar.take(H, P)
        kT = ar.take(2, G, SEQ)
        att = ar.take(H, P)
        probs = ar.take(2, SEQ)
        probsT = ar.take(2, SEQ)
        state = ar.take(H, HD)
        vz = ar.take(H, HD)
        tmp = ar.take(4, 512)
        rot_t = tmp
        tanh_rg = ar.take(512)
        cs_buf = ar.take(64)
        cp_buf = ar.take(64)
        cpT = ar.take(P)
        ar = base.part(0, NT * D_IN)
        key_rows = ar.take(BG, 512)
        val_rows = ar.take(BG, 512)
        ar = base.part(r2, R2W)
        s_state = ar.take(HD, HD)
        s_prod = ar.take(HD, HD)
        q_mask = ar.take(BG, 64)
        own_q = ar.take(BG, 64)
        keyT = ar.take(2, 512)
        s_prod_flat = s_prod.rearrange("p d e -> p (d e)")
        s_scores = s_prod_flat[:, 0:1028]
        s_probs = s_prod_flat[:, 1028:2056]
        s_rows = ar.take(12, HD)
        s_probsT = ar.take(8, 64)
        cmp_p = ar.take(256)
        cmp_pT = ar.take(2, 64)
        s_small = ar.take(256)
        s_o = ar.take(4, HD)
        sqT = ar.take(64)
        xa = base.part(0, NT * D_IN)
        w_mk = xa.take(KC, 512)
        w_mv = xa.take(KC, 512)
        mem_x = xa.take(2, D)
        ar = base.part(r2, R2W)
        hnT2 = ar.take(KC, 520)
        w_mq = ar.take(KC, 512)
        mT = ar.take(KC, NMEM)
        mv = ar.take(2, 512)
        mkT = ar.take(HM, NMEM)
        qT_m = ar.take(HM, 520)
        xa = base.part(0, NT * D_IN)
        w_out = xa.take(KC, D)
        catT = xa.take(2, KC, P)
        hn_buf2 = xa.take(2, D)
        sq_junk2 = xa.take(D)
        mk = xa.take(2, 512)
        xa = base.part(0, NT * D_IN)
        mem_k = xa.take(DB, D)
        mem_v = xa.take(DB, D)
        w_mo = base.part(NT * D_IN, NT * D).take(HM, D)
        ar = base.part(r2, R2W)
        oT_m = ar.take(HM, 520)
        m_probs = ar.take(2, NMEM)
        m_probsT = ar.take(2, NMEM)
        ar = base.part(r2 + KC * 520 + KC * 512, KC * NMEM)
        qm_mask = ar.take(32, 32)
        own_m = ar.take(32, 32)
        ar = base.part(r2 + KC * 520, KC * 512)
        mkT_s = ar.take(2, 512)
        ms_probs = ar.take(NMEM)
        ms_probsT = ar.take(2, 32)
        ar = base.part(0, XW)
        hn3 = ar.take(NT, D)
        gates_p = ar.take(NT, SLOTS)
        act_p = ar.take(SLOTS)
        act_turn = ar.take(RING)
        coef = ar.take(SLOTS)
        gtmp = ar.take(2, SLOTS)
        acc = ar.take(D)
        idx_s = ar.take(DB)
        gate_s = ar.take(DB)
        coef_m = ar.take(DB, DB)
        skT = ar.take(H, 256)
        ring_at = ar.at
        peer = Arena(arena, ring_at, words)
        ring = peer.take(RING, D)
        hn_s = peer.take(DB, D)
        peer = Arena(arena, ring_at, words)
        wq = peer.take(KC, D)
        hnT3 = peer.take(KC, 520)
        qT_p = peer.take(H, 520)
        sub_k = peer.take(H, P)
        sq_junk3 = peer.take(D)
        peer = Arena(arena, ring_at, words)
        s_all = peer.take(16, NKEY)
        cand = peer.take(H, 256)
        onehot = peer.take(SLOTS, 16)
        top_v = peer.take(16, TOPK)
        top_f = peer.take(16, TOPK)
        best_v = peer.take(H, TOPK)
        best_e = peer.take(H, TOPK)
        ab_f = peer.take(2, SLOTS)
        pick = peer.take(2, SLOTS)
        assert peer.at <= ring_at + KC * D
        top_i = sb("top_i", [P, 16, TOPK], U32)
        best_i = sb("best_i", [P, H, TOPK], U32)
        ab_i = sb("ab_i", [P, 2, SLOTS], U32)
        expert = sb("expert", [P, PT, SLOTS], U32)
        expert_s = sb("expert_s", [P, DB], U32)
        cursor = sb("cursor", [P, RING], U32)

        x_in = sem("x_in")
        consts_in = sem("consts_in")
        N_CONST = 0
        mean_ready = sem("mean_ready")
        rstd_ready = sem("rstd_ready")
        hn_ready = sem("hn_ready")
        hnT_done = sem("hnT_done")
        hnT_ready = sem("hnT_ready")
        w_in_loaded = [sem("w_in_even"), sem("w_in_odd")]
        proj_done = sem("proj_done")
        proj_ready = sem("proj_ready")
        rotated = sem("rotated")
        rows_stored = sem("rows_stored")
        idx_ready = sem("idx_ready")
        blk_in = [sem("blk_even"), sem("blk_odd")]
        own_blk_in = sem("own_blk_in")
        cmpw_in = sem("cmpw_in")
        blkT_done = sem("blkT_done")
        blkT_ready = sem("blkT_ready")
        cmp_done = sem("cmp_done")
        cmp_ready = sem("cmp_ready")
        cv_stored = sem("cv_stored")
        vblk_in = sem("vblk_in")
        vblk_zero = sem("vblk_zero")
        headT_done = sem("headT_done")
        headT_ready = sem("headT_ready")
        att_done = sem("att_done")
        att_ready = sem("att_ready")
        vz_ready = sem("vz_ready")
        ret_done = sem("ret_done")
        state_ready = sem("state_ready")
        cs_done = sem("cs_done")
        cs_ready = sem("cs_ready")
        cs_exp = sem("cs_exp")
        cp_ready = sem("cp_ready")
        cpT_done = sem("cpT_done")
        cpT_ready = sem("cpT_ready")
        co_done = sem("co_done")
        co_used = sem("co_used")
        sc_done = sem("sc_done")
        max_ready = sem("max_ready")
        exp_ready = sem("exp_ready")
        pT_done = sem("pT_done")
        pT_ready = sem("pT_ready")
        ao_done = sem("ao_done")
        ao_used = sem("ao_used")
        tanh_ready = sem("tanh_ready")
        gate_exp = sem("gate_exp")
        cat_ready = sem("cat_ready")
        state_stored = sem("state_stored")
        s_rows_in = sem("s_rows_in")
        s_state_in = sem("s_state_in")
        s_stored = sem("s_stored")
        s_cat_in = sem("s_cat_in")
        sT_done = sem("sT_done")
        sT_ready = sem("sT_ready")
        qmask_ready = sem("qmask_ready")
        key_in = [sem("page_keys_in"), sem("window_keys_in")]
        val_in = [sem("page_values_in"), sem("window_values_in")]
        gn_var = sem("gn_var")
        gn_rstd = sem("gn_rstd")
        s_keyT_done = sem("s_keyT_done")
        s_keyT_ready = sem("s_keyT_ready")
        s_sc_done = sem("s_sc_done")
        s_max = sem("s_max")
        s_exp = sem("s_exp")
        s_pT_done = sem("s_pT_done")
        s_pT_ready = sem("s_pT_ready")
        s_oT_done = sem("s_oT_done")
        s_oT_ready = sem("s_oT_ready")
        s_o_done = sem("s_o_done")
        s_imp = sem("s_imp")
        s_imp_done = sem("s_imp_done")
        s_branch = sem("s_branch")
        w_out_in = sem("w_out_in")
        catT_done = sem("catT_done")
        catT_ready = sem("catT_ready")
        out_done = sem("out_done")
        out_added = sem("out_added")
        memw_in = sem("memw_in")
        mem_in = sem("mem_in")
        mkv_done = sem("mkv_done")
        mkv_ready = sem("mkv_ready")
        mkT_done = sem("mkT_done")
        mkT_ready = sem("mkT_ready")
        mq_in = sem("mq_in")
        qm_done = sem("qm_done")
        qm_ready = sem("qm_ready")
        m_sc_done = sem("m_sc_done")
        m_max = sem("m_max")
        m_exp = sem("m_exp")
        m_norm = sem("m_norm")
        m_pT_done = sem("m_pT_done")
        m_pT_ready = sem("m_pT_ready")
        m_oT_done = sem("m_oT_done")
        m_oT_ready = sem("m_oT_ready")
        memkv_in = sem("memkv_in")
        mo_in = sem("mo_in")
        m_qmask = sem("m_qmask")
        m_keyT_done = sem("m_keyT_done")
        m_keyT_ready = sem("m_keyT_ready")
        mo_done = sem("mo_done")
        mo_added = sem("mo_added")
        wq_in = sem("wq_in")
        sub_in = sem("sub_in")
        subT_done = sem("subT_done")
        subT_ready = sem("subT_ready")
        qp_done = sem("qp_done")
        qp_ready = sem("qp_ready")
        ps_done = sem("ps_done")
        ps_ready = sem("ps_ready")
        best_shift = sem("best_shift")
        best_exp = sem("best_exp")
        routed = sem("routed")
        rt_done = sem("rt_done")
        hns_stored = sem("hns_stored")
        hns_in = sem("hns_in")
        cursor_ready = sem("cursor_ready")
        row_in = [sem(f"row_in{k}") for k in range(RING)]
        row_used = sem("row_used")
        act_kept = sem("act_kept")
        gelu_in = sem("gelu_in")
        gelu_tanh = sem("gelu_tanh")
        coefm_ready = sem("coefm_ready")
        se_done = sem("se_done")
        sk_zero = sem("sk_zero")
        x_done = sem("x_done")
        y_ready = sem("y_ready")
        y_stored = sem("y_stored")
        vector_order = sem("vector_order")
        pool_order = sem("pool_order")
        scalar_order = sem("scalar_order")

        class Order:

            def __init__(self, eng, s):
                self.eng, self.sem, self.n = eng, s, 0

            def __call__(self, ins):
                ins.then_inc(self.sem, 1)
                self.n += 1
                self.eng.wait_ge(self.sem, self.n)

        const_loads = [
            (gn_gain, c["gn_gain"]), (gn_rows[0:64, :], c["gn_rows"]), (cmp_bv, c["cmp_bv"]),
            (cmp_bk[0:64, :], c["cmp_bk"]), (ident, c["ident"]), (tri, c["tri"]), (decay, c["decay"]),
            (xi, c["xi"]), (zeta, c["zeta"]), (g_chunk, c["g_chunk"]), (gamma1[0:64, :], c["gamma1"]),
            (cmp_vis, c["cmp_vis"]), (cmp_neg, c["cmp_neg"]), (rot_ret, c["rot_ret"]), (rot_nsa, c["rot_nsa"]),
            (own_neg[0:64, :], c["own_neg"]), (group[0:64, :], c["group"]), (blk_excl[0:64, :], c["blk_excl"]),
            (blk_rank[0:64, :], c["blk_rank"]), (row_add, c["row_add"]), (iota16, c["iota16"]),
            (eye8, c["eye8"]), (page_i, a["page_rows"]),
        ]
        MEMT = [5, 6]

        heads64 = sc_heads.rearrange("x b (h d) -> x (b h) d", d=HD)
        S_RQ, S_RK, S_RV, S_RG, S_NQ, S_SK, S_SV, S_WK, S_WV, S_Y, S_T, S_U = range(12)
        N_SROWS = 5 + 4 + 2

        block = ctx.enter_context(nc.Block())

        @block.sync
        def _(sp):
            for t in range(NT):
                src = a["x_prompt"][0, t * P:(t + 1) * P, :] if t < PT else a["x_sample"][:, 0, :]
                sp.dma_start(h[0:rows_of(t), t, :], src).then_inc(x_in, 16)
            for i, name in enumerate(("norm_mix_g", "norm_mem_g", "mem_norm_g", "norm_ffn_g", "norm_final_g")):
                sp.dma_start(gain[:, i, :], a[name].partition_broadcast(P)).then_inc(consts_in, 16)
            for dst, src in const_loads:
                sp.dma_start(dst[:], src).then_inc(consts_in, 16)
            w_in = a["w_in"].rearrange("(k p) n -> p k n", p=P)
            for i, (c0, n) in enumerate(CHUNKS):
                if i >= 2:
                    sp.wait_ge(proj_done, NT * (i - 1))
                sp.dma_start(w_buf[:, i % 2, :, 0:n], w_in[:, :, c0:c0 + n]).then_inc(w_in_loaded[i % 2], 16)
            for t in range(NT):
                sp.wait_ge(rotated, t + 1)
                R = rows_of(t)
                if t < PT:
                    for name, c0 in (("p_cmp_k", C_CK), ("p_cmp_v", C_CV), ("p_slc_k", C_SK), ("p_slc_v", C_SV)):
                        sp.dma_start(out[name][0, 0, t].rearrange("g k d -> k g d"),
                                     proj[t][:, c0:c0 + P].rearrange("p (g d) -> p g d", g=G)
                                     ).then_inc(rows_stored, 16)
                    for name, c0 in (("p_win_k", C_WK), ("p_win_v", C_WV)):
                        sp.dma_start(out[name][0, 0, :, t * P:(t + 1) * P].rearrange("g k d -> k g d"),
                                     proj[t][:, c0:c0 + P].rearrange("p (g d) -> p g d", g=G)
                                     ).then_inc(rows_stored, 16)
                else:
                    for name, c0 in (("s_cmp_k", C_CK), ("s_cmp_v", C_CV), ("s_slc_k", C_SK), ("s_slc_v", C_SV)):
                        sp.dma_start(out[name][0].rearrange("b g x d -> b (g x d)"),
                                     proj[t][0:R, c0:c0 + P]).then_inc(rows_stored, 16)
                    for name, c0 in (("s_win_k", C_WK), ("s_win_v", C_WV)):
                        sp.dma_start(out[name][0, :, :, 511, :], proj[t][0:R, c0:c0 + P].rearrange(
                            "p (g d) -> p g d", g=G)).then_inc(rows_stored, 16)
                    sp.dma_start(sc_heads.rearrange("x b n -> b x n"), proj[t][0:R, 0:5 * 512].rearrange(
                        "p (x n) -> p x n", x=5)).then_inc(rows_stored, 16)
                    sp.dma_start(sc_gates, proj[t][0:R, C_NG:C_NG + 3 * H]).then_inc(rows_stored, 16)
            ROWS_STORED = 16 * (PT * 6 + 8)
            for name, src in (("s_win_k", "cache_win_k"), ("s_win_v", "cache_win_v")):
                sp.dma_start(out[name][0, :, :, 0:511, :], a[src][0, :, :, 1:512, :]).then_inc(y_stored, 16)
            sp.wait_ge(proj_done, NT * len(CHUNKS))
            for i in range(2):
                sp.dma_start(cmp_w[:, i, :, :], a["cmp_w"][0, i].rearrange("j d e -> (j d) e").rearrange(
                    "(m q) e -> q m e", q=P)).then_inc(cmpw_in, 16)
            sp.wait_ge(rows_stored, ROWS_STORED)
            for i, name in enumerate(("p_cmp_k", "p_cmp_v")):
                n = 3 * i + 2
                if n >= 2:
                    sp.wait_ge(blkT_done, 8 * (n - 1))
                sp.dma_start(blk_buf[0:BG, n % 2, :], out[name][0, 0].rearrange(
                    "n g (k j) d -> (n g k) (j d)", k=2)).then_inc(own_blk_in, 16)
            sp.wait_ge(cmp_ready, 6)
            sp.dma_start(sc_cv, cv_out[0:BG, :]).then_inc(cv_stored, 16)
            sp.wait_ge(cv_stored, 16)
            sp.wait_ge(vblk_zero, 1)
            cvr = sc_cv.rearrange("(n g k) d -> g n k d", g=G, k=2)
            for hh in range(H):
                sp.dma_start(c_vblk[hh * 8:hh * 8 + 8, hh * HD:(hh + 1) * HD], cvr[hh // R4]).then_inc(vblk_in, 16)
            sp.wait_ge(state_ready, PT)
            sp.dma_start(out["p_state"][0, 0].rearrange("h d e -> d h e"), state[0:HD, :, :]).then_inc(state_stored, 16)
            sp.wait_ge(cat_ready, PT)
            for i in range(5):
                sp.dma_start(s_rows[0:64, i, :], heads64[i]).then_inc(s_rows_in, 16)
            for i, name in ((S_SK, "s_slc_k"), (S_SV, "s_slc_v")):
                src = out[name][0].rearrange("b g x d -> (b g) x d")
                sp.dma_start(s_rows[0:64, i, :], src.broadcast_to((BG, R4, HD))).then_inc(s_rows_in, 16)
            for i, name in ((S_WK, "s_win_k"), (S_WV, "s_win_v")):
                src = out[name][0].rearrange("b g k d -> (b g) k d")[:, 511:512, :]
                sp.dma_start(s_rows[0:64, i, :], src.broadcast_to((BG, R4, HD))).then_inc(s_rows_in, 16)
            sp.dma_start(col[0:64, 0:3], sc_gates.rearrange("b (h x) -> (b h) x", x=3)).then_inc(s_rows_in, 16)
            sp.dma_start(own_q[0:64, :, :], c["own_q"]).then_inc(s_rows_in, 16)
            sp.dma_start(s_state[0:64, :, :], a["state_ret"][0].rearrange("b h d e -> (b h) d e")).then_inc(s_state_in, 16)
            sp.wait_ge(s_branch, 1)
            sp.dma_start(out["s_state"][0].rearrange("b h d e -> (b h) d e"), s_state[0:64, :, :]).then_inc(s_stored, 16)
            sp.wait_ge(s_branch, 3)
            for dst, name in ((key_rows, "cache_win_k"), (val_rows, "cache_win_v")):
                sp.dma_start(dst[:, :, 0:256], a[name][0].rearrange("b g (p j) d -> p (b g) (j d)", p=P)
                             ).then_inc((key_in if name == "cache_win_k" else val_in)[1], 16)
            sp.wait_ge(s_branch, 4)
            sp.dma_start(sc_cat[0].rearrange("b (h d) -> (b h) d", d=HD), s_rows[0:64, S_Y, :]).then_inc(s_stored, 16)
            sp.dma_start(sc_cat[1].rearrange("b (h d) -> (b h) d", d=HD), s_o[0:64, 3, :]).then_inc(s_stored, 16)
            sp.wait_ge(s_stored, 48)
            sp.dma_start(cat[0:DB, SAMPLE, :].rearrange("p (x n) -> p x n", x=2),
                         sc_cat.rearrange("x b n -> b x n")).then_inc(s_cat_in, 16)
            for dst, name in ((w_mk, "w_mk"), (w_mv, "w_mv")):
                sp.dma_start(dst, a[name].rearrange("(k p) n -> p k n", p=P)).then_inc(memw_in, 16)
            for t in range(2):
                sp.dma_start(mem_x[:, t, :], a["mem_prompt"][0, t * P:(t + 1) * P, :]).then_inc(mem_in, 16)
            sp.dma_start(w_mq, a["w_mq"].rearrange("(k p) n -> p k n", p=P)).then_inc(mq_in, 16)
            for n in range(4):
                sp.wait_ge(mkv_ready, n + 1)
                buf, name, t = (mk, "p_mem_k", n) if n < 2 else (mv, "p_mem_v", n - 2)
                sp.dma_start(out[name][0, 0, t * P:(t + 1) * P].rearrange("m h d -> m (h d)"),
                             buf[:, t, :]).then_inc(y_stored, 16)
            sp.dma_start(w_out, a["w_out"].rearrange("(k p) n -> p k n", p=P)).then_inc(w_out_in, 16)
            sp.wait_ge(out_done, 2 * NT)
            sp.dma_start(w_mo, a["w_mo"].rearrange("(k p) n -> p k n", p=P)).then_inc(mo_in, 16)
            sp.wait_ge(hn_ready, NT + 2 + NT)
            sp.wait_ge(hnT_done, 2 * (NT + 2 + NT))
            sp.wait_ge(y_stored, 16 * 6)
            for dst, name in ((mem_k, "cache_mem_k"), (mem_v, "cache_mem_v")):
                sp.dma_start(dst, a[name][0].rearrange("b (p m) h d -> p b (m h d)", m=2)).then_inc(memkv_in, 16)
            sp.wait_ge(qm_ready, 2 * HM)
            sp.dma_start(own_m, c["own_m"]).then_inc(memkv_in, 16)
            sp.wait_ge(mo_done, 2 * NT)
            sp.dma_start(wq, a["peer_wq"].rearrange("(k p) n -> p k n", p=P)).then_inc(wq_in, 16)
            sp.dma_start(sub_k.rearrange("p h (x d) -> p h x d", x=2), a["peer_subkeys"][0].rearrange("h x k d -> k h x d")).then_inc(sub_in, 16)
            sp.wait_ge(hn_ready, 3 * NT + 2)
            sp.dma_start(sc_hn, hn3[0:DB, SAMPLE, :]).then_inc(hns_stored, 16)
            sp.wait_ge(hns_stored, 16)
            sp.wait_ge(routed, NT + 1)
            sp.dma_start(hn_s.rearrange("p b d -> p (b d)"), sc_hn.rearrange("b d -> (b d)").partition_broadcast(P)).then_inc(hns_in, 16)
            for t in range(NT):
                R = rows_of(t)
                sp.wait_ge(y_ready, t + 1)
                dst = out["y_prompt"][0, t * P:(t + 1) * P, :] if t < PT else out["y_sample"][:, 0, :]
                sp.dma_start(dst, hn3[0:R, t, :]).then_inc(y_stored, 16)
            sp.wait_ge(rows_stored, ROWS_STORED)
            sp.wait_ge(state_stored, 16)
            sp.wait_ge(s_stored, 48)
            sp.wait_ge(y_stored, 16 * (2 + 4 + NT))

        @block.gpsimd
        def _(pool):
            order = Order(pool, pool_order)
            norms = [0]

            def norm_rstd(R):
                n = norms[0]
                norms[0] += 1
                pool.wait_ge(mean_ready, n + 1)
                m, r = mean_sq[0:R, n % 16:n % 16 + 1], rstd[0:R, n % 16:n % 16 + 1]
                order(pool.tensor_scalar(m, m, EPS, None, ALU.add))
                pool.tensor_tensor(r, m, half_neg[0:R, 0:1], ALU.pow).then_inc(rstd_ready, 1)

            def group_rstd(t):
                R, n = (P, H) if t < PT else (64, 1)
                pool.wait_ge(gn_var, t + 1)
                pool.tensor_tensor(gn_r[0:R, 0:n], gn_v[0:R, 0:n], half_neg[0:R, 0:n], ALU.pow).then_inc(gn_rstd, 1)

            order(pool.memset(half_neg, -0.5))
            pool.memset(c_vblk[0:64, :], 0.0).then_inc(vblk_zero, 1)
            for t in range(NT):
                norm_rstd(rows_of(t))
            pool.wait_ge(idx_ready, 2)
            pool.wait_ge(proj_done, NT * len(CHUNKS))
            for i, name in enumerate(("cache_cmp_k", "cache_cmp_v")):
                src = a[name][0].rearrange("n g (k j) d -> (n g k) (j d)", k=2)
                for x in range(2):
                    n = 3 * i + x
                    if n >= 2:
                        pool.wait_ge(blkT_done, 8 * (n - 1))
                    pool.indirect_dma_start(
                        out=blk_buf[:, n % 2, :], out_offset=None, in_=src,
                        in_offset=bass.IndirectOffsetOnAxis(ap=blk_idx[:, x:x + 1], axis=0)
                    ).then_inc(blk_in[n % 2], 16)
            for t in range(PT):
                group_rstd(t)
            pool.wait_ge(cat_ready, PT)
            for dst, name in ((key_rows, "cache_slc_k"), (val_rows, "cache_slc_v")):
                src = a[name][0].rearrange("n g (q j) d -> (n g q) (j d)", q=16)
                for bg in range(BG):
                    pool.indirect_dma_start(
                        out=dst[:, bg, :], out_offset=None, in_=src,
                        in_offset=bass.IndirectOffsetOnAxis(ap=row_idx[:, bg:bg + 1], axis=0)
                    ).then_inc((key_in if name == "cache_slc_k" else val_in)[0], 16)
            group_rstd(PT)
            norm_rstd(P)
            norm_rstd(P)
            for t in range(NT):
                norm_rstd(rows_of(t))
            for t in range(NT):
                norm_rstd(rows_of(t))
            pool.wait_ge(routed, NT + 1)

            def gather(name, idx, k):
                pool.indirect_dma_start(
                    out=ring[:, k, :], out_offset=None, in_=a[name][0],
                    in_offset=bass.IndirectOffsetOnAxis(ap=idx, axis=0)).then_inc(row_in[k], 16)

            for k in range(RING):
                gather("peer_u", expert[:, 0, k:k + 1], k)
            turned = 1
            for t in range(PT):
                for name in ("peer_u", "peer_v"):
                    begin = 1 if turned == 1 else 0
                    done = turned - begin
                    with pool.Fori(begin, TURNS) as i:
                        for k in range(RING):
                            pool.wait_ge(row_used, (i + (done - 1)) * RING + (k + 1))
                            pool.tensor_copy(cursor[:, k:k + 1], expert[:, t, bass.ds(i * RING + k, 1)]
                                             ).then_inc(cursor_ready, 1)
                            pool.wait_ge(routed, NT + 1)
                            pool.wait_ge(cursor_ready, (i + (done - 1)) * RING + (k + 1))
                            gather(name, cursor[:, k:k + 1], k)
                    turned += TURNS - begin
            for name in ("peer_u", "peer_v"):
                for b in range(DB):
                    k = b + (DB if name == "peer_v" else 0)
                    pool.wait_ge(row_used, (turned - 1) * RING + k + 1)
                    gather(name, expert_s[:, b:b + 1], k)
            for t in range(NT):
                norm_rstd(rows_of(t))

        @block.tensor
        def _(pe):
            freed = {}
            norms = [0]

            def claim(b):
                if b in freed:
                    pe.wait_ge(*freed.pop(b))
                return banks[b]

            def transpose_rows(src, R, s_ready, n_ready):
                n = norms[0]
                norms[0] += 1
                pe.wait_ge(hn_ready, n + 1)
                for half in range(2):
                    bank = claim(half)
                    for q in range(4):
                        k = 4 * half + q
                        ins = pe.transpose(bank[:, q * P:q * P + R], src[0:R, k * P:(k + 1) * P], ident[0:R, 0:R])
                    ins.then_inc(hnT_done, 1)
                    freed[half] = (hnT_ready, 2 * n + half + 1)

            pe.wait_ge(consts_in, 16 * (5 + len(const_loads)))
            for t in range(NT):
                transpose_rows(hn_buf[:, t % 2, :], rows_of(t), None, None)
            n = 0
            for i, (c0, w) in enumerate(CHUNKS):
                pe.wait_ge(w_in_loaded[i % 2], 16 * (i // 2 + 1))
                for t in range(NT):
                    if i == 0:
                        pe.wait_ge(hnT_ready, 2 * (t + 1))
                    R = rows_of(t)
                    b = 2 + n % 4
                    bank = claim(b)
                    for k in range(KC):
                        ins = pe.matmul(bank[0:R, 0:w], hnT[:, k, t * P:t * P + R], w_buf[:, i % 2, k, 0:w],
                                        start=(k == 0), stop=(k == KC - 1))
                    ins.then_inc(proj_done, 1)
                    n += 1
                    freed[b] = (proj_ready, n)

            def cmp_products(unit, m):
                kind, x = divmod(unit, 3)
                R = P if x < 2 else BG
                pe.wait_ge(blkT_ready, 8 * unit + m + 1)
                acc_bank = banks[4 + unit % 2]
                for q in range(4):
                    j = 4 * m + q
                    rows, w = blkT[:, m % 2, q, 0:R], cmp_w[:, kind, j, :]
                    if kind == 0:
                        ins = pe.matmul(acc_bank[0:HD, 0:R], w, rows, start=(j == 0), stop=(j == 31))
                    else:
                        ins = pe.matmul(acc_bank[0:R, 0:HD], rows, w, start=(j == 0), stop=(j == 31))
                if m == 7:
                    ins.then_inc(cmp_done, 1)
                    freed[4 + unit % 2] = (cmp_ready, unit + 1)

            for unit in range(6):
                R = P if unit % 3 < 2 else BG
                if unit % 3 == 2:
                    pe.wait_ge(own_blk_in, 16 * (unit // 3 + 1))
                else:
                    pe.wait_ge(blk_in[unit % 2], 16 * (1 + (unit >= 3)))
                if unit == 0:
                    pe.wait_ge(cmpw_in, 32)
                claim(4 + unit % 2)
                for m in range(8):
                    bank = claim(m % 2)
                    for q in range(4):
                        j = 4 * m + q
                        ins = pe.transpose(bank[:, q * P:q * P + R], blk_buf[0:R, unit % 2, j * P:(j + 1) * P],
                                           ident[0:R, 0:R])
                    ins.then_inc(blkT_done, 1)
                    freed[m % 2] = (blkT_ready, 8 * unit + m + 1)
                    if m:
                        cmp_products(unit, m - 1)
                cmp_products(unit, 7)

            def att_scores(t, u):
                kind, hh = divmod(u % 16, H)
                b, N = u % 2, P * (t + 1)
                bank = claim(b)
                pe.matmul(bank[:, 0:N], nqT[0:HD, hh, :], kT[0:HD, kind, hh // R4, 0:N], start=True, stop=False)
                pe.matmul(bank[:, N - P:N], ident, tri, start=False, stop=True).then_inc(sc_done, 1)
                freed[b] = (exp_ready, u + 1)

            def att_probsT(t, u):
                b = 3 + u % 2
                bank = claim(b)
                pe.wait_ge(exp_ready, u + 1)
                for j in range(t + 1):
                    ins = pe.transpose(bank[:, j * P:(j + 1) * P], probs[:, u % 2, j * P:(j + 1) * P], ident)
                ins.then_inc(pT_done, 1)
                freed[b] = (pT_ready, u + 1)

            def att_values(t, u):
                kind, hh = divmod(u % 16, H)
                b = 5 + kind
                if hh == 0:
                    claim(b)
                c0 = (C_SV, C_WV)[kind] + hh // R4 * HD
                pe.wait_ge(pT_ready, u + 1)
                for j in range(t + 1):
                    ins = pe.matmul(banks[b][:, hh * HD:(hh + 1) * HD], probsT[:, u % 2, j * P:(j + 1) * P],
                                    proj[j][:, c0:c0 + HD], start=(j == 0), stop=(j == t))
                if hh == H - 1:
                    ins.then_inc(ao_done, 1)
                    freed[b] = (ao_used, 2 * t + kind + 1)

            for t in range(PT):
                pe.wait_ge(rotated, t + 1)
                heads = [C_RQ + HD * x for x in range(H)] + [C_RK + HD * x for x in range(H)] + \
                        [C_NQ + HD * x for x in range(H)] + [C_SK, C_SK + HD, C_WK, C_WK + HD]
                for m in range(7):
                    bank = claim(m % 2)
                    for q in range(4):
                        c0 = heads[4 * m + q]
                        ins = pe.transpose(bank[0:HD, q * P:(q + 1) * P], proj[t][:, c0:c0 + HD], ident)
                    ins.then_inc(headT_done, 1)
                    freed[m % 2] = (headT_ready, 7 * t + m + 1)
                pe.wait_ge(headT_ready, 7 * t + 4)
                for m in range(2):
                    bank = claim(2 + m)
                    for q in range(4):
                        ins = pe.matmul(bank[:, q * P:(q + 1) * P], rkT[0:HD, 4 * m + q, :], rqT[0:HD, 4 * m + q, :],
                                        start=True, stop=True)
                    ins.then_inc(att_done, 1)
                    freed[2 + m] = (att_ready, 2 * t + m + 1)
                if t == 0:
                    pe.wait_ge(cmp_ready, 6)
                pe.wait_ge(headT_ready, 7 * t + 6)
                bank = claim(7)
                for hh in range(H):
                    keys = c_kT[0:HD, 256:272].rearrange("p (n g k) -> p n g k", g=G, k=2)[:, :, hh // R4, :]
                    ins = pe.matmul(bank[:, hh * 8:(hh + 1) * 8], nqT[0:HD, hh, :], keys, start=True, stop=True)
                ins.then_inc(cs_done, 1)
                freed[7] = (cs_ready, t + 1)
                for b in (4, 5, 6):
                    claim(b)
                if t:
                    pe.wait_ge(state_ready, t)
                    for hh in range(H):
                        pe.matmul(banks[4][:, hh * HD:(hh + 1) * HD], rqT[0:HD, hh, :], state[0:HD, hh, :],
                                  start=True, stop=True)
                pe.wait_ge(vz_ready, t + 1)
                for hh in range(H):
                    pe.matmul(banks[6][0:HD, hh * HD:(hh + 1) * HD], proj[t][:, C_RK + hh * HD:C_RK + (hh + 1) * HD],
                              vz[:, hh, :], start=True, stop=True)
                pe.wait_ge(att_ready, 2 * t + 2)
                for hh in range(H):
                    ins = pe.matmul(banks[5][:, hh * HD:(hh + 1) * HD], att[:, hh, :],
                                    proj[t][:, C_RV + hh * HD:C_RV + (hh + 1) * HD], start=True, stop=True)
                ins.then_inc(ret_done, 1)
                for b in (4, 5, 6):
                    freed[b] = (state_ready, t + 1)
                bank = claim(7)
                pe.wait_ge(cp_ready, t + 1)
                pe.transpose(bank[0:64, 0:P], cp_buf, ident).then_inc(cpT_done, 1)
                freed[7] = (cpT_ready, t + 1)
                bank = claim(2)
                if t == 0:
                    pe.wait_ge(vblk_in, 16 * H)
                pe.wait_ge(cpT_ready, t + 1)
                pe.matmul(bank[:, 0:512], cpT[0:64, :], c_vblk[0:64, :], start=True, stop=True).then_inc(co_done, 1)
                freed[2] = (co_used, t + 1)
                pe.wait_ge(headT_ready, 7 * t + 7)
                u0 = 2 * H * t
                att_scores(t, u0)
                for u in range(u0, u0 + 2 * H):
                    if u + 1 < u0 + 2 * H:
                        att_scores(t, u + 1)
                    att_probsT(t, u)
                    att_values(t, u)

            pe.wait_ge(s_rows_in, 16 * N_SROWS)
            bank = claim(0)
            pe.transpose(bank[0:64, 0:64], s_rows[0:64, S_NQ, :], ident[0:64, 0:64]).then_inc(sT_done, 1)
            freed[0] = (sT_ready, 1)
            pe.wait_ge(sT_ready, 1)
            bank = claim(1)
            pe.matmul(bank[0:64, 0:256], sqT[0:64, :], c_kT[0:HD, 0:256], start=True, stop=True).then_inc(s_sc_done, 1)
            freed[1] = (s_max, 1)
            pe.wait_ge(s_imp, 1)
            bank = claim(2)
            for x in range(2):
                ins = pe.transpose(bank[:, x * 64:(x + 1) * 64], cmp_p[0:64, x * P:(x + 1) * P], ident[0:64, 0:64])
            ins.then_inc(s_pT_done, 1)
            freed[2] = (s_pT_ready, 1)
            pe.wait_ge(s_pT_ready, 1)
            bank = claim(3)
            pe.matmul(bank[0:64, 64:80], group[0:64, :], s_small[0:64, 32:48], start=True, stop=True)
            for x in range(2):
                ins = pe.matmul(bank[0:64, 0:64], cmp_pT[:, x, :], c_v[:, x, :], start=(x == 0), stop=(x == 1))
            ins.then_inc(s_o_done, 1)
            freed[3] = (s_branch, 2)
            pe.wait_ge(qmask_ready, 1)
            gi = 0
            for kind, nj in enumerate((8, 4)):
                nc_ = nj // 4
                pe.wait_ge(key_in[kind], (16 * BG, 16)[kind])
                for cc in range(nc_):
                    claim(4 + cc)

                def key_scores(i, gi):
                    bg, cc = divmod(i, nc_)
                    pe.wait_ge(s_keyT_ready, gi + 1)
                    ins = pe.matmul(banks[4 + cc][0:64, :], q_mask[0:HD, bg, :], keyT[0:HD, gi % 2, :],
                                    start=(bg == 0), stop=(bg == BG - 1))
                    return ins

                for i in range(BG * nc_):
                    bg, cc = divmod(i, nc_)
                    bank = claim(gi % 2)
                    for q in range(4):
                        j = 4 * cc + q
                        ins = pe.transpose(bank[0:HD, q * P:(q + 1) * P], key_rows[:, bg, j * HD:(j + 1) * HD], ident)
                    ins.then_inc(s_keyT_done, 1)
                    freed[gi % 2] = (s_keyT_ready, gi + 1)
                    if i:
                        key_scores(i - 1, gi - 1)
                    gi += 1
                key_scores(BG * nc_ - 1, gi - 1).then_inc(s_sc_done, 1)
                for cc in range(nc_):
                    freed[4 + cc] = (s_max, 2 + kind)
                bank = claim(6)
                pe.wait_ge(s_exp, 2 + kind)
                for j in range(nj):
                    ins = pe.transpose(bank[:, j * 64:(j + 1) * 64], s_probs[0:64, j * P:(j + 1) * P],
                                       ident[0:64, 0:64])
                ins.then_inc(s_pT_done, 1)
                freed[6] = (s_pT_ready, 2 + kind)
                pe.wait_ge(val_in[kind], (16 * BG, 16)[kind])
                pe.wait_ge(s_pT_ready, 2 + kind)
                bank = claim(7)
                for bg in range(BG):
                    for j in range(nj):
                        ins = pe.matmul(bank[0:HD, bg * R4:(bg + 1) * R4], val_rows[:, bg, j * HD:(j + 1) * HD],
                                        s_probsT[:, j, bg * R4:(bg + 1) * R4], start=(j == 0), stop=(j == nj - 1))
                ins.then_inc(s_oT_done, 1)
                freed[7] = (s_oT_ready, 1 + kind)
                pe.wait_ge(s_oT_ready, 1 + kind)
                bank = claim(3)
                pe.transpose(bank[0:64, 0:64], s_o[0:HD, 0, :], ident[0:64, 0:64]).then_inc(s_o_done, 1)
                freed[3] = (s_branch, 3 + kind)

            for t in range(2):
                transpose_rows(hn_buf2[:, (NT + t) % 2, :], P, None, None)
            pe.wait_ge(hnT_ready, 2 * (NT + 2))
            pe.wait_ge(memw_in, 32)
            for n in range(4):
                w, t = divmod(n, 2)
                b = 2 + n
                bank = claim(b)
                for k in range(KC):
                    ins = pe.matmul(bank[:, :], mT[:, k, t * P:(t + 1) * P], (w_mk, w_mv)[w][:, k, :],
                                    start=(k == 0), stop=(k == KC - 1))
                ins.then_inc(mkv_done, 1)
                freed[b] = (mkv_ready, n + 1)
            pe.wait_ge(mkv_ready, 2)
            for t in range(2):
                bank = claim(t)
                for hh in range(HM):
                    ins = pe.transpose(bank[:, hh * P:(hh + 1) * P], mk[:, t, hh * P:(hh + 1) * P], ident)
                ins.then_inc(mkT_done, 1)
                freed[t] = (mkT_ready, t + 1)

            pe.wait_ge(w_out_in, 16)
            n = 0
            for t in range(NT):
                R = rows_of(t)
                if t < PT:
                    pe.wait_ge(cat_ready, t + 1)
                else:
                    pe.wait_ge(s_cat_in, 16)
                for half in range(2):
                    bank = claim(half)
                    for q in range(4):
                        k = 4 * half + q
                        ins = pe.transpose(bank[:, q * P:q * P + R], cat[0:R, t, k * P:(k + 1) * P], ident[0:R, 0:R])
                    ins.then_inc(catT_done, 1)
                    freed[half] = (catT_ready, 2 * t + half + 1)
                pe.wait_ge(catT_ready, 2 * t + 2)
                for half in range(2):
                    b = 2 + n % 4
                    bank = claim(b)
                    for k in range(KC):
                        ins = pe.matmul(bank[0:R, :], catT[:, t % 2, k, 0:R], w_out[:, k, half * 512:(half + 1) * 512],
                                        start=(k == 0), stop=(k == KC - 1))
                    ins.then_inc(out_done, 1)
                    n += 1
                    freed[b] = (out_added, n)

            for t in range(NT):
                transpose_rows(hn_buf2[:, (NT + 2 + t) % 2, :], rows_of(t), None, None)
            pe.wait_ge(mq_in, 16)
            pe.wait_ge(hnT_ready, 2 * (2 * NT + 2))
            for n in range(2 * HM):
                hh, small = divmod(n, 2)
                b = 2 + n % 4
                bank = claim(b)
                w0, w = (512, DB) if small else (0, 512)
                for k in range(KC):
                    ins = pe.matmul(bank[:, 0:w], w_mq[:, k, hh * P:(hh + 1) * P], hnT2[:, k, w0:w0 + w],
                                    start=(k == 0), stop=(k == KC - 1))
                ins.then_inc(qm_done, 1)
                freed[b] = (qm_ready, n + 1)
            pe.wait_ge(qm_ready, 2 * HM)
            pe.wait_ge(mkT_ready, 2)

            def mem_scores(v):
                t, hh = divmod(v, HM)
                bank = claim(v % 2)
                pe.matmul(bank[:, 0:NMEM], qT_m[:, hh, t * P:(t + 1) * P], mkT[:, hh, :],
                          start=True, stop=True).then_inc(m_sc_done, 1)
                freed[v % 2] = (m_exp, v + 1)

            mem_scores(0)
            for v in range(PT * HM):
                hh = v % HM
                if v + 1 < PT * HM:
                    mem_scores(v + 1)
                b = 6 + v % 2
                bank = claim(b)
                pe.wait_ge(m_norm, v + 1)
                for x in range(2):
                    ins = pe.transpose(bank[:, x * P:(x + 1) * P], m_probs[:, v % 2, x * P:(x + 1) * P], ident)
                ins.then_inc(m_pT_done, 1)
                freed[b] = (m_pT_ready, v + 1)
                b = 4 + v % 2
                bank = claim(b)
                pe.wait_ge(m_pT_ready, v + 1)
                for x in range(2):
                    ins = pe.matmul(bank[:, 0:P], mv[:, x, hh * P:(hh + 1) * P], m_probsT[:, v % 2, x * P:(x + 1) * P],
                                    start=(x == 0), stop=(x == 1))
                ins.then_inc(m_oT_done, 1)
                freed[b] = (m_oT_ready, v + 1)

            V = PT * HM
            pe.wait_ge(m_qmask, 1)
            pe.wait_ge(memkv_in, 48)
            claim(2)

            def mem_key_scores(g):
                b, pair = divmod(g, 2)
                pe.wait_ge(m_keyT_ready, g + 1)
                for x in range(2):
                    cc = (2 * pair + x) * DB + b
                    ins = pe.matmul(banks[2][0:32, 0:NMEM], qm_mask[:, cc, :], mkT_s[:, g % 2, x * NMEM:(x + 1) * NMEM],
                                    start=(g == 0 and x == 0), stop=(g == 2 * DB - 1 and x == 1))
                return ins

            for g in range(2 * DB):
                b, pair = divmod(g, 2)
                bank = claim(g % 2)
                for x in range(2):
                    for m in range(2):
                        c0 = m * 512 + (2 * pair + x) * P
                        ins = pe.transpose(bank[:, x * NMEM + m * P:x * NMEM + (m + 1) * P], mem_k[:, b, c0:c0 + P], ident)
                ins.then_inc(m_keyT_done, 1)
                freed[g % 2] = (m_keyT_ready, g + 1)
                if g:
                    mem_key_scores(g - 1)
            mem_key_scores(2 * DB - 1).then_inc(m_sc_done, 1)
            freed[2] = (m_exp, V + 1)
            bank = claim(3)
            pe.wait_ge(m_norm, V + 1)
            for m in range(2):
                ins = pe.transpose(bank[:, m * 32:(m + 1) * 32], ms_probs[0:32, m * P:(m + 1) * P], ident[0:32, 0:32])
            ins.then_inc(m_pT_done, 1)
            freed[3] = (m_pT_ready, V + 1)
            bank = claim(4)
            pe.wait_ge(m_pT_ready, V + 1)
            for hh in range(HM):
                for b in range(DB):
                    cc = hh * DB + b
                    for m in range(2):
                        c0 = m * 512 + hh * P
                        ins = pe.matmul(bank[:, cc:cc + 1], mem_v[:, b, c0:c0 + P], ms_probsT[:, m, cc:cc + 1],
                                        start=(m == 0), stop=(m == 1))
            ins.then_inc(m_oT_done, 1)
            freed[4] = (m_oT_ready, V + 1)
            pe.wait_ge(mo_in, 16)
            pe.wait_ge(m_oT_ready, V + 1)
            n = 0
            for t in range(NT):
                R = rows_of(t)
                for half in range(2):
                    b = (5, 6, 7, 0)[n % 4]
                    bank = claim(b)
                    for hh in range(HM):
                        ins = pe.matmul(bank[0:R, :], oT_m[:, hh, t * P:t * P + R], w_mo[:, hh, half * 512:(half + 1) * 512],
                                        start=(hh == 0), stop=(hh == HM - 1))
                    ins.then_inc(mo_done, 1)
                    n += 1
                    freed[b] = (mo_added, n)

            for t in range(NT):
                transpose_rows(hn3[:, t, :], rows_of(t), None, None)
            pe.wait_ge(sub_in, 16)
            for half in range(2):
                bank = claim(half)
                for q in range(4):
                    ins = pe.transpose(bank[:, q * P:(q + 1) * P], sub_k[:, 4 * half + q, :], ident)
                ins.then_inc(subT_done, 1)
                freed[half] = (subT_ready, half + 1)
            pe.wait_ge(wq_in, 16)
            pe.wait_ge(hnT_ready, 2 * (3 * NT + 2))
            for n in range(2 * H):
                hh, small = divmod(n, 2)
                b = 2 + n % 4
                bank = claim(b)
                w0, w = (512, DB) if small else (0, 512)
                for k in range(KC):
                    ins = pe.matmul(bank[:, 0:w], wq[:, k, hh * P:(hh + 1) * P], hnT3[:, k, w0:w0 + w],
                                    start=(k == 0), stop=(k == KC - 1))
                ins.then_inc(qp_done, 1)
                freed[b] = (qp_ready, n + 1)
            pe.wait_ge(qp_ready, 2 * H)
            pe.wait_ge(subT_ready, 2)
            for t in range(NT):
                R = rows_of(t)
                for m in range(4):
                    b = 4 + m
                    bank = claim(b)
                    for x in range(2):
                        hh = 2 * m + x
                        ins = pe.matmul(bank[0:R, x * 256:(x + 1) * 256], qT_p[:, hh, t * P:t * P + R], skT[:, hh, :],
                                        start=True, stop=True)
                    ins.then_inc(ps_done, 1)
                    freed[b] = (ps_ready, 4 * t + m + 1)
            bank = claim(0)
            pe.wait_ge(routed, PT + 1)
            pe.transpose(bank[:, 0:DB], pick[0:DB, 0, :], ident[0:DB, 0:DB])
            pe.transpose(bank[:, DB:2 * DB], gates_p[0:DB, SAMPLE, :], ident[0:DB, 0:DB]).then_inc(rt_done, 1)

            for half in range(2):
                claim(6 + half)
            pe.wait_ge(coefm_ready, 1)
            turns = 2 * PT * TURNS
            for b in range(DB):
                k = DB + b
                pe.wait_ge(row_in[k], 16 * (turns + 1))
                for half in range(2):
                    ins = pe.matmul(banks[6 + half][0:DB, :], coef_m[:, b, :], ring[:, k, half * 512:(half + 1) * 512],
                                    start=(b == 0), stop=(b == DB - 1))
            ins.then_inc(se_done, 1)

        @block.scalar
        def _(act):
            norms = [0]
            order = Order(act, scalar_order)

            def mean_square(x, junk, s=None, v=None):
                n = norms[0]
                norms[0] += 1
                R = x.shape[0]
                if s is not None:
                    act.wait_ge(s, v)
                if n:
                    act.wait_ge(mean_ready, n)
                act.activation(junk[0:R, :], x, ACT.Square, scale=1.0 / 32,
                               accum_out=mean_sq[0:R, n % 16:n % 16 + 1]).then_inc(mean_ready, 1)

            copied = [0]

            def copy_rowsT(dst, c0, R):
                n = copied[0]
                copied[0] += 1
                for half in range(2):
                    act.wait_ge(hnT_done, 2 * n + half + 1)
                    act.activation(dst[:, 4 * half:4 * half + 4, c0:c0 + R],
                                   banks[half][:, :].rearrange("p (k r) -> p k r", k=4)[:, :, 0:R],
                                   ACT.Copy).then_inc(hnT_ready, 1)

            act.wait_ge(x_in, 16 * NT)
            for t in range(NT):
                mean_square(h[0:rows_of(t), t, :], sq_junk)
            for t in range(NT):
                copy_rowsT(hnT, t * P, rows_of(t))
            n = 0
            for c0, w in CHUNKS:
                for t in range(NT):
                    R = rows_of(t)
                    act.wait_ge(proj_done, n + 1)
                    act.activation(proj[t][0:R, c0:c0 + w], banks[2 + n % 4][0:R, 0:w], ACT.Copy).then_inc(proj_ready, 1)
                    n += 1
            for unit in range(6):
                R = P if unit % 3 < 2 else BG
                for m in range(8):
                    act.wait_ge(blkT_done, 8 * unit + m + 1)
                    act.activation(blkT[:, m % 2, :, 0:R], banks[m % 2][:, :].rearrange("p (k r) -> p k r", k=4)[:, :, 0:R],
                                   ACT.Copy).then_inc(blkT_ready, 1)
            for t in range(PT):
                for m in range(7):
                    act.wait_ge(headT_done, 7 * t + m + 1)
                    src = banks[m % 2][0:HD, :].rearrange("p (k r) -> p k r", k=4)
                    if m < 6:
                        dst = (rqT, rkT, nqT)[m // 2][0:HD, 4 * (m % 2):4 * (m % 2) + 4, :]
                    else:
                        dst = kT[0:HD, :, :, t * P:(t + 1) * P].rearrange("p x g r -> p (x g) r")
                    act.activation(dst, src, ACT.Copy, scale=0.125 if m in (4, 5) else 1.0).then_inc(headT_ready, 1)
                if t:
                    act.wait_ge(cat_ready, t)
                act.activation(tanh_rg, proj[t][:, C_RG:C_RG + 512], ACT.Tanh, scale=0.5).then_inc(tanh_ready, 1)
                act.activation(gate, proj[t][:, C_NG:C_NG + 3 * H], ACT.Tanh, scale=0.5).then_inc(tanh_ready, 1)
                act.wait_ge(cs_ready, t + 1)
                act.activation(cp_buf, cs_buf, ACT.Exp).then_inc(cs_exp, 1)
                act.wait_ge(cpT_done, t + 1)
                act.activation(cpT[0:64, :], banks[7][0:64, 0:P], ACT.Copy).then_inc(cpT_ready, 1)
                for u in range(2 * H * t, 2 * H * (t + 1)):
                    kind, hh = divmod(u % 16, H)
                    N = P * (t + 1)
                    act.wait_ge(max_ready, u + 1)
                    if u >= 2:
                        act.wait_ge(pT_done, u - 1)
                    act.activation(probs[:, u % 2, 0:N], banks[u % 2][:, 0:N], ACT.Exp,
                                   bias=neg_max[:, u % 16:u % 16 + 1],
                                   accum_out=exp_sum[:, kind, hh:hh + 1]).then_inc(exp_ready, 1)
            act.wait_ge(s_rows_in, 16 * N_SROWS)
            act.activation(s_rows[0:64, S_T, :], s_rows[0:64, S_RG, :], ACT.Tanh, scale=0.5).then_inc(tanh_ready, 1)
            act.activation(gate[0:64, 0:3], col[0:64, 0:3], ACT.Tanh, scale=0.5).then_inc(tanh_ready, 1)
            act.wait_ge(sT_done, 1)
            act.activation(sqT[0:64, :], banks[0][0:64, 0:64], ACT.Copy, scale=0.125).then_inc(sT_ready, 1)
            act.wait_ge(s_max, 1)
            act.activation(cmp_p[0:64, :], s_scores[0:64, 0:256], ACT.Exp, bias=neg_max[0:64, 0:1],
                           accum_out=exp_sum[0:64, 0, 0:1]).then_inc(s_exp, 1)
            act.wait_ge(s_pT_done, 1)
            act.activation(cmp_pT, banks[2][:, 0:128].rearrange("p (x r) -> p x r", x=2), ACT.Copy).then_inc(s_pT_ready, 1)
            gi = 0
            for kind, nj in enumerate((8, 4)):
                for i in range(BG * nj // 4):
                    act.wait_ge(s_keyT_done, gi + 1)
                    act.activation(keyT[0:HD, gi % 2, :], banks[gi % 2][0:HD, :], ACT.Copy).then_inc(s_keyT_ready, 1)
                    gi += 1
                act.wait_ge(s_max, 2 + kind)
                N = nj * P + 1
                act.activation(s_probs[0:64, 0:N], s_scores[0:64, 0:N], ACT.Exp, bias=neg_max[0:64, 1 + kind:2 + kind],
                               accum_out=exp_sum[0:64, 0, 1 + kind:2 + kind]).then_inc(s_exp, 1)
                act.wait_ge(s_pT_done, 2 + kind)
                act.activation(s_probsT[:, 0:nj, :], banks[6][:, 0:nj * 64].rearrange("p (x r) -> p x r", x=nj),
                               ACT.Copy).then_inc(s_pT_ready, 1)
                act.wait_ge(s_oT_done, 1 + kind)
                act.activation(s_o[0:HD, 0, :], banks[7][0:HD, 0:64], ACT.Copy).then_inc(s_oT_ready, 1)
            act.wait_ge(mem_in, 32)
            for t in range(2):
                mean_square(mem_x[:, t, :], sq_junk2)
            for t in range(2):
                copy_rowsT(mT, t * P, P)
            for n in range(4):
                act.wait_ge(mkv_done, n + 1)
                act.activation((mk, mv)[n // 2][:, n % 2, :], banks[2 + n][:, :], ACT.Copy).then_inc(mkv_ready, 1)
            for t in range(2):
                act.wait_ge(mkT_done, t + 1)
                act.activation(mkT[:, :, t * P:(t + 1) * P], banks[t][:, :].rearrange("p (k r) -> p k r", k=4),
                               ACT.Copy).then_inc(mkT_ready, 1)
            for t in range(NT):
                R = rows_of(t)
                for half in range(2):
                    act.wait_ge(catT_done, 2 * t + half + 1)
                    act.activation(catT[:, t % 2, 4 * half:4 * half + 4, 0:R],
                                   banks[half][:, :].rearrange("p (k r) -> p k r", k=4)[:, :, 0:R],
                                   ACT.Copy).then_inc(catT_ready, 1)
            for t in range(NT):
                mean_square(h[0:rows_of(t), t, :], sq_junk2, out_added, 2 * (t + 1))
            for t in range(NT):
                copy_rowsT(hnT2, t * P, rows_of(t))
            for n in range(2 * HM):
                hh, small = divmod(n, 2)
                w0, w = (512, DB) if small else (0, 512)
                act.wait_ge(qm_done, n + 1)
                act.activation(qT_m[:, hh, w0:w0 + w], banks[2 + n % 4][:, 0:w], ACT.Copy,
                               scale=HDM ** -0.5).then_inc(qm_ready, 1)
            for v in range(PT * HM + 1):
                last = v == PT * HM
                t, hh = divmod(v, HM)
                if last:
                    for g in range(2 * DB):
                        act.wait_ge(m_keyT_done, g + 1)
                        act.activation(mkT_s[:, g % 2, :], banks[g % 2][:, :], ACT.Copy).then_inc(m_keyT_ready, 1)
                R = 32 if last else P
                dst = ms_probs if last else m_probs[:, v % 2, :]
                act.wait_ge(m_max, v + 1)
                act.activation(dst[0:R, :], banks[2 if last else v % 2][0:R, 0:NMEM], ACT.Exp,
                               bias=neg_max[0:R, v % 2:v % 2 + 1],
                               accum_out=exp_sum[0:R, 0, v % 2:v % 2 + 1]).then_inc(m_exp, 1)
                act.wait_ge(m_pT_done, v + 1)
                if last:
                    act.activation(ms_probsT, banks[3][:, 0:64].rearrange("p (x r) -> p x r", x=2), ACT.Copy
                                   ).then_inc(m_pT_ready, 1)
                    act.wait_ge(m_oT_done, v + 1)
                    act.activation(oT_m[:, :, 512:520], banks[4][:, 0:32].rearrange("p (k r) -> p k r", k=HM), ACT.Copy
                                   ).then_inc(m_oT_ready, 1)
                else:
                    act.activation(m_probsT[:, v % 2, :], banks[6 + v % 2][:, 0:NMEM], ACT.Copy).then_inc(m_pT_ready, 1)
                    act.wait_ge(m_oT_done, v + 1)
                    act.activation(oT_m[:, hh, t * P:(t + 1) * P], banks[4 + v % 2][:, 0:P], ACT.Copy
                                   ).then_inc(m_oT_ready, 1)
            for t in range(NT):
                mean_square(h[0:rows_of(t), t, :], sq_junk3, mo_added, 2 * (t + 1))
            for t in range(NT):
                copy_rowsT(hnT3, t * P, rows_of(t))
            act.wait_ge(sk_zero, 1)
            for half in range(2):
                act.wait_ge(subT_done, half + 1)
                src = banks[half][:, :].rearrange("p (k r) -> p k r", k=4)
                act.activation(skT[0:64, 4 * half:4 * half + 4, 0:P], src[0:64], ACT.Copy)
                act.activation(skT[64:P, 4 * half:4 * half + 4, P:2 * P], src[64:P], ACT.Copy).then_inc(subT_ready, 1)
            for n in range(2 * H):
                hh, small = divmod(n, 2)
                w0, w = (512, DB) if small else (0, 512)
                act.wait_ge(qp_done, n + 1)
                act.activation(qT_p[:, hh, w0:w0 + w], banks[2 + n % 4][:, 0:w], ACT.Copy).then_inc(qp_ready, 1)
            for t in range(NT):
                R = rows_of(t)
                if t:
                    act.wait_ge(routed, t)
                for m in range(4):
                    act.wait_ge(ps_done, 4 * t + m + 1)
                    act.activation(s_all[0:R, 4 * m:4 * m + 4, :], banks[4 + m][0:R, :].rearrange("p (k r) -> p k r", k=4),
                                   ACT.Copy).then_inc(ps_ready, 1)
                act.wait_ge(best_shift, t + 1)
                act.activation(best_e[0:R], best_e[0:R], ACT.Exp).then_inc(best_exp, 1)
            for t in range(NT):
                act.wait_ge(gelu_in, t + 1)
                act.activation(gtmp[:, 0, 0:SLOTS if t < PT else DB], gtmp[:, 0, 0:SLOTS if t < PT else DB],
                               ACT.Tanh, scale=GELU_B).then_inc(gelu_tanh, 1)
            for t in range(NT):
                R = rows_of(t)
                mean_square(h[0:R, t, :], acc, x_done, t + 1)

        @block.vector
        def _(dve):
            order = Order(dve, vector_order)
            norms = [0]
            tt, ts, stt, red = dve.tensor_tensor, dve.tensor_scalar, dve.scalar_tensor_tensor, dve.tensor_reduce

            def normed(dst, x, which):
                n = norms[0]
                norms[0] += 1
                R = x.shape[0]
                dve.wait_ge(rstd_ready, n + 1)
                if n >= 2:
                    dve.wait_ge(hnT_done, min(2 * (n - 1), 2 * (3 * NT + 2)))
                stt(out=dst[0:R, :], in0=x, scalar=rstd[0:R, n % 16:n % 16 + 1], in1=gain[0:R, which, :],
                    op0=ALU.mult, op1=ALU.mult).then_inc(hn_ready, 1)

            dve.wait_ge(consts_in, 16 * (5 + len(const_loads)))
            for t in range(NT):
                normed(hn_buf[:, t % 2, :], h[0:rows_of(t), t, :], MIX)
            order(dve.tensor_copy(page_f, page_i[:, :]))
            ts(blk_idx[:, :], page_f[:, 0:2], 4.0, row_add[:, 0:1], ALU.mult, ALU.add).then_inc(idx_ready, 1)
            for g in range(G):
                ins = ts(row_idx[:, g:BG:G], page_f[:, 2:10], 32.0, row_add[:, 1 + g:2 + g], ALU.mult, ALU.add)
            ins.then_inc(idx_ready, 1)

            def rotate(x1, x2, cos, sin, t4):
                tt(t4[0], x1, cos, ALU.mult)
                tt(t4[1], x2, sin, ALU.mult)
                tt(t4[2], x1, sin, ALU.mult)
                order(tt(t4[3], x2, cos, ALU.mult))
                tt(x1, t4[0], t4[1], ALU.subtract)
                return tt(x2, t4[2], t4[3], ALU.add)

            dve.wait_ge(proj_ready, NT * len(CHUNKS))
            for t in range(NT):
                R = rows_of(t)
                x = proj[t][0:R, 0:1024].rearrange("p (s h d) -> p s h d", s=2, h=H)
                tab = [rot_ret[0:R, t, i].unsqueeze(2).broadcast_to((R, 2, H, 32)) for i in range(2)]
                tv = [rot_t[0:R, i, :].rearrange("p (s h d) -> p s h d", s=2, h=H) for i in range(4)]
                order(rotate(x[:, :, :, 0:32], x[:, :, :, 32:64], tab[0], tab[1], tv))
                x = proj[t][0:R, C_NQ:C_NQ + 512].rearrange("p (h d) -> p h d", h=H)
                tab = [rot_nsa[0:R, t, i].unsqueeze(1).broadcast_to((R, H, 8)) for i in range(2)]
                tv = [rot_t[0:R, i, 0:64].rearrange("p (h d) -> p h d", h=H) for i in range(4)]
                order(rotate(x[:, :, 0:8], x[:, :, 8:16], tab[0], tab[1], tv))
                x = proj[t][0:R, C_CK:C_CK + 768].rearrange("p (y z g d) -> p y z g d", y=3, z=2, g=G)[:, :, 0]
                tab = [rot_nsa[0:R, t, i].unsqueeze(1).unsqueeze(1).broadcast_to((R, 3, G, 8)) for i in range(2)]
                tv = [rot_t[0:R, i, 0:48].rearrange("p (y g d) -> p y g d", y=3, g=G) for i in range(4)]
                rotate(x[:, :, :, 0:8], x[:, :, :, 8:16], tab[0], tab[1], tv).then_inc(rotated, 1)
                dve.wait_ge(rotated, t + 1)

            for unit in range(6):
                dve.wait_ge(cmp_done, unit + 1)
                bank = banks[4 + unit % 2]
                x = unit % 3
                if unit < 3:
                    R = P if x < 2 else BG
                    ins = ts(c_kT[0:HD, x * P:x * P + R], bank[0:HD, 0:R], cmp_bk[0:HD, :], None, ALU.add)
                elif x < 2:
                    ins = tt(c_v[:, x, :], bank[:, 0:HD], cmp_bv, ALU.add)
                else:
                    ins = tt(cv_out[0:BG, :], bank[0:BG, 0:HD], cmp_bv[0:BG, :], ALU.add)
                ins.then_inc(cmp_ready, 1)

            def wide(v, R, n=H, m=HD):
                return v.unsqueeze(2).broadcast_to((R, n, m))

            def heads(v, n=H):
                return v.rearrange("p (h d) -> p h d", h=n)

            def group_norm(o, sq, mean, R, n, t):
                order(red(mean, o, AX.X, ALU.add))
                order(ts(mean, mean, 1.0 / HD, None, ALU.mult))
                order(tt(o, o, wide(mean, R, n), ALU.subtract))
                order(tt(sq, o, o, ALU.mult))
                order(red(gn_v[0:R, 0:n], sq, AX.X, ALU.add))
                ts(gn_v[0:R, 0:n], gn_v[0:R, 0:n], 1.0 / HD, EPS, ALU.mult, ALU.add).then_inc(gn_var, 1)
                dve.wait_ge(gn_rstd, t + 1)
                order(tt(o, o, wide(gn_r[0:R, 0:n], R, n), ALU.mult))

            def branch_max(t, u):
                N = P * (t + 1)
                dve.wait_ge(sc_done, u + 1)
                red(neg_max[:, u % 16:u % 16 + 1], banks[u % 2][:, 0:N], AX.X, ALU.max, negate=True
                    ).then_inc(max_ready, 1)

            for t in range(PT):
                o, sq, x3, x4 = (heads(tmp[:, i, :]) for i in range(4))
                if t:
                    dve.wait_ge(ret_done, t)
                tt(vz, heads(proj[t][:, C_RV:C_RV + 512]), wide(zeta, P), ALU.mult).then_inc(vz_ready, 1)
                for m in range(2):
                    dve.wait_ge(att_done, 2 * t + m + 1)
                    tt(att[:, 4 * m:4 * m + 4, :], banks[2 + m][:, :].rearrange("p (k r) -> p k r", k=4),
                       decay[:, 4 * m:4 * m + 4, :], ALU.mult).then_inc(att_ready, 1)
                dve.wait_ge(cs_done, t + 1)
                cs3, cp3 = heads(cs_buf), heads(cp_buf)
                vis = cmp_vis[:, t, :].unsqueeze(1).broadcast_to((P, H, 8))
                neg = cmp_neg[:, t, :].unsqueeze(1).broadcast_to((P, H, 8))
                order(tt(cs3, heads(banks[7][:, 0:64]), neg, ALU.add))
                order(red(col[:, 0:8], cs3, AX.X, ALU.max))
                tt(cs3, cs3, wide(col[:, 0:8], P, H, 8), ALU.subtract).then_inc(cs_ready, 1)
                dve.wait_ge(cs_exp, t + 1)
                order(tt(cp3, cp3, vis, ALU.mult))
                order(red(col[:, 8:16], cp3, AX.X, ALU.add))
                order(ts(col[:, 8:16], col[:, 8:16], 1e-30, None, ALU.max))
                order(dve.reciprocal(col[:, 16:24], col[:, 8:16]))
                tt(cp3, cp3, wide(col[:, 16:24], P, H, 8), ALU.mult).then_inc(cp_ready, 1)
                dve.wait_ge(ret_done, t + 1)
                if t:
                    order(tt(o, heads(banks[4][:, :]), wide(xi, P), ALU.mult))
                    order(tt(o, o, heads(banks[5][:, :]), ALU.add))
                    order(tt(state[0:HD], state[0:HD], wide(g_chunk[0:HD], HD), ALU.mult))
                    tt(state[0:HD], state[0:HD], heads(banks[6][0:HD, :]), ALU.add).then_inc(state_ready, 1)
                else:
                    order(dve.tensor_copy(o, heads(banks[5][:, :])))
                    dve.tensor_copy(state[0:HD], heads(banks[6][0:HD, :])).then_inc(state_ready, 1)
                group_norm(o, sq, col[:, 24:32], P, H, t)
                order(tt(tmp[:, 0, :], tmp[:, 0, :], gn_gain, ALU.mult))
                dve.wait_ge(tanh_ready, 2 * t + 2)
                order(stt(out=tmp[:, 1, :], in0=tanh_rg, scalar=1.0, in1=proj[t][:, C_RG:C_RG + 512],
                          op0=ALU.add, op1=ALU.mult))
                stt(out=cat[:, t, 0:512], in0=tmp[:, 0, :], scalar=0.5, in1=tmp[:, 1, :], op0=ALU.mult, op1=ALU.mult)
                order(ts(gate, gate, 0.5, 0.5, ALU.mult, ALU.add))
                gate3 = gate.rearrange("p (h x) -> p h x", x=3)
                nsa = heads(cat[:, t, 512:1024])
                dve.wait_ge(co_done, t + 1)
                tt(nsa, heads(banks[2][:, :]), wide(gate3[:, :, 0], P), ALU.mult).then_inc(co_used, 1)
                dve.wait_ge(co_used, t + 1)
                u0 = 2 * H * t
                branch_max(t, u0)
                for u in range(u0, u0 + 2 * H):
                    if u + 1 < u0 + 2 * H:
                        branch_max(t, u + 1)
                    N = P * (t + 1)
                    dve.wait_ge(pT_done, u + 1)
                    dve.tensor_copy(probsT[:, u % 2, 0:N], banks[3 + u % 2][:, 0:N]).then_inc(pT_ready, 1)
                    if u % H == H - 1:
                        kind = u % 16 // H
                        dve.wait_ge(ao_done, 2 * t + kind + 1)
                        order(dve.reciprocal(gate_w, exp_sum[:, kind, :]))
                        order(tt(gate_w, gate_w, gate3[:, :, 1 + kind], ALU.mult))
                        tt(x3, heads(banks[5 + kind][:, :]), wide(gate_w, P), ALU.mult).then_inc(ao_used, 1)
                        dve.wait_ge(ao_used, 2 * t + kind + 1)
                        ins = tt(nsa, nsa, x3, ALU.add)
                        if kind:
                            ins.then_inc(cat_ready, 1)
                        else:
                            order(ins)

            dve.wait_ge(s_rows_in, 16 * N_SROWS)
            dve.wait_ge(s_state_in, 16)
            row = lambda i: s_rows[0:64, i, :]
            r64 = lambda v: v[0:64]
            q_d = row(S_RQ).unsqueeze(2).broadcast_to((64, HD, HD))
            k_d = row(S_RK).unsqueeze(2).broadcast_to((64, HD, HD))
            v_e = row(S_RV).unsqueeze(1).broadcast_to((64, HD, HD))
            order(tt(s_prod[0:64], s_state[0:64], q_d, ALU.mult))
            order(red(row(S_Y), s_prod[0:64].rearrange("p d e -> p e d"), AX.X, ALU.add))
            order(ts(row(S_Y), row(S_Y), gamma1[0:64, :], None, ALU.mult))
            order(dve.tensor_tensor_reduce(out=row(S_U), in0=row(S_RQ), in1=row(S_RK), scale=1.0, scalar=0.0,
                                           op0=ALU.mult, op1=ALU.add, accum_out=col[0:64, 8:9]))
            order(stt(out=row(S_Y), in0=row(S_RV), scalar=col[0:64, 8:9], in1=row(S_Y), op0=ALU.mult, op1=ALU.add))
            order(tt(s_prod[0:64], k_d, v_e, ALU.mult))
            stt(out=s_state[0:64].rearrange("p d e -> p (d e)"), in0=s_state[0:64].rearrange("p d e -> p (d e)"),
                scalar=gamma1[0:64, :], in1=s_prod[0:64].rearrange("p d e -> p (d e)"),
                op0=ALU.mult, op1=ALU.add).then_inc(s_branch, 1)
            y3 = row(S_Y).unsqueeze(1)
            group_norm(y3, row(S_U).unsqueeze(1), col[0:64, 9:10], 64, 1, PT)
            order(tt(row(S_Y), row(S_Y), gn_rows[0:64, :], ALU.mult))
            dve.wait_ge(tanh_ready, 2 * PT + 2)
            order(stt(out=row(S_U), in0=row(S_T), scalar=1.0, in1=row(S_RG), op0=ALU.add, op1=ALU.mult))
            order(stt(out=row(S_Y), in0=row(S_Y), scalar=0.5, in1=row(S_U), op0=ALU.mult, op1=ALU.mult))
            order(ts(gate[0:64, 0:3], gate[0:64, 0:3], 0.5, 0.5, ALU.mult, ALU.add))
            dve.wait_ge(sT_ready, 1)
            tt(q_mask[0:64], own_q[0:64], sqT[0:64, :].unsqueeze(1).broadcast_to((64, BG, 64)), ALU.mult
               ).then_inc(qmask_ready, 1)
            dve.wait_ge(s_sc_done, 1)
            order(tt(s_scores[0:64, 0:256], banks[1][0:64, 0:256], own_neg[0:64, :], ALU.add))
            red(neg_max[0:64, 0:1], s_scores[0:64, 0:256], AX.X, ALU.max, negate=True).then_inc(s_max, 1)
            dve.wait_ge(s_exp, 1)
            order(dve.reciprocal(col[0:64, 10:11], exp_sum[0:64, 0, 0:1]))
            order(ts(cmp_p[0:64, :], cmp_p[0:64, :], col[0:64, 10:11], None, ALU.mult))
            order(red(s_small[0:64, 0:32], cmp_p[0:64, :].rearrange("p (x y) -> p y x", x=8), AX.X, ALU.add))
            red(s_small[0:64, 32:48].rearrange("p (i k) -> p i k", k=2),
                s_small[0:64, 0:32].rearrange("p (i g k) -> p i k g", g=G, k=2), AX.X, ALU.add).then_inc(s_imp, 1)
            dve.wait_ge(s_o_done, 1)
            order(ts(s_o[0:64, 3, :], banks[3][0:64, 0:64], gate[0:64, 0:1], None, ALU.mult))
            imp, eq, key = (s_small[0:64, x:x + 16] for x in (48, 64, 80))
            tt(imp, banks[3][0:64, 64:80], blk_excl[0:64, :], ALU.add).then_inc(s_branch, 1)
            dve.wait_ge(s_branch, 2)
            order(red(col[0:64, 11:12], imp, AX.X, ALU.min))
            order(ts(eq, imp, col[0:64, 11:12], None, ALU.is_equal))
            order(tt(key, eq, blk_rank[0:64, :], ALU.mult))
            order(red(col[0:64, 12:13], key, AX.X, ALU.max))
            order(ts(drop_neg[0:64, :], key, col[0:64, 12:13], NEG, ALU.is_equal, ALU.mult))
            for kind, nj in enumerate((8, 4)):
                N = nj * P
                dve.wait_ge(s_sc_done, 2 + kind)
                for cc in range(nj // 4):
                    if kind == 0:
                        v = "p (j y x) -> p j y x"
                        ins = tt(s_scores[0:64, cc * 512:(cc + 1) * 512].rearrange(v, j=4, y=16),
                                 banks[4 + cc][0:64, :].rearrange(v, j=4, y=16),
                                 drop_neg[0:64, :].unsqueeze(1).unsqueeze(3).broadcast_to((64, 4, 16, 8)), ALU.add)
                    else:
                        ins = dve.tensor_copy(s_scores[0:64, 0:512], banks[4][0:64, :])
                order(ins)
                if kind == 1:
                    order(ts(s_scores[0:64, 0:1], s_scores[0:64, 0:1], NEG, None, ALU.add))
                order(dve.tensor_tensor_reduce(out=row(S_U), in0=row(S_NQ), in1=row((S_SK, S_WK)[kind]), scale=0.125,
                                               scalar=0.0, op0=ALU.mult, op1=ALU.add,
                                               accum_out=s_scores[0:64, N:N + 1]))
                red(neg_max[0:64, 1 + kind:2 + kind], s_scores[0:64, 0:N + 1], AX.X, ALU.max, negate=True
                    ).then_inc(s_max, 1)
                dve.wait_ge(s_exp, 2 + kind)
                order(dve.reciprocal(col[0:64, 13:14], exp_sum[0:64, 0, 1 + kind:2 + kind]))
                order(tt(col[0:64, 13:14], col[0:64, 13:14], gate[0:64, 1 + kind:2 + kind], ALU.mult))
                dve.wait_ge(s_o_done, 2 + kind)
                order(stt(out=s_o[0:64, 1, :], in0=row((S_SV, S_WV)[kind]), scalar=s_probs[0:64, N:N + 1],
                          in1=banks[3][0:64, 0:64], op0=ALU.mult, op1=ALU.add))
                stt(out=s_o[0:64, 3, :], in0=s_o[0:64, 1, :], scalar=col[0:64, 13:14], in1=s_o[0:64, 3, :],
                    op0=ALU.mult, op1=ALU.add).then_inc(s_branch, 1)
                dve.wait_ge(s_branch, 3 + kind)

            for t in range(2):
                normed(hn_buf2[:, (NT + t) % 2, :], mem_x[:, t, :], MEMN)
            n = 0
            for t in range(NT):
                R = rows_of(t)
                for half in range(2):
                    dve.wait_ge(out_done, n + 1)
                    hv = h[0:R, t, half * 512:(half + 1) * 512]
                    tt(hv, hv, banks[2 + n % 4][0:R, :], ALU.add).then_inc(out_added, 1)
                    n += 1
            for t in range(NT):
                normed(hn_buf2[:, (NT + 2 + t) % 2, :], h[0:rows_of(t), t, :], MEM)

            def mem_max(v):
                dve.wait_ge(m_sc_done, v + 1)
                R = P if v < PT * HM else 32
                b = v % 2 if v < PT * HM else 2
                red(neg_max[0:R, v % 2:v % 2 + 1], banks[b][0:R, 0:NMEM], AX.X, ALU.max, negate=True
                    ).then_inc(m_max, 1)

            mem_max(0)
            for v in range(PT * HM + 1):
                last = v == PT * HM
                if v + 1 < PT * HM:
                    mem_max(v + 1)
                R = 32 if last else P
                if last:
                    dve.wait_ge(qm_ready, 2 * HM)
                    dve.wait_ge(memkv_in, 48)
                    tt(qm_mask.rearrange("p c (h b) -> p c h b", h=HM), own_m.rearrange("p c (h b) -> p c h b", h=HM),
                       qT_m[:, :, 512:520].unsqueeze(1).broadcast_to((P, 32, HM, DB)), ALU.mult).then_inc(m_qmask, 1)
                    mem_max(v)
                dst = ms_probs if last else m_probs[:, v % 2, :]
                dve.wait_ge(m_exp, v + 1)
                order(dve.reciprocal(col[0:R, 14:15], exp_sum[0:R, 0, v % 2:v % 2 + 1]))
                ts(dst[0:R, :], dst[0:R, :], col[0:R, 14:15], None, ALU.mult).then_inc(m_norm, 1)
            n = 0
            for t in range(NT):
                R = rows_of(t)
                for half in range(2):
                    dve.wait_ge(mo_done, n + 1)
                    hv = h[0:R, t, half * 512:(half + 1) * 512]
                    tt(hv, hv, banks[(5, 6, 7, 0)[n % 4]][0:R, :], ALU.add).then_inc(mo_added, 1)
                    n += 1

            for t in range(NT):
                normed(hn3[:, t, :], h[0:rows_of(t), t, :], FFN)
            dve.memset(skT, 0.0).then_inc(sk_zero, 1)
            for t in range(NT):
                R = rows_of(t)
                dve.wait_ge(ps_ready, 4 * (t + 1))

                def top16(vals, idx, src, n):
                    for x in range(n):
                        ins = dve.max(vals[0:R, x, 0:8], src[0:R, x, :])
                    order(ins)
                    for x in range(n):
                        dve.max_index(idx[0:R, x, 0:8], vals[0:R, x, 0:8], src[0:R, x, :])
                        ins = dve.match_replace(src[0:R, x, :], vals[0:R, x, 0:8], src[0:R, x, :], -3.0e38)
                    order(ins)
                    for x in range(n):
                        ins = dve.max(vals[0:R, x, 8:16], src[0:R, x, :])
                    order(ins)
                    for x in range(n):
                        ins = dve.max_index(idx[0:R, x, 8:16], vals[0:R, x, 8:16], src[0:R, x, :])
                    order(ins)

                top16(top_v, top_i, s_all, 16)
                order(dve.tensor_copy(top_f[0:R], top_i[0:R]))
                for hh in range(H):
                    ins = tt(cand[0:R, hh, :].rearrange("p (i j) -> p i j", i=TOPK),
                             top_v[0:R, 2 * hh, :].unsqueeze(2).broadcast_to((R, TOPK, TOPK)),
                             top_v[0:R, 2 * hh + 1, :].unsqueeze(1).broadcast_to((R, TOPK, TOPK)), ALU.add)
                order(ins)
                top16(best_v, best_i, cand, H)
                flat = best_i[0:R].rearrange("p h k -> p (h k)")
                ts(ab_i[0:R, 0, :], flat, 4, None, ALU.logical_shift_right)
                order(ts(ab_i[0:R, 1, :], flat, 15, None, ALU.bitwise_and))
                order(dve.tensor_copy(ab_f[0:R], ab_i[0:R]))
                for x in range(2):
                    order(tt(onehot[0:R], ab_f[0:R, x, :].unsqueeze(2).broadcast_to((R, SLOTS, 16)),
                             iota16[0:R].unsqueeze(1).broadcast_to((R, SLOTS, 16)), ALU.is_equal))
                    for hh in range(H):
                        v = onehot[0:R, hh * TOPK:(hh + 1) * TOPK, :]
                        ins = tt(v, v, top_f[0:R, 2 * hh + x, :].unsqueeze(1).broadcast_to((R, TOPK, 16)), ALU.mult)
                    order(ins)
                    order(red(pick[0:R, x, :], onehot[0:R], AX.X, ALU.add))
                tt(best_e[0:R], best_v[0:R], best_v[0:R, :, 0:1].broadcast_to((R, H, TOPK)), ALU.subtract
                   ).then_inc(best_shift, 1)
                order(stt(out=pick[0:R, 0, :], in0=pick[0:R, 0, :], scalar=float(NKEY), in1=pick[0:R, 1, :],
                          op0=ALU.mult, op1=ALU.add))
                if t < PT:
                    order(dve.tensor_copy(expert[0:R, t, :], pick[0:R, 0, :]))
                dve.wait_ge(best_exp, t + 1)
                order(red(col[0:R, 16:24], best_e[0:R], AX.X, ALU.add))
                order(dve.reciprocal(col[0:R, 24:32], col[0:R, 16:24]))
                tt(heads(gates_p[0:R, t, :]), best_e[0:R], wide(col[0:R, 24:32], R, H, TOPK), ALU.mult
                   ).then_inc(routed, 1)
            dve.wait_ge(rt_done, 1)
            dve.tensor_copy(gate_s, banks[0][:, DB:2 * DB])
            dve.tensor_copy(expert_s[:, :], banks[0][:, 0:DB]).then_inc(routed, 1)
            dve.wait_ge(routed, NT + 1)

            def expert_weights(c_out, x, g, n, t):
                w = gtmp[:, :, 0:n]
                order(tt(w[:, 0, :], x, x, ALU.mult))
                order(ts(w[:, 0, :], w[:, 0, :], GELU_A, 1.0, ALU.mult, ALU.add))
                tt(w[:, 0, :], w[:, 0, :], x, ALU.mult).then_inc(gelu_in, 1)
                dve.wait_ge(gelu_tanh, t + 1)
                order(stt(out=w[:, 1, :], in0=w[:, 0, :], scalar=1.0, in1=x, op0=ALU.add, op1=ALU.mult))
                order(stt(out=c_out, in0=w[:, 1, :], scalar=0.5, in1=g, op0=ALU.mult, op1=ALU.mult))

            turns = 0
            for t in range(PT):
                with dve.Fori(0, TURNS) as i:
                    for k in range(RING):
                        dve.wait_ge(row_in[k], (i + (turns + 1)) * 16)
                        dve.tensor_tensor_reduce(out=ring[:, k, :], in0=ring[:, k, :], in1=hn3[:, t, :], scale=1.0,
                                                 scalar=0.0, op0=ALU.mult, op1=ALU.add,
                                                 accum_out=act_turn[:, k:k + 1]).then_inc(row_used, 1)
                    dve.wait_ge(row_used, (i + (turns + 1)) * RING)
                    dve.tensor_copy(act_p[:, bass.ds(i * RING, RING)], act_turn).then_inc(act_kept, 1)
                    dve.wait_ge(act_kept, i + (turns // 2 + 1))
                turns += TURNS
                dve.wait_ge(row_used, turns * RING)
                expert_weights(coef, act_p, gates_p[:, t, :], SLOTS, t)
                with dve.Fori(0, TURNS) as i:
                    for k in range(RING):
                        dve.wait_ge(row_in[k], (i + (turns + 1)) * 16)
                        dve.wait_ge(row_used, (i + turns) * RING + k)
                        stt(out=h[:, t, :], in0=ring[:, k, :], scalar=coef[:, bass.ds(i * RING + k, 1)],
                            in1=h[:, t, :], op0=ALU.mult, op1=ALU.add).then_inc(row_used, 1)
                turns += TURNS
                dve.wait_ge(row_used, turns * RING)
                dve.tensor_copy(acc[:, 0:1], coef[:, 0:1]).then_inc(x_done, 1)
            dve.wait_ge(hns_in, 16)
            for b in range(DB):
                dve.wait_ge(row_in[b], 16 * (turns + 1))
                dve.tensor_tensor_reduce(out=ring[:, b, :], in0=ring[:, b, :], in1=hn_s[:, b, :], scale=1.0,
                                         scalar=0.0, op0=ALU.mult, op1=ALU.add,
                                         accum_out=act_p[:, b:b + 1]).then_inc(row_used, 1)
            dve.wait_ge(row_used, turns * RING + DB)
            expert_weights(coef[:, 0:DB], act_p[:, 0:DB], gate_s, DB, PT)
            tt(coef_m, eye8, coef[:, 0:DB].unsqueeze(1).broadcast_to((P, DB, DB)), ALU.mult).then_inc(coefm_ready, 1)
            dve.wait_ge(se_done, 1)
            for half in range(2):
                hv = h[0:DB, SAMPLE, half * 512:(half + 1) * 512]
                ins = tt(hv, hv, banks[6 + half][0:DB, :], ALU.add)
            ins.then_inc(x_done, 1)
            for t in range(NT):
                n = norms[0]
                norms[0] += 1
                R = rows_of(t)
                dve.wait_ge(rstd_ready, n + 1)
                stt(out=hn3[0:R, t, :], in0=h[0:R, t, :], scalar=rstd[0:R, n % 16:n % 16 + 1], in1=gain[0:R, FIN, :],
                    op0=ALU.mult, op1=ALU.mult).then_inc(y_ready, 1)


def shape_constants():
    import numpy as np
    f = np.float32
    c = {}
    c["ident"] = np.eye(P, dtype=f)
    q, k = np.arange(P)[:, None], np.arange(P)[None, :]
    c["tri"] = np.where(k <= q, 0.0, NEG).astype(f)
    lg = np.log(f(1.0) - f(2.0) ** (-5.0 - np.arange(H, dtype=f))).astype(f)
    lg = lg.astype(np.float64)
    diff = (k - q).astype(np.float64)
    c["decay"] = np.where(diff[:, None, :] >= 0, np.exp(lg[None, :, None] * np.maximum(diff, 0)[:, None, :]), 0.0).astype(f)
    i = np.arange(P, dtype=np.float64)[:, None]
    c["xi"] = np.exp(lg[None, :] * (i + 1)).astype(f)
    c["zeta"] = np.exp(lg[None, :] * (P - 1 - i)).astype(f)
    c["g_chunk"] = np.broadcast_to(np.exp(lg * P)[None, :], (P, H)).astype(f)
    c["gamma1"] = np.tile(np.exp(lg), DB)[:, None].astype(f)
    tok = np.arange(SEQ).reshape(PT, P)
    blk_end = np.arange(8) * CMP + CMP - 1
    vis = (blk_end[None, None, :] <= tok[:, :, None]).transpose(1, 0, 2)
    c["cmp_vis"] = vis.astype(f)
    c["cmp_neg"] = np.where(vis, 0.0, NEG).astype(f)
    pos = np.concatenate([tok, np.full((1, P), PAST)]).astype(f).T

    def table(half, theta):
        inv = (f(theta) ** (-np.arange(half, dtype=f) / f(half))).astype(f)
        ang = (pos[:, :, None] * inv).astype(f).astype(np.float64)
        return np.cos(ang), np.sin(ang)
    cos, sin = table(32, 10000.0)
    scale = np.array([1.0, HD ** -0.5])[None, None, :, None]
    c["rot_ret"] = np.stack([cos[:, :, None] * scale, sin[:, :, None] * scale], 2).astype(f)
    cos, sin = table(8, 500000.0)
    c["rot_nsa"] = np.stack([cos, sin], 2).astype(f)
    qs = np.arange(64)
    blk = np.arange(256)
    own = (qs[:, None] // H == blk[None, :] // 32) & (qs[:, None] // R4 % G == blk[None, :] // 2 % G)
    c["own_neg"] = np.where(own, 0.0, NEG).astype(f)
    c["group"] = (qs[:, None] // R4 == qs[None, :] // R4).astype(f)
    c["blk_excl"] = np.broadcast_to(np.where(np.arange(16) == 0, 1e4, 0.0), (64, 16)).astype(f)
    c["blk_rank"] = np.broadcast_to(np.arange(1.0, 17.0), (64, 16)).astype(f)
    p = np.arange(P)
    c["row_add"] = np.stack([p % 4, p % 16, p % 16 + 16], 1).astype(f)
    c["iota16"] = np.broadcast_to(np.arange(16), (P, 16)).astype(f)
    c["eye8"] = np.broadcast_to(np.eye(DB), (P, DB, DB)).astype(f)
    c["own_q"] = np.broadcast_to((np.arange(BG)[:, None] == qs[None, :] // R4)[None], (64, BG, 64)).astype(f)
    c["own_m"] = np.broadcast_to(np.eye(32), (P, 32, 32)).astype(f)
    return {k: np.ascontiguousarray(v) for k, v in c.items()}


_DIRECT = ["x_prompt", "x_sample", "mem_prompt", "state_ret", "cache_cmp_k", "cache_cmp_v", "cache_slc_k",
           "cache_slc_v", "cache_win_k", "cache_win_v", "cache_mem_k", "cache_mem_v", "cmp_w", "peer_subkeys",
           "peer_u", "peer_v", "norm_final_g"]
_LAYER = ["norm_mix_g", "w_in", "w_out", "norm_mem_g", "mem_norm_g", "w_mq", "w_mk", "w_mv", "w_mo", "norm_ffn_g",
          "peer_wq"]
_OUTS = [("y_prompt", (1, SEQ, D)), ("y_sample", (DB, 1, D)), ("p_state", (1, 1, H, HD, HD)),
         ("p_cmp_k", (1, 1, PT, G, P, HD)), ("p_cmp_v", (1, 1, PT, G, P, HD)),
         ("p_slc_k", (1, 1, PT, G, P, HD)), ("p_slc_v", (1, 1, PT, G, P, HD)),
         ("p_win_k", (1, 1, G, 512, HD)), ("p_win_v", (1, 1, G, 512, HD)),
         ("p_mem_k", (1, 1, NMEM, HM, HDM)), ("p_mem_v", (1, 1, NMEM, HM, HDM)),
         ("s_state", (1, DB, H, HD, HD)),
         ("s_cmp_k", (1, DB, G, 1, HD)), ("s_cmp_v", (1, DB, G, 1, HD)),
         ("s_slc_k", (1, DB, G, 1, HD)), ("s_slc_v", (1, DB, G, 1, HD)),
         ("s_win_k", (1, DB, G, 512, HD)), ("s_win_v", (1, DB, G, 512, HD))]


def kernel(**inputs):
    import numpy as np
    import concourse.bacc as bacc
    from concourse.bass_utils import run_bass_kernel_spmd

    arrays = {}
    for name in _DIRECT:
        arrays[name] = np.ascontiguousarray(inputs[name])
    for name in _LAYER:
        arrays[name] = np.ascontiguousarray(inputs[name])[0]
    table = np.asarray(inputs["page_table"]).astype(np.int32)
    arrays["page_rows"] = np.concatenate([np.repeat(table.reshape(2, 32), 4, axis=1).T,
                                          np.repeat(table.T, 16, axis=0)], axis=1)
    gn = np.asarray(inputs["ret_gn_g"])[0]
    consts = shape_constants()
    consts["gn_gain"] = np.broadcast_to(gn[None, :], (P, 512))
    consts["gn_rows"] = np.tile(gn.reshape(H, HD), (DB, 1))
    consts["cmp_bv"] = np.broadcast_to(np.asarray(inputs["cmp_b"])[0, 1][None, :], (P, HD))
    consts["cmp_bk"] = np.asarray(inputs["cmp_b"])[0, 0][:, None]

    nc = bacc.Bacc("TRN2", target_bir_lowering=False, num_devices=1)

    def declare(group, prefix):
        aps = {}
        for name, value in group.items():
            value = np.ascontiguousarray(value)
            feed[prefix + name] = value
            aps[name] = nc.dram_tensor(prefix + name, value.shape, mybir.dt.from_np(value.dtype),
                                       kind="ExternalInput").ap()
        return aps

    feed = {}
    a = declare(arrays, "in_")
    c = declare(consts, "const_")
    out = {name: nc.dram_tensor("out_" + name, shape, F32, kind="ExternalOutput").ap() for name, shape in _OUTS}
    trunk_kernel(nc, a, c, out)
    r = run_bass_kernel_spmd(nc, [feed], core_ids=[0])
    return tuple(r.results[0]["out_" + name] for name, _ in _OUTS)
```

```python
from contextlib import ExitStack

import concourse.bass as bass
from concourse import mybir

ALU = mybir.AluOpType
ACT = mybir.ActivationFunctionType
AX = mybir.AxisListType
F32 = mybir.dt.float32
U32 = mybir.dt.uint32

P = 128
D = 1024
KC = D // P
SEQ = 512
PT = SEQ // P
DB = 8
NT = PT + 1
SAMPLE = PT
H = 8
HD = 64
G = 2
R4 = H // G
CMP = 64
PAST = 1024
PAGES = PAST // P
BG = DB * G
NMEM = 256
HM = 4
HDM = 128
NKEY = 128
TOPK = 16
SLOTS = H * TOPK
D_IN = 4 * 512 + 512 + 6 * P + 3 * H
C_RQ, C_RK, C_RV, C_RG, C_NQ, C_CK, C_CV, C_SK, C_SV, C_WK, C_WV, C_NG = (
    0, 512, 1024, 1536, 2048, 2560, 2688, 2816, 2944, 3072, 3200, 3328)
CHUNKS = [(c, min(512, D_IN - c)) for c in range(0, D_IN, 512)]
EPS = 1e-6
NEG = -1.0e30
RING = 8
TURNS = SLOTS // RING
ROWS = 2 * SLOTS
STEP_TURNS = ((1, 1), (2, 2), (3, 3), (4, 5), (5, 8), (6, 9), (7, 21), (8, 25), (9, 26), (10, 28), (11, 30),
              (12, 31), (13, 32), (14, 33), (15, 38), (16, 39), (17, 43), (18, 44), (19, 45), (20, 46), (21, 47),
              (22, 51), (23, 52), (24, 56), (25, 57), (26, 62))
GELU_A = 0.044715
GELU_B = 0.7978845608028654


def rows_of(t):
    return P if t < PT else DB


class Arena:

    def __init__(self, tensor, at, end):
        self.tensor, self.at, self.end = tensor, at, end

    def take(self, *shape):
        n = 1
        for s in shape:
            n *= s
        a = self.at
        self.at += n
        assert self.at <= self.end, (self.at, self.end)
        v = self.tensor[:, a:a + n]
        names = "abcd"[:len(shape)]
        if len(shape) > 1:
            v = v.rearrange(f"p ({' '.join(names)}) -> p {' '.join(names)}", **dict(zip(names, shape)))
        return v

    def part(self, off, size):
        return Arena(self.tensor, self.at + off, self.at + off + size)


def trunk_kernel(nc, a, c, out):
    with ExitStack() as ctx:
        def sb(name, shape, dt=F32):
            return ctx.enter_context(nc.sbuf_tensor(name, shape, dt))

        def sem(name):
            return ctx.enter_context(nc.semaphore(name))

        def scratch(name, shape):
            return nc.dram_tensor(name, shape, F32, kind="Internal").ap()

        banks = [ctx.enter_context(nc.psum_tensor(f"bank{i}", [P, 512], F32)) for i in range(8)]

        sc_heads = scratch("sc_heads", (5, DB, 512))
        sc_gates = scratch("sc_gates", (DB, 3 * H))
        sc_cv = scratch("sc_cv", (BG, HD))
        sc_cat = scratch("sc_cat", (2, DB, 512))
        sc_hn = scratch("sc_hn", (DB, D))

        words = 51900
        arena = sb("arena", [P, words])
        base = Arena(arena, 0, words)
        h = base.take(NT, D)
        gain = base.take(3, D)
        MIX, MEM, FFN = range(3)
        eps_col = base.take(1)
        waited = base.take(1)
        gn_rows = base.take(HD)
        cmp_bv = base.take(HD)
        cmp_bk = base.take(1)
        ident = base.take(P)
        xi = base.take(H)
        zeta = base.take(H)
        g_chunk = base.take(H)
        gamma1 = base.take(1)
        cmp_vis = base.take(PT, H)
        cmp_neg = base.take(PT, H)
        own_neg = base.take(256)
        group = base.take(64)
        blk_excl = base.take(16)
        blk_rank = base.take(16)
        page_f = base.take(10)
        row_add = base.take(3)
        iota16 = base.take(16)
        eye8 = base.take(DB, DB)
        mean_sq = base.take(16)
        rstd = base.take(16)
        gn_v = base.take(H)
        gn_r = base.take(H)
        neg_max = base.take(16)
        exp_sum = base.take(2, H)
        gate = base.take(3 * H)
        gate_w = base.take(H)
        drop_neg = base.take(16)
        c_kT = base.take(272)
        c_v = base.take(2, HD)
        col = base.take(160)
        blk_idx = sb("blk_idx", [P, 2], U32)
        row_idx = sb("row_idx", [P, BG], U32)
        page_i = sb("page_i", [P, 10], mybir.dt.int32)
        x0 = base.at
        XW = words - x0

        proj = [base.part(t * D_IN, D_IN).take(D_IN) for t in range(NT)]
        cat = base.part(NT * D_IN, NT * D).take(NT, D)
        r2 = NT * D_IN + NT * D
        MIXC = 512 + P + H * P + NT * 128 + NT * 16 + 512
        R2W = XW - r2 - MIXC
        ar = base.part(XW - MIXC, MIXC)
        gn_gain = ar.take(512)
        tri = ar.take(P)
        decay = ar.take(H, P)
        rot_ret = ar.take(NT, 2, 2, 32)
        rot_nsa = ar.take(NT, 2, 8)
        c_vblk = ar.take(512)
        ar = base.part(r2, R2W)
        hnT = ar.take(KC, 520)
        hn_buf = ar.take(2, D)
        w_buf = ar.take(2, KC, 512)
        sq_junk = cat[:, 0, :]
        ar = base.part(r2, R2W)
        blk_buf = ar.take(2, CMP * HD)
        cmp_w = ar.take(2, 32, HD)
        blkT = ar.take(2, 4, P)
        cv_out = ar.take(HD)
        ar = base.part(r2, R2W)
        rqT = ar.take(H, P)
        rkT = ar.take(H, P)
        nqT = ar.take(H, P)
        kT = ar.take(2, G, SEQ)
        att = ar.take(H, P)
        probs = ar.take(2, SEQ)
        probsT = ar.take(2, SEQ)
        state = ar.take(H, HD)
        vz = ar.take(H, HD)
        tmp = ar.take(4, 512)
        rot_t = tmp
        tanh_rg = ar.take(512)
        cs_buf = ar.take(64)
        cp_buf = ar.take(64)
        cpT = ar.take(P)
        W_BANK, RING_AT, AREA2 = 0, KC * D, 2 * KC * D
        AREA2W = r2 - 2 * D - AREA2
        ar = base.part(r2, XW - r2)
        hn3 = ar.take(NT, D)
        s_all = ar.take(2, H * 256)
        s_held = hn3[:, 3:NT, :].rearrange("p t n -> p (t n)")
        skT = ar.take(H, 256)
        mv = ar.take(2, 512)
        mkT = ar.take(HM, NMEM)
        act_p = ar.take(SLOTS)
        act_part = ar.take(32)
        coef = ar.take(SLOTS)
        gate_t = ar.take(SLOTS)
        gtmp = ar.take(2, SLOTS)
        gate_s = ar.take(DB)
        coef_m = ar.take(DB, DB)
        s_head = ar.take(2, NKEY)
        cand = ar.take(256)
        onehot = ar.take(2, TOPK, 16)
        top_v = ar.take(2, TOPK)
        top_f = ar.take(2, TOPK)
        head_v = ar.take(TOPK)
        best_v = ar.take(2, SLOTS)
        best_e = ar.take(SLOTS)
        ab_f = ar.take(2, TOPK)
        pick = ar.take(2, TOPK)
        expert_f = ar.take(SLOTS)
        AREA1, AREA1W = ar.at - x0, XW - (ar.at - x0)
        top_i = sb("top_i", [P, 2, TOPK], U32)
        head_i = sb("head_i", [P, TOPK], U32)
        ab_i = sb("ab_i", [P, 2, TOPK], U32)
        expert = sb("expert", [P, PT, SLOTS], U32)
        expert_s = sb("expert_s", [P, DB], U32)
        cursor = sb("cursor", [P, RING], U32)
        ring = base.part(RING_AT, RING * D).take(RING, D)
        hn_s = base.part(W_BANK, DB * D).take(DB, D)

        ar = base.part(W_BANK, BG * 512)
        key_rows = ar.take(BG, 512)
        val_rows = key_rows
        ar = base.part(W_BANK, BG * 512)
        win_keys = ar.take(BG, 256)
        win_vals = ar.take(BG, 256)
        ar = base.part(W_BANK, BG * 512)
        s_state = ar.take(HD, HD)
        s_prod = ar.take(HD, HD)
        ar = base.part(AREA2, AREA2W)
        q_mask = ar.take(BG, 64)
        own_q = ar.take(BG, 64)
        keyT = ar.take(2, 512)
        cmp_p = ar.take(256)
        ar = base.part(AREA1, AREA1W)
        s_scores = ar.take(1028)
        s_probs = s_scores
        s_probsT = ar.take(8, 64)
        s_rows = ar.take(12, HD)
        cmp_pT = ar.take(2, 64)
        s_small = ar.take(96)
        s_o = ar.take(4, HD)
        sqT = ar.take(64)
        ar = base.part(W_BANK, KC * D)
        w_mk = ar.take(KC, 512)
        w_mv = ar.take(KC, 512)
        mem_x = s_all[:, 0, :].rearrange("p (t n) -> p t n", t=2)
        memn_gain = hn3[:, 3, :]
        sub_k = hn3[:, SAMPLE, :].rearrange("p (h n) -> p h n", h=H)
        ar = base.part(AREA1, AREA1W)
        mT = ar.take(KC, NMEM)
        mk = ar.take(2, 512)
        ar = base.part(W_BANK, KC * D)
        w_mq = ar.take(KC, 512)
        w_mo = ar.take(HM, D)
        mem_piece = base.part(W_BANK, 4 * D).take(4, D)

        class Group:
            pass

        front, back = Group(), Group()
        front.tiles, back.tiles = (0, 1, 2), (3, SAMPLE)
        front.width, back.width = 3 * P, P + DB
        front.at, back.at = {0: 0, 1: P, 2: 2 * P}, {3: 0, SAMPLE: P}
        front.w_out = front.wq = base.part(RING_AT, KC * D).take(KC, D)
        back.w_out = back.wq = base.part(W_BANK, KC * D).take(KC, D)
        front.hnT = base.part(AREA1, AREA1W).take(KC, front.width)
        catT2 = s_all[:, 1, :].rearrange("p (b k r) -> p b k r", b=2, k=KC)
        front.catT = {t: catT2[:, t % 2] for t in front.tiles}
        ar = base.part(NT * D_IN, 3 * D)
        front.qT_m = ar.take(HM, front.width)
        front.oT_m = ar.take(HM, front.width)
        front.qT_p = base.part(NT * D_IN, 3 * D).take(H, front.width)
        probs_at = s_all[:, 0, :].rearrange("p (x b n) -> p x b n", x=4, b=2)
        front.m_probs, front.m_probsT = probs_at[:, 0], probs_at[:, 1]
        ar = base.part(AREA1, AREA1W)
        back.hnT = ar.take(KC, back.width)
        back.catT = {t: back.hnT[:, :, back.at[t]:back.at[t] + rows_of(t)] for t in back.tiles}
        back.qT_p = Arena(arena, ar.at, ar.end).take(H, back.width)
        back.qT_m = ar.take(HM, back.width)
        back.oT_m = ar.take(HM, back.width)
        back.m_probs = ar.take(2, NMEM)
        back.m_probsT = ar.take(2, NMEM)
        ar = base.part(AREA2, AREA2W)
        qm_mask = ar.take(32, 32)
        own_m = ar.take(32, 32)
        mkT_s = ar.take(2, 512)
        ms_probs = ar.take(NMEM)
        ms_probsT = ar.take(2, 32)

        x_in = sem("x_in")
        consts_in = sem("consts_in")
        eps_set = sem("eps_set")
        mean_ready = sem("mean_ready")
        std_ready = sem("std_ready")
        hn_ready = sem("hn_ready")
        hnT_done = sem("hnT_done")
        hnT_ready = sem("hnT_ready")
        w_in_loaded = [sem("w_in_even"), sem("w_in_odd")]
        proj_done = sem("proj_done")
        proj_ready = sem("proj_ready")
        rotated = sem("rotated")
        rows_stored = sem("rows_stored")
        idx_ready = sem("idx_ready")
        blk_in = [sem("blk_even"), sem("blk_odd")]
        own_blk_in = sem("own_blk_in")
        cmpw_in = sem("cmpw_in")
        blkT_done = sem("blkT_done")
        blkT_ready = sem("blkT_ready")
        cmp_done = sem("cmp_done")
        cmp_ready = sem("cmp_ready")
        cv_stored = sem("cv_stored")
        vblk_in = sem("vblk_in")
        vblk_zero = sem("vblk_zero")
        headT_done = sem("headT_done")
        headT_ready = sem("headT_ready")
        att_done = sem("att_done")
        att_ready = sem("att_ready")
        vz_ready = sem("vz_ready")
        ret_done = sem("ret_done")
        state_ready = sem("state_ready")
        cs_done = sem("cs_done")
        cs_ready = sem("cs_ready")
        cs_exp = sem("cs_exp")
        cp_ready = sem("cp_ready")
        cpT_done = sem("cpT_done")
        cpT_ready = sem("cpT_ready")
        co_done = sem("co_done")
        co_used = sem("co_used")
        sc_done = sem("sc_done")
        max_ready = sem("max_ready")
        exp_ready = sem("exp_ready")
        pT_done = sem("pT_done")
        pT_ready = sem("pT_ready")
        ao_done = sem("ao_done")
        ao_used = sem("ao_used")
        tanh_ready = sem("tanh_ready")
        gate_exp = sem("gate_exp")
        cat_ready = sem("cat_ready")
        state_stored = sem("state_stored")
        s_rows_in = sem("s_rows_in")
        s_state_in = sem("s_state_in")
        s_stored = sem("s_stored")
        s_cat_in = sem("s_cat_in")
        cat_stored = sem("cat_stored")
        sT_done = sem("sT_done")
        sT_ready = sem("sT_ready")
        qmask_ready = sem("qmask_ready")
        key_in = [sem("page_keys_in"), sem("window_keys_in")]
        val_in = [sem("page_values_in"), sem("window_values_in")]
        gn_var = sem("gn_var")
        gn_std = sem("gn_std")
        s_keyT_done = sem("s_keyT_done")
        s_keyT_ready = sem("s_keyT_ready")
        s_sc_done = sem("s_sc_done")
        s_max = sem("s_max")
        s_exp = sem("s_exp")
        s_pT_done = sem("s_pT_done")
        s_pT_ready = sem("s_pT_ready")
        s_oT_done = sem("s_oT_done")
        s_oT_ready = sem("s_oT_ready")
        s_o_done = sem("s_o_done")
        s_imp = sem("s_imp")
        s_imp_done = sem("s_imp_done")
        s_branch = sem("s_branch")
        w_out_in = sem("w_out_in")
        catT_done = sem("catT_done")
        catT_ready = sem("catT_ready")
        out_done = sem("out_done")
        out_added = sem("out_added")
        memw_in = sem("memw_in")
        mem_in = sem("mem_in")
        mkv_done = sem("mkv_done")
        mkv_ready = sem("mkv_ready")
        mkT_done = sem("mkT_done")
        mkT_ready = sem("mkT_ready")
        mq_in = sem("mq_in")
        qm_done = sem("qm_done")
        qm_ready = sem("qm_ready")
        m_sc_done = sem("m_sc_done")
        m_max = sem("m_max")
        m_exp = sem("m_exp")
        m_norm = sem("m_norm")
        m_pT_done = sem("m_pT_done")
        m_pT_ready = sem("m_pT_ready")
        m_oT_done = sem("m_oT_done")
        m_oT_ready = sem("m_oT_ready")
        memkv_in = sem("memkv_in")
        mo_in = sem("mo_in")
        m_qmask = sem("m_qmask")
        m_keyT_done = sem("m_keyT_done")
        m_keyT_ready = sem("m_keyT_ready")
        mo_done = sem("mo_done")
        mo_added = sem("mo_added")
        wq_in = sem("wq_in")
        sub_in = sem("sub_in")
        subT_done = sem("subT_done")
        subT_ready = sem("subT_ready")
        qp_done = sem("qp_done")
        qp_ready = sem("qp_ready")
        ps_done = sem("ps_done")
        ps_ready = sem("ps_ready")
        scores_moved = sem("scores_moved")
        best_shift = sem("best_shift")
        best_exp = sem("best_exp")
        routed = sem("routed")
        gates_ready = sem("gates_ready")
        rt_done = sem("rt_done")
        samples_routed = sem("samples_routed")
        hns_stored = sem("hns_stored")
        hns_in = sem("hns_in")
        cursor_ready = sem("cursor_ready")
        row_in = [sem(f"row_in{k}") for k in range(RING)]
        row_used = sem("row_used")
        act_kept = sem("act_kept")
        gelu_in = sem("gelu_in")
        gelu_tanh = sem("gelu_tanh")
        coefm_ready = sem("coefm_ready")
        se_done = sem("se_done")
        sk_zero = sem("sk_zero")
        x_done = sem("x_done")
        y_ready = sem("y_ready")
        y_stored = sem("y_stored")
        fin_gain_in = sem("fin_gain_in")
        own_m_in = sem("own_m_in")
        own_q_in = sem("own_q_in")
        s_cat_ready = sem("s_cat_ready")
        vector_order = sem("vector_order")
        pool_order = sem("pool_order")
        scalar_order = sem("scalar_order")

        class Order:

            def __init__(self, eng, s):
                self.eng, self.sem, self.n = eng, s, 0

            def __call__(self, ins):
                ins.then_inc(self.sem, 1)
                self.n += 1
                self.eng.wait_ge(self.sem, self.n)

        const_loads = [
            (gn_gain, c["gn_gain"]), (gn_rows[0:64, :], c["gn_rows"]), (cmp_bv, c["cmp_bv"]),
            (cmp_bk[0:64, :], c["cmp_bk"]), (ident, c["ident"]), (tri, c["tri"]), (decay, c["decay"]),
            (xi, c["xi"]), (zeta, c["zeta"]), (g_chunk, c["g_chunk"]), (gamma1[0:64, :], c["gamma1"]),
            (cmp_vis, c["cmp_vis"]), (cmp_neg, c["cmp_neg"]), (rot_ret, c["rot_ret"]), (rot_nsa, c["rot_nsa"]),
            (own_neg[0:64, :], c["own_neg"]), (group[0:64, :], c["group"]), (blk_excl[0:64, :], c["blk_excl"]),
            (blk_rank[0:64, :], c["blk_rank"]), (row_add, c["row_add"]), (iota16, c["iota16"]),
            (eye8, c["eye8"]), (page_i, a["page_rows"]),
        ]
        heads64 = sc_heads.rearrange("x b (h d) -> x (b h) d", d=HD)
        S_RQ, S_RK, S_RV, S_RG, S_NQ, S_SK, S_SV, S_WK, S_WV, S_Y, S_T, S_U = range(12)
        N_SROWS = 5 + 4 + 1

        step_turn = dict(STEP_TURNS)
        LAST_STEP = max(step_turn)
        STEP_AT = [max([s for s, turn in step_turn.items() if turn <= x], default=0)
                   for x in range(2 * ROWS // RING)]

        def advance(steps, last):
            while last > advanced.setdefault(steps, 0):
                advanced[steps] = next(steps)

        advanced = {}
        block = ctx.enter_context(nc.Block())

        @block.sync
        def _(sp):
            for t in range(NT):
                src = a["x_prompt"][0, t * P:(t + 1) * P, :] if t < PT else a["x_sample"][:, 0, :]
                sp.dma_start(h[0:rows_of(t), t, :], src).then_inc(x_in, 16)
            for i, name in enumerate(("norm_mix_g", "norm_mem_g", "norm_ffn_g")):
                sp.dma_start(gain[:, i, :], a[name].partition_broadcast(P)).then_inc(consts_in, 16)
            for dst, src in const_loads:
                sp.dma_start(dst[:], src).then_inc(consts_in, 16)
            w_in = a["w_in"].rearrange("(k p) n -> p k n", p=P)
            for i, (c0, n) in enumerate(CHUNKS):
                if i >= 2:
                    sp.wait_ge(proj_done, NT * (i - 1))
                sp.dma_start(w_buf[:, i % 2, :, 0:n], w_in[:, :, c0:c0 + n]).then_inc(w_in_loaded[i % 2], 16)
            for t in range(NT):
                sp.wait_ge(rotated, t + 1)
                R = rows_of(t)
                if t < PT:
                    for name, c0 in (("p_cmp_k", C_CK), ("p_cmp_v", C_CV), ("p_slc_k", C_SK), ("p_slc_v", C_SV)):
                        sp.dma_start(out[name][0, 0, t].rearrange("g k d -> k g d"),
                                     proj[t][:, c0:c0 + P].rearrange("p (g d) -> p g d", g=G)
                                     ).then_inc(rows_stored, 16)
                    for name, c0 in (("p_win_k", C_WK), ("p_win_v", C_WV)):
                        sp.dma_start(out[name][0, 0, :, t * P:(t + 1) * P].rearrange("g k d -> k g d"),
                                     proj[t][:, c0:c0 + P].rearrange("p (g d) -> p g d", g=G)
                                     ).then_inc(rows_stored, 16)
                else:
                    for name, c0 in (("s_cmp_k", C_CK), ("s_cmp_v", C_CV), ("s_slc_k", C_SK), ("s_slc_v", C_SV)):
                        sp.dma_start(out[name][0].rearrange("b g x d -> b (g x d)"),
                                     proj[t][0:R, c0:c0 + P]).then_inc(rows_stored, 16)
                    for name, c0 in (("s_win_k", C_WK), ("s_win_v", C_WV)):
                        sp.dma_start(out[name][0, :, :, 511, :], proj[t][0:R, c0:c0 + P].rearrange(
                            "p (g d) -> p g d", g=G)).then_inc(rows_stored, 16)
                    sp.dma_start(sc_heads.rearrange("x b n -> b x n"), proj[t][0:R, 0:5 * 512].rearrange(
                        "p (x n) -> p x n", x=5)).then_inc(rows_stored, 16)
                    sp.dma_start(sc_gates, proj[t][0:R, C_NG:C_NG + 3 * H]).then_inc(rows_stored, 16)
            ROWS_STORED = 16 * (PT * 6 + 8)
            for name, src in (("s_win_k", "cache_win_k"), ("s_win_v", "cache_win_v")):
                sp.dma_start(out[name][0, :, :, 0:511, :], a[src][0, :, :, 1:512, :]).then_inc(y_stored, 16)
            sp.wait_ge(proj_done, NT * len(CHUNKS))
            for i in range(2):
                sp.dma_start(cmp_w[:, i, :, :], a["cmp_w"][0, i].rearrange("j d e -> (j d) e").rearrange(
                    "(m q) e -> q m e", q=P)).then_inc(cmpw_in, 16)
            sp.wait_ge(rows_stored, ROWS_STORED)
            for i, name in enumerate(("p_cmp_k", "p_cmp_v")):
                n = 3 * i + 2
                if n >= 2:
                    sp.wait_ge(blkT_done, 8 * (n - 1))
                sp.dma_start(blk_buf[0:BG, n % 2, :], out[name][0, 0].rearrange(
                    "n g (k j) d -> (n g k) (j d)", k=2)).then_inc(own_blk_in, 16)
            sp.wait_ge(cmp_ready, 6)
            sp.dma_start(sc_cv, cv_out[0:BG, :]).then_inc(cv_stored, 16)
            sp.wait_ge(cv_stored, 16)
            sp.wait_ge(vblk_zero, 1)
            cvr = sc_cv.rearrange("(n g k) d -> g n k d", g=G, k=2)
            for hh in range(H):
                sp.dma_start(c_vblk[hh * 8:hh * 8 + 8, hh * HD:(hh + 1) * HD], cvr[hh // R4]).then_inc(vblk_in, 16)
            sp.wait_ge(state_ready, PT)
            sp.dma_start(out["p_state"][0, 0].rearrange("h d e -> d h e"), state[0:HD, :, :]).then_inc(state_stored, 16)
            sp.wait_ge(cat_ready, PT)
            sp.wait_ge(state_stored, 16)
            for t in range(2):
                sp.dma_start(mem_x[:, t, :], a["mem_prompt"][0, t * P:(t + 1) * P, :]).then_inc(mem_in, 16)
            sp.dma_start(memn_gain, a["mem_norm_g"].partition_broadcast(P)).then_inc(mem_in, 16)
            w_out = a["w_out"].rearrange("(k p) n -> p k n", p=P)
            sp.dma_start(front.w_out, w_out).then_inc(w_out_in, 16)
            for dst, name in ((w_mk, "w_mk"), (w_mv, "w_mv")):
                sp.dma_start(dst, a[name].rearrange("(k p) n -> p k n", p=P)).then_inc(memw_in, 16)
            sp.dma_start(sub_k.rearrange("p h (x d) -> p h x d", x=2),
                         a["peer_subkeys"][0].rearrange("h x k d -> k h x d")).then_inc(sub_in, 16)
            sp.dma_start(gain[:, MIX, :], a["norm_final_g"].partition_broadcast(P)).then_inc(fin_gain_in, 16)

            def memory_weights():
                sp.dma_start(w_mq, a["w_mq"].rearrange("(k p) n -> p k n", p=P)).then_inc(mq_in, 16)
                sp.dma_start(w_mo, a["w_mo"].rearrange("(k p) n -> p k n", p=P)).then_inc(mo_in, 16)

            wq = a["peer_wq"].rearrange("(k p) n -> p k n", p=P)
            sp.wait_ge(out_done, 2 * len(front.tiles))
            sp.dma_start(front.wq, wq).then_inc(wq_in, 16)
            sp.wait_ge(mkv_done, 4)
            memory_weights()
            for n in range(4):
                sp.wait_ge(mkv_ready, n + 1)
                buf, name, t = (mk, "p_mem_k", n) if n < 2 else (mv, "p_mem_v", n - 2)
                sp.dma_start(out[name][0, 0, t * P:(t + 1) * P].rearrange("m h d -> m (h d)"),
                             buf[:, t, :]).then_inc(y_stored, 16)
            sp.wait_ge(qp_done, H)
            for i in range(5):
                sp.dma_start(s_rows[0:64, i, :], heads64[i]).then_inc(s_rows_in, 16)
            for i, name in ((S_SK, "s_slc_k"), (S_SV, "s_slc_v")):
                src = out[name][0].rearrange("b g x d -> (b g) x d")
                sp.dma_start(s_rows[0:64, i, :], src.broadcast_to((BG, R4, HD))).then_inc(s_rows_in, 16)
            for i, name in ((S_WK, "s_win_k"), (S_WV, "s_win_v")):
                src = out[name][0].rearrange("b g k d -> (b g) k d")[:, 511:512, :]
                sp.dma_start(s_rows[0:64, i, :], src.broadcast_to((BG, R4, HD))).then_inc(s_rows_in, 16)
            sp.dma_start(col[0:64, 0:3], sc_gates.rearrange("b (h x) -> (b h) x", x=3)).then_inc(s_rows_in, 16)
            sp.wait_ge(ps_done, 4 * len(front.tiles))
            sp.dma_start(own_q[0:64, :, :], c["own_q"]).then_inc(own_q_in, 16)
            sp.wait_ge(s_oT_done, 1)
            for dst, name, s in ((win_keys, "cache_win_k", key_in[1]), (win_vals, "cache_win_v", val_in[1])):
                sp.dma_start(dst, a[name][0].rearrange("b g (p j) d -> p (b g) (j d)", p=P)).then_inc(s, 16)
            sp.wait_ge(s_oT_done, 2)
            sp.dma_start(s_state[0:64, :, :], a["state_ret"][0].rearrange("b h d e -> (b h) d e")).then_inc(s_state_in, 16)
            sp.wait_ge(s_branch, 4)
            sp.dma_start(out["s_state"][0].rearrange("b h d e -> (b h) d e"), s_state[0:64, :, :]).then_inc(s_stored, 16)
            sp.wait_ge(s_cat_ready, 1)
            sp.dma_start(sc_cat[0].rearrange("b (h d) -> (b h) d", d=HD), s_rows[0:64, S_Y, :]).then_inc(cat_stored, 16)
            sp.dma_start(sc_cat[1].rearrange("b (h d) -> (b h) d", d=HD), s_o[0:64, 3, :]).then_inc(cat_stored, 16)
            sp.wait_ge(cat_stored, 32)
            sp.dma_start(cat[0:DB, SAMPLE, :].rearrange("p (x n) -> p x n", x=2),
                         sc_cat.rearrange("x b n -> b x n")).then_inc(s_cat_in, 16)
            sp.wait_ge(s_stored, 16)
            sp.dma_start(back.w_out, w_out).then_inc(w_out_in, 16)
            sp.dma_start(own_m, c["own_m"]).then_inc(own_m_in, 16)
            sp.wait_ge(out_done, 2 * NT)
            memory_weights()
            for piece, (s, v) in enumerate(((qm_done, 2 * HM), (m_keyT_done, DB), (m_keyT_done, 2 * DB),
                                            (m_oT_done, PT * HM + 1))):
                name, b0 = ("cache_mem_k", "cache_mem_v")[piece // 2], 4 * (piece % 2)
                sp.wait_ge(s, v)
                sp.dma_start(mem_piece, a[name][0].rearrange("b (p m) h d -> p b (m h d)", m=2)[:, b0:b0 + 4, :]
                             ).then_inc(memkv_in, 16)
            sp.wait_ge(mo_done, 2 * NT)
            sp.dma_start(back.wq, wq).then_inc(wq_in, 16)
            sp.wait_ge(hn_ready, 3 * NT + 2)
            sp.dma_start(sc_hn, hn3[0:DB, SAMPLE, :]).then_inc(hns_stored, 16)
            sp.wait_ge(hns_stored, 16)
            sp.wait_ge(qp_done, 2 * H)
            sp.dma_start(hn_s.rearrange("p b d -> p (b d)"), sc_hn.rearrange("b d -> (b d)").partition_broadcast(P)).then_inc(hns_in, 16)
            for t in range(NT):
                R = rows_of(t)
                sp.wait_ge(y_ready, t + 1)
                dst = out["y_prompt"][0, t * P:(t + 1) * P, :] if t < PT else out["y_sample"][:, 0, :]
                sp.dma_start(dst, hn3[0:R, t, :]).then_inc(y_stored, 16)
            sp.wait_ge(rows_stored, ROWS_STORED)
            sp.wait_ge(state_stored, 16)
            sp.wait_ge(s_stored, 16)
            sp.wait_ge(cat_stored, 32)
            sp.wait_ge(hns_stored, 16)
            sp.wait_ge(y_stored, 16 * (2 + 4 + NT))

        @block.gpsimd
        def _(pool):
            pool.wait_ge(idx_ready, 2)
            pool.wait_ge(proj_done, NT * len(CHUNKS))
            for i, name in enumerate(("cache_cmp_k", "cache_cmp_v")):
                src = a[name][0].rearrange("n g (k j) d -> (n g k) (j d)", k=2)
                for x in range(2):
                    n = 3 * i + x
                    if n >= 2:
                        pool.wait_ge(blkT_done, 8 * (n - 1))
                    pool.indirect_dma_start(
                        out=blk_buf[:, n % 2, :], out_offset=None, in_=src,
                        in_offset=bass.IndirectOffsetOnAxis(ap=blk_idx[:, x:x + 1], axis=0)
                    ).then_inc(blk_in[n % 2], 16)

            def gather_pages(dst, name, s):
                src = a[name][0].rearrange("n g (q j) d -> (n g q) (j d)", q=16)
                for bg in range(BG):
                    pool.indirect_dma_start(
                        out=dst[:, bg, :], out_offset=None, in_=src,
                        in_offset=bass.IndirectOffsetOnAxis(ap=row_idx[:, bg:bg + 1], axis=0)).then_inc(s, 16)

            pool.wait_ge(mo_done, 2 * len(front.tiles))
            gather_pages(key_rows, "cache_slc_k", key_in[0])

            def gather(name, idx, k):
                pool.indirect_dma_start(
                    out=ring[:, k, :], out_offset=None, in_=a[name][0],
                    in_offset=bass.IndirectOffsetOnAxis(ap=idx, axis=0)).then_inc(row_in[k], 16)

            def gather_row(name, t, slot, used, k, heads_known):
                pool.wait_ge(row_used, used)
                pool.tensor_copy(cursor[:, k:k + 1], expert[:, t, bass.ds(slot, 1)]).then_inc(cursor_ready, 1)
                pool.wait_ge(routed, heads_known)
                pool.wait_ge(cursor_ready, used)
                gather(name, cursor[:, k:k + 1], k)

            pool.wait_ge(routed, 1)
            for k in range(RING):
                gather("peer_u", expert[:, 0, k:k + 1], k)
            for r in range(RING, TOPK):
                gather_row("peer_u", 0, r, r - RING + 1, r % RING, 1)
            with pool.Fori(1, H) as i:
                pool.wait_ge(routed, i + 1)
                for r in range(TOPK):
                    gather_row("peer_u", 0, i * TOPK + r, i * TOPK + (r - RING + 1), r % RING, 1)
            pool.wait_ge(s_sc_done, 2)
            gather_pages(val_rows, "cache_slc_v", val_in[0])
            for t in range(PT):
                for table, name in enumerate(("peer_u", "peer_v")):
                    if t == 0 and table == 0:
                        continue
                    n0 = ROWS * t + SLOTS * table
                    pool.wait_ge(routed, H * (t + 1))
                    with pool.Fori(0, TURNS) as i:
                        for k in range(RING):
                            gather_row(name, t, i * RING + k, i * RING + (n0 + k - RING + 1), k, H * (t + 1))
            pool.wait_ge(samples_routed, 1)
            for x, name in enumerate(("peer_u", "peer_v")):
                for b in range(DB):
                    pool.wait_ge(row_used, ROWS * PT + DB * x + b - RING + 1)
                    gather(name, expert_s[:, b:b + 1], b)

        @block.tensor
        def _(pe):
            freed = {}
            norms = [0]

            def claim(b):
                if b in freed:
                    pe.wait_ge(*freed.pop(b))
                return banks[b]

            def transpose_rows(src, R):
                n = norms[0]
                norms[0] += 1
                pe.wait_ge(hn_ready, n + 1)
                for half in range(2):
                    bank = claim(half)
                    for q in range(4):
                        k = 4 * half + q
                        ins = pe.transpose(bank[:, q * P:q * P + R], src[0:R, k * P:(k + 1) * P], ident[0:R, 0:R])
                    ins.then_inc(hnT_done, 1)
                    freed[half] = (hnT_ready, 2 * n + half + 1)

            pe.wait_ge(consts_in, 16 * (3 + len(const_loads)))
            for t in range(NT):
                transpose_rows(hn_buf[:, t % 2, :], rows_of(t))
            n = 0
            for i, (c0, w) in enumerate(CHUNKS):
                pe.wait_ge(w_in_loaded[i % 2], 16 * (i // 2 + 1))
                for t in range(NT):
                    if i == 0:
                        pe.wait_ge(hnT_ready, 2 * (t + 1))
                    R = rows_of(t)
                    b = 2 + n % 4
                    bank = claim(b)
                    for k in range(KC):
                        ins = pe.matmul(bank[0:R, 0:w], hnT[:, k, t * P:t * P + R], w_buf[:, i % 2, k, 0:w],
                                        start=(k == 0), stop=(k == KC - 1))
                    ins.then_inc(proj_done, 1)
                    n += 1
                    freed[b] = (proj_ready, n)

            def cmp_products(unit, m):
                kind, x = divmod(unit, 3)
                R = P if x < 2 else BG
                pe.wait_ge(blkT_ready, 8 * unit + m + 1)
                acc_bank = banks[4 + unit % 2]
                for q in range(4):
                    j = 4 * m + q
                    rows, w = blkT[:, m % 2, q, 0:R], cmp_w[:, kind, j, :]
                    if kind == 0:
                        ins = pe.matmul(acc_bank[0:HD, 0:R], w, rows, start=(j == 0), stop=(j == 31))
                    else:
                        ins = pe.matmul(acc_bank[0:R, 0:HD], rows, w, start=(j == 0), stop=(j == 31))
                if m == 7:
                    ins.then_inc(cmp_done, 1)
                    freed[4 + unit % 2] = (cmp_ready, unit + 1)

            for unit in range(6):
                R = P if unit % 3 < 2 else BG
                if unit % 3 == 2:
                    pe.wait_ge(own_blk_in, 16 * (unit // 3 + 1))
                else:
                    pe.wait_ge(blk_in[unit % 2], 16 * (1 + (unit >= 3)))
                if unit == 0:
                    pe.wait_ge(cmpw_in, 32)
                claim(4 + unit % 2)
                for m in range(8):
                    bank = claim(m % 2)
                    for q in range(4):
                        j = 4 * m + q
                        ins = pe.transpose(bank[:, q * P:q * P + R], blk_buf[0:R, unit % 2, j * P:(j + 1) * P],
                                           ident[0:R, 0:R])
                    ins.then_inc(blkT_done, 1)
                    freed[m % 2] = (blkT_ready, 8 * unit + m + 1)
                    if m:
                        cmp_products(unit, m - 1)
                cmp_products(unit, 7)

            def att_scores(t, u):
                kind, hh = divmod(u % 16, H)
                b, N = u % 2, P * (t + 1)
                bank = claim(b)
                pe.matmul(bank[:, 0:N], nqT[0:HD, hh, :], kT[0:HD, kind, hh // R4, 0:N], start=True, stop=False)
                pe.matmul(bank[:, N - P:N], ident, tri, start=False, stop=True).then_inc(sc_done, 1)
                freed[b] = (exp_ready, u + 1)

            def att_probsT(t, u):
                b = 3 + u % 2
                bank = claim(b)
                pe.wait_ge(exp_ready, u + 1)
                for j in range(t + 1):
                    ins = pe.transpose(bank[:, j * P:(j + 1) * P], probs[:, u % 2, j * P:(j + 1) * P], ident)
                ins.then_inc(pT_done, 1)
                freed[b] = (pT_ready, u + 1)

            def att_values(t, u):
                kind, hh = divmod(u % 16, H)
                b = 5 + kind
                if hh == 0:
                    claim(b)
                c0 = (C_SV, C_WV)[kind] + hh // R4 * HD
                pe.wait_ge(pT_ready, u + 1)
                for j in range(t + 1):
                    ins = pe.matmul(banks[b][:, hh * HD:(hh + 1) * HD], probsT[:, u % 2, j * P:(j + 1) * P],
                                    proj[j][:, c0:c0 + HD], start=(j == 0), stop=(j == t))
                if hh == H - 1:
                    ins.then_inc(ao_done, 1)
                    freed[b] = (ao_used, 2 * t + kind + 1)

            for t in range(PT):
                pe.wait_ge(rotated, t + 1)
                heads = [C_RQ + HD * x for x in range(H)] + [C_RK + HD * x for x in range(H)] + \
                        [C_NQ + HD * x for x in range(H)] + [C_SK, C_SK + HD, C_WK, C_WK + HD]
                for m in range(7):
                    bank = claim(m % 2)
                    for q in range(4):
                        c0 = heads[4 * m + q]
                        ins = pe.transpose(bank[0:HD, q * P:(q + 1) * P], proj[t][:, c0:c0 + HD], ident)
                    ins.then_inc(headT_done, 1)
                    freed[m % 2] = (headT_ready, 7 * t + m + 1)
                pe.wait_ge(headT_ready, 7 * t + 4)
                for m in range(2):
                    bank = claim(2 + m)
                    for q in range(4):
                        ins = pe.matmul(bank[:, q * P:(q + 1) * P], rkT[0:HD, 4 * m + q, :], rqT[0:HD, 4 * m + q, :],
                                        start=True, stop=True)
                    ins.then_inc(att_done, 1)
                    freed[2 + m] = (att_ready, 2 * t + m + 1)
                if t == 0:
                    pe.wait_ge(cmp_ready, 6)
                pe.wait_ge(headT_ready, 7 * t + 6)
                bank = claim(7)
                for hh in range(H):
                    keys = c_kT[0:HD, 256:272].rearrange("p (n g k) -> p n g k", g=G, k=2)[:, :, hh // R4, :]
                    ins = pe.matmul(bank[:, hh * 8:(hh + 1) * 8], nqT[0:HD, hh, :], keys, start=True, stop=True)
                ins.then_inc(cs_done, 1)
                freed[7] = (cs_ready, t + 1)
                for b in (4, 5, 6):
                    claim(b)
                if t:
                    pe.wait_ge(state_ready, t)
                    for hh in range(H):
                        pe.matmul(banks[4][:, hh * HD:(hh + 1) * HD], rqT[0:HD, hh, :], state[0:HD, hh, :],
                                  start=True, stop=True)
                pe.wait_ge(vz_ready, t + 1)
                for hh in range(H):
                    pe.matmul(banks[6][0:HD, hh * HD:(hh + 1) * HD], proj[t][:, C_RK + hh * HD:C_RK + (hh + 1) * HD],
                              vz[:, hh, :], start=True, stop=True)
                pe.wait_ge(att_ready, 2 * t + 2)
                for hh in range(H):
                    ins = pe.matmul(banks[5][:, hh * HD:(hh + 1) * HD], att[:, hh, :],
                                    proj[t][:, C_RV + hh * HD:C_RV + (hh + 1) * HD], start=True, stop=True)
                ins.then_inc(ret_done, 1)
                for b in (4, 5, 6):
                    freed[b] = (state_ready, t + 1)
                bank = claim(7)
                pe.wait_ge(cp_ready, t + 1)
                pe.transpose(bank[0:64, 0:P], cp_buf, ident).then_inc(cpT_done, 1)
                freed[7] = (cpT_ready, t + 1)
                bank = claim(2)
                if t == 0:
                    pe.wait_ge(vblk_in, 16 * H)
                pe.wait_ge(cpT_ready, t + 1)
                pe.matmul(bank[:, 0:512], cpT[0:64, :], c_vblk[0:64, :], start=True, stop=True).then_inc(co_done, 1)
                freed[2] = (co_used, t + 1)
                pe.wait_ge(headT_ready, 7 * t + 7)
                u0 = 2 * H * t
                att_scores(t, u0)
                for u in range(u0, u0 + 2 * H):
                    if u + 1 < u0 + 2 * H:
                        att_scores(t, u + 1)
                    att_probsT(t, u)
                    att_values(t, u)

            def output_projection(grp, nth):
                for t in grp.tiles:
                    R = rows_of(t)
                    if t == SAMPLE:
                        pe.wait_ge(s_cat_in, 16)
                    for half in range(2):
                        bank = claim(half)
                        for q in range(4):
                            k = 4 * half + q
                            ins = pe.transpose(bank[:, q * P:q * P + R], cat[0:R, t, k * P:(k + 1) * P], ident[0:R, 0:R])
                        ins.then_inc(catT_done, 1)
                        freed[half] = (catT_ready, 2 * t + half + 1)
                    pe.wait_ge(w_out_in, 16 * nth)
                    pe.wait_ge(catT_ready, 2 * t + 2)
                    for half in range(2):
                        n = 2 * t + half
                        b = 2 + n % 4
                        bank = claim(b)
                        for k in range(KC):
                            ins = pe.matmul(bank[0:R, :], grp.catT[t][:, k, 0:R],
                                            grp.w_out[:, k, half * 512:(half + 1) * 512],
                                            start=(k == 0), stop=(k == KC - 1))
                        ins.then_inc(out_done, 1)
                        freed[b] = (out_added, n + 1)

            def memory_queries(grp, nth):
                for t in grp.tiles:
                    transpose_rows(hn3[:, t, :], rows_of(t))
                pe.wait_ge(mq_in, 16 * nth)
                pe.wait_ge(hnT_ready, 2 * norms[0])
                for hh in range(HM):
                    n = HM * (nth - 1) + hh
                    b = 2 + n % 4
                    bank = claim(b)
                    for k in range(KC):
                        ins = pe.matmul(bank[:, 0:grp.width], w_mq[:, k, hh * P:(hh + 1) * P], grp.hnT[:, k, :],
                                        start=(k == 0), stop=(k == KC - 1))
                    ins.then_inc(qm_done, 1)
                    freed[b] = (qm_ready, n + 1)
                pe.wait_ge(qm_ready, HM * nth)

            def memory_attention(grp):
                units = [(t, hh) for t in grp.tiles if t < PT for hh in range(HM)]
                v0 = HM * units[0][0]

                def mem_scores(v):
                    t, hh = divmod(v, HM)
                    at = grp.at[t]
                    bank = claim(v % 2)
                    pe.matmul(bank[:, 0:NMEM], grp.qT_m[:, hh, at:at + P], mkT[:, hh, :],
                              start=True, stop=True).then_inc(m_sc_done, 1)
                    freed[v % 2] = (m_exp, v + 1)

                mem_scores(v0)
                for v in range(v0, v0 + len(units)):
                    hh = v % HM
                    if v + 1 < v0 + len(units):
                        mem_scores(v + 1)
                    b = 6 + v % 2
                    bank = claim(b)
                    pe.wait_ge(m_norm, v + 1)
                    for x in range(2):
                        ins = pe.transpose(bank[:, x * P:(x + 1) * P], grp.m_probs[:, v % 2, x * P:(x + 1) * P], ident)
                    ins.then_inc(m_pT_done, 1)
                    freed[b] = (m_pT_ready, v + 1)
                    b = 4 + v % 2
                    bank = claim(b)
                    pe.wait_ge(m_pT_ready, v + 1)
                    for x in range(2):
                        ins = pe.matmul(bank[:, 0:P], mv[:, x, hh * P:(hh + 1) * P],
                                        grp.m_probsT[:, v % 2, x * P:(x + 1) * P], start=(x == 0), stop=(x == 1))
                    ins.then_inc(m_oT_done, 1)
                    freed[b] = (m_oT_ready, v + 1)

            def memory_output(grp, nth):
                pe.wait_ge(mo_in, 16 * nth)
                for t in grp.tiles:
                    R, at = rows_of(t), grp.at[t]
                    for half in range(2):
                        n = 2 * t + half
                        b = 2 + n % 2
                        bank = claim(b)
                        for hh in range(HM):
                            ins = pe.matmul(bank[0:R, :], grp.oT_m[:, hh, at:at + R],
                                            w_mo[:, hh, half * 512:(half + 1) * 512],
                                            start=(hh == 0), stop=(hh == HM - 1))
                        ins.then_inc(mo_done, 1)
                        freed[b] = (mo_added, n + 1)

            def expert_queries(grp, nth):
                for t in grp.tiles:
                    transpose_rows(hn3[:, t, :], rows_of(t))
                pe.wait_ge(wq_in, 16 * nth)
                pe.wait_ge(hnT_ready, 2 * norms[0])
                for hh in range(H):
                    n = H * (nth - 1) + hh
                    b = 2 + n % 4
                    bank = claim(b)
                    for k in range(KC):
                        ins = pe.matmul(bank[:, 0:grp.width], grp.wq[:, k, hh * P:(hh + 1) * P], grp.hnT[:, k, :],
                                        start=(k == 0), stop=(k == KC - 1))
                    ins.then_inc(qp_done, 1)
                    freed[b] = (qp_ready, n + 1)
                pe.wait_ge(qp_ready, H * nth)

            def key_scores_of(grp):
                for t in grp.tiles:
                    R, at = rows_of(t), grp.at[t]
                    for m in range(4):
                        b = 4 + m
                        bank = claim(b)
                        for x in range(2):
                            hh = 2 * m + x
                            ins = pe.matmul(bank[0:R, x * 256:(x + 1) * 256], grp.qT_p[:, hh, at:at + R], skT[:, hh, :],
                                            start=True, stop=True)
                        ins.then_inc(ps_done, 1)
                        freed[b] = (ps_ready, 4 * t + m + 1)

            pe.wait_ge(cat_ready, PT)
            output_projection(front, 1)
            for t in range(2):
                transpose_rows(hn3[:, t, :], P)
            pe.wait_ge(hnT_ready, 2 * (NT + 2))
            pe.wait_ge(memw_in, 32)
            for n in range(4):
                w, t = divmod(n, 2)
                b = (6, 7, 2, 3)[n]
                bank = claim(b)
                for k in range(KC):
                    ins = pe.matmul(bank[:, :], mT[:, k, t * P:(t + 1) * P], (w_mk, w_mv)[w][:, k, :],
                                    start=(k == 0), stop=(k == KC - 1))
                ins.then_inc(mkv_done, 1)
                freed[b] = (mkv_ready, n + 1)
            pe.wait_ge(mkv_ready, 2)
            for t in range(2):
                bank = claim(t)
                for hh in range(HM):
                    ins = pe.transpose(bank[:, hh * P:(hh + 1) * P], mk[:, t, hh * P:(hh + 1) * P], ident)
                ins.then_inc(mkT_done, 1)
                freed[t] = (mkT_ready, t + 1)
            pe.wait_ge(sub_in, 16)
            for half in range(2):
                bank = claim(4 + half)
                for q in range(4):
                    ins = pe.transpose(bank[:, q * P:(q + 1) * P], sub_k[:, 4 * half + q, :], ident)
                ins.then_inc(subT_done, 1)
                freed[4 + half] = (subT_ready, half + 1)
            memory_queries(front, 1)
            pe.wait_ge(mkT_ready, 2)
            memory_attention(front)
            pe.wait_ge(m_oT_ready, HM * len(front.tiles))
            memory_output(front, 1)
            expert_queries(front, 1)
            pe.wait_ge(subT_ready, 2)
            key_scores_of(front)

            pe.wait_ge(s_rows_in, 16 * N_SROWS)
            bank = claim(0)
            pe.transpose(bank[0:64, 0:64], s_rows[0:64, S_NQ, :], ident[0:64, 0:64]).then_inc(sT_done, 1)
            freed[0] = (sT_ready, 1)
            pe.wait_ge(sT_ready, 1)
            bank = claim(1)
            pe.matmul(bank[0:64, 0:256], sqT[0:64, :], c_kT[0:HD, 0:256], start=True, stop=True).then_inc(s_sc_done, 1)
            freed[1] = (s_max, 1)
            pe.wait_ge(s_imp, 1)
            bank = claim(2)
            for x in range(2):
                ins = pe.transpose(bank[:, x * 64:(x + 1) * 64], cmp_p[0:64, x * P:(x + 1) * P], ident[0:64, 0:64])
            ins.then_inc(s_pT_done, 1)
            freed[2] = (s_pT_ready, 1)
            pe.wait_ge(s_pT_ready, 1)
            bank = claim(3)
            pe.matmul(bank[0:64, 64:80], group[0:64, :], s_small[0:64, 32:48], start=True, stop=True)
            for x in range(2):
                ins = pe.matmul(bank[0:64, 0:64], cmp_pT[:, x, :], c_v[:, x, :], start=(x == 0), stop=(x == 1))
            ins.then_inc(s_o_done, 1)
            freed[3] = (s_branch, 1)
            pe.wait_ge(qmask_ready, 1)
            gi = 0
            for kind, nj in enumerate((8, 4)):
                nc_ = nj // 4
                keys, vals = ((key_rows, val_rows), (win_keys, win_vals))[kind]
                pe.wait_ge(key_in[kind], (16 * BG, 16)[kind])
                for cc in range(nc_):
                    claim(4 + cc)

                def key_scores(i, gi):
                    bg, cc = divmod(i, nc_)
                    pe.wait_ge(s_keyT_ready, gi + 1)
                    ins = pe.matmul(banks[4 + cc][0:64, :], q_mask[0:HD, bg, :], keyT[0:HD, gi % 2, :],
                                    start=(bg == 0), stop=(bg == BG - 1))
                    return ins

                for i in range(BG * nc_):
                    bg, cc = divmod(i, nc_)
                    bank = claim(gi % 2)
                    for q in range(4):
                        j = 4 * cc + q
                        ins = pe.transpose(bank[0:HD, q * P:(q + 1) * P], keys[:, bg, j * HD:(j + 1) * HD], ident)
                    ins.then_inc(s_keyT_done, 1)
                    freed[gi % 2] = (s_keyT_ready, gi + 1)
                    if i:
                        key_scores(i - 1, gi - 1)
                    gi += 1
                key_scores(BG * nc_ - 1, gi - 1).then_inc(s_sc_done, 1)
                for cc in range(nc_):
                    freed[4 + cc] = (s_max, 2 + kind)
                bank = claim(6)
                pe.wait_ge(s_exp, 2 + kind)
                for j in range(nj):
                    ins = pe.transpose(bank[:, j * 64:(j + 1) * 64], s_probs[0:64, j * P:(j + 1) * P],
                                       ident[0:64, 0:64])
                ins.then_inc(s_pT_done, 1)
                freed[6] = (s_pT_ready, 2 + kind)
                pe.wait_ge(val_in[kind], (16 * BG, 16)[kind])
                pe.wait_ge(s_pT_ready, 2 + kind)
                bank = claim(7)
                for bg in range(BG):
                    for j in range(nj):
                        ins = pe.matmul(bank[0:HD, bg * R4:(bg + 1) * R4], vals[:, bg, j * HD:(j + 1) * HD],
                                        s_probsT[:, j, bg * R4:(bg + 1) * R4], start=(j == 0), stop=(j == nj - 1))
                ins.then_inc(s_oT_done, 1)
                freed[7] = (s_oT_ready, 1 + kind)
                pe.wait_ge(s_oT_ready, 1 + kind)
                bank = claim(3)
                pe.transpose(bank[0:64, 0:64], s_o[0:HD, 0, :], ident[0:64, 0:64]).then_inc(s_o_done, 1)
                freed[3] = (s_branch, 2 + kind)

            output_projection(back, 2)
            memory_queries(back, 2)
            memory_attention(back)
            V = PT * HM
            pe.wait_ge(m_qmask, 1)
            claim(2)

            def mem_key_scores(g):
                b, pair = divmod(g, 2)
                pe.wait_ge(m_keyT_ready, g + 1)
                for x in range(2):
                    cc = (2 * pair + x) * DB + b
                    ins = pe.matmul(banks[2][0:32, 0:NMEM], qm_mask[:, cc, :], mkT_s[:, g % 2, x * NMEM:(x + 1) * NMEM],
                                    start=(g == 0 and x == 0), stop=(g == 2 * DB - 1 and x == 1))
                return ins

            for g in range(2 * DB):
                b, pair = divmod(g, 2)
                if g % DB == 0:
                    pe.wait_ge(memkv_in, 16 * (g // DB + 1))
                bank = claim(g % 2)
                for x in range(2):
                    for m in range(2):
                        c0 = m * 512 + (2 * pair + x) * P
                        ins = pe.transpose(bank[:, x * NMEM + m * P:x * NMEM + (m + 1) * P],
                                           mem_piece[:, b % 4, c0:c0 + P], ident)
                ins.then_inc(m_keyT_done, 1)
                freed[g % 2] = (m_keyT_ready, g + 1)
                if g:
                    mem_key_scores(g - 1)
            mem_key_scores(2 * DB - 1).then_inc(m_sc_done, 1)
            freed[2] = (m_exp, V + 1)
            bank = claim(3)
            pe.wait_ge(m_norm, V + 1)
            for m in range(2):
                ins = pe.transpose(bank[:, m * 32:(m + 1) * 32], ms_probs[0:32, m * P:(m + 1) * P], ident[0:32, 0:32])
            ins.then_inc(m_pT_done, 1)
            freed[3] = (m_pT_ready, V + 1)
            bank = claim(4)
            pe.wait_ge(m_pT_ready, V + 1)
            for b in range(DB):
                if b % 4 == 0:
                    pe.wait_ge(memkv_in, 16 * (3 + b // 4))
                for hh in range(HM):
                    cc = hh * DB + b
                    for m in range(2):
                        c0 = m * 512 + hh * P
                        ins = pe.matmul(bank[:, cc:cc + 1], mem_piece[:, b % 4, c0:c0 + P], ms_probsT[:, m, cc:cc + 1],
                                        start=(m == 0), stop=(m == 1))
                if b % 4 == 3:
                    ins.then_inc(m_oT_done, 1)
            freed[4] = (m_oT_ready, V + 1)
            pe.wait_ge(m_oT_ready, V + 1)
            memory_output(back, 2)
            expert_queries(back, 2)
            key_scores_of(back)

            bank = claim(0)
            pe.wait_ge(gates_ready, 1)
            pe.transpose(bank[:, 0:DB], expert_f[0:DB, :], ident[0:DB, 0:DB])
            pe.transpose(bank[:, DB:2 * DB], gate_t[0:DB, :], ident[0:DB, 0:DB]).then_inc(rt_done, 1)

            for half in range(2):
                claim(6 + half)
            pe.wait_ge(coefm_ready, 1)
            for b in range(DB):
                pe.wait_ge(row_in[b], 16 * (ROWS * PT // RING + 2))
                for half in range(2):
                    ins = pe.matmul(banks[6 + half][0:DB, :], coef_m[:, b, :], ring[:, b, half * 512:(half + 1) * 512],
                                    start=(b == 0), stop=(b == DB - 1))
            ins.then_inc(se_done, 1)

        @block.scalar
        def _(act):
            norms = [0]
            order = Order(act, scalar_order)

            def mean_square(x, junk, s=None, v=None):
                n = norms[0]
                norms[0] += 1
                R = x.shape[0]
                if s is not None:
                    act.wait_ge(s, v)
                act.activation(junk[0:R, :], x, ACT.Square, scale=1.0 / 32,
                               accum_out=mean_sq[0:R, n % 16:n % 16 + 1]).then_inc(mean_ready, 1)
                act.wait_ge(mean_ready, n + 1)
                act.activation(rstd[0:R, n % 16:n % 16 + 1], mean_sq[0:R, n % 16:n % 16 + 1], ACT.Sqrt,
                               bias=eps_col[0:R, :]).then_inc(std_ready, 1)

            copied = [0]

            def copy_rowsT(dst, c0, R):
                n = copied[0]
                copied[0] += 1
                for half in range(2):
                    act.wait_ge(hnT_done, 2 * n + half + 1)
                    act.activation(dst[:, 4 * half:4 * half + 4, c0:c0 + R],
                                   banks[half][:, :].rearrange("p (k r) -> p k r", k=4)[:, :, 0:R],
                                   ACT.Copy).then_inc(hnT_ready, 1)

            act.wait_ge(x_in, 16 * NT)
            act.wait_ge(eps_set, 1)
            for t in range(NT):
                mean_square(h[0:rows_of(t), t, :], sq_junk)
            for t in range(NT):
                copy_rowsT(hnT, t * P, rows_of(t))
            n = 0
            for c0, w in CHUNKS:
                for t in range(NT):
                    R = rows_of(t)
                    act.wait_ge(proj_done, n + 1)
                    act.activation(proj[t][0:R, c0:c0 + w], banks[2 + n % 4][0:R, 0:w], ACT.Copy).then_inc(proj_ready, 1)
                    n += 1
            for unit in range(6):
                R = P if unit % 3 < 2 else BG
                for m in range(8):
                    act.wait_ge(blkT_done, 8 * unit + m + 1)
                    act.activation(blkT[:, m % 2, :, 0:R], banks[m % 2][:, :].rearrange("p (k r) -> p k r", k=4)[:, :, 0:R],
                                   ACT.Copy).then_inc(blkT_ready, 1)
            for t in range(PT):
                for m in range(7):
                    act.wait_ge(headT_done, 7 * t + m + 1)
                    src = banks[m % 2][0:HD, :].rearrange("p (k r) -> p k r", k=4)
                    if m < 6:
                        dst = (rqT, rkT, nqT)[m // 2][0:HD, 4 * (m % 2):4 * (m % 2) + 4, :]
                    else:
                        dst = kT[0:HD, :, :, t * P:(t + 1) * P].rearrange("p x g r -> p (x g) r")
                    act.activation(dst, src, ACT.Copy, scale=0.125 if m in (4, 5) else 1.0).then_inc(headT_ready, 1)
                if t:
                    act.wait_ge(cat_ready, t)
                act.activation(tanh_rg, proj[t][:, C_RG:C_RG + 512], ACT.Tanh, scale=0.5).then_inc(tanh_ready, 1)
                act.activation(gate, proj[t][:, C_NG:C_NG + 3 * H], ACT.Tanh, scale=0.5).then_inc(tanh_ready, 1)
                act.wait_ge(cs_ready, t + 1)
                act.activation(cp_buf, cs_buf, ACT.Exp).then_inc(cs_exp, 1)
                act.wait_ge(cpT_done, t + 1)
                act.activation(cpT[0:64, :], banks[7][0:64, 0:P], ACT.Copy).then_inc(cpT_ready, 1)
                act.wait_ge(gn_var, t + 1)
                act.activation(gn_r[:, 0:H], gn_v[:, 0:H], ACT.Sqrt, bias=eps_col).then_inc(gn_std, 1)
                for u in range(2 * H * t, 2 * H * (t + 1)):
                    kind, hh = divmod(u % 16, H)
                    N = P * (t + 1)
                    act.wait_ge(max_ready, u + 1)
                    if u >= 2:
                        act.wait_ge(pT_done, u - 1)
                    act.activation(probs[:, u % 2, 0:N], banks[u % 2][:, 0:N], ACT.Exp,
                                   bias=neg_max[:, u % 16:u % 16 + 1],
                                   accum_out=exp_sum[:, kind, hh:hh + 1]).then_inc(exp_ready, 1)
            def rows_transposed(grp):
                for t in grp.tiles:
                    R = rows_of(t)
                    for half in range(2):
                        act.wait_ge(catT_done, 2 * t + half + 1)
                        act.activation(grp.catT[t][:, 4 * half:4 * half + 4, 0:R],
                                       banks[half][:, :].rearrange("p (k r) -> p k r", k=4)[:, :, 0:R],
                                       ACT.Copy).then_inc(catT_ready, 1)

            def tile_norms(grp, s):
                for t in grp.tiles:
                    mean_square(h[0:rows_of(t), t, :], hn3[:, t, :], s, 2 * (t + 1))

            def memory_queries(grp, nth):
                for t in grp.tiles:
                    copy_rowsT(grp.hnT, grp.at[t], rows_of(t))
                for hh in range(HM):
                    n = HM * (nth - 1) + hh
                    act.wait_ge(qm_done, n + 1)
                    act.activation(grp.qT_m[:, hh, :], banks[2 + n % 4][:, 0:grp.width], ACT.Copy,
                                   scale=HDM ** -0.5).then_inc(qm_ready, 1)

            def memory_unit(grp, v):
                t, hh = divmod(v, HM)
                at = grp.at[t]
                act.wait_ge(m_max, v + 1)
                act.activation(grp.m_probs[:, v % 2, :], banks[v % 2][:, 0:NMEM], ACT.Exp,
                               bias=neg_max[:, v % 2:v % 2 + 1],
                               accum_out=exp_sum[:, 0, v % 2:v % 2 + 1]).then_inc(m_exp, 1)
                act.wait_ge(m_pT_done, v + 1)
                act.activation(grp.m_probsT[:, v % 2, :], banks[6 + v % 2][:, 0:NMEM], ACT.Copy).then_inc(m_pT_ready, 1)
                act.wait_ge(m_oT_done, v + 1)
                act.activation(grp.oT_m[:, hh, at:at + P], banks[4 + v % 2][:, 0:P], ACT.Copy).then_inc(m_oT_ready, 1)

            def expert_queries(grp, nth):
                for t in grp.tiles:
                    copy_rowsT(grp.hnT, grp.at[t], rows_of(t))
                for hh in range(H):
                    n = H * (nth - 1) + hh
                    act.wait_ge(qp_done, n + 1)
                    act.activation(grp.qT_p[:, hh, :], banks[2 + n % 4][:, 0:grp.width], ACT.Copy).then_inc(qp_ready, 1)

            def key_scores_of(t):
                R = rows_of(t)
                if t > 2:
                    act.wait_ge(routed, H * (t - 1))
                dst = s_held if t == 2 else s_all[:, t % 2, :]
                for m in range(4):
                    act.wait_ge(ps_done, 4 * t + m + 1)
                    act.activation(dst[0:R, m * 512:(m + 1) * 512], banks[4 + m][0:R, :], ACT.Copy
                                   ).then_inc(ps_ready, 1)

            def expert_weights(t):
                R, n = (P, SLOTS) if t < PT else (DB, DB)
                act.wait_ge(best_shift, t + 1)
                act.activation(best_e[0:R, :], best_e[0:R, :], ACT.Exp).then_inc(best_exp, 1)
                act.wait_ge(gelu_in, t + 1)
                act.activation(gtmp[:, 0, 0:n], gtmp[:, 0, 0:n], ACT.Tanh, scale=GELU_B).then_inc(gelu_tanh, 1)

            act.wait_ge(cat_ready, PT)
            act.wait_ge(state_stored, 16)
            act.wait_ge(mem_in, 48)
            for t in range(2):
                mean_square(mem_x[:, t, :], hn3[:, t, :])
            rows_transposed(front)
            for t in range(2):
                copy_rowsT(mT, t * P, P)
            tile_norms(front, out_added)
            for n in range(4):
                act.wait_ge(mkv_done, n + 1)
                act.activation((mk, mv)[n // 2][:, n % 2, :], banks[(6, 7, 2, 3)[n]][:, :], ACT.Copy).then_inc(mkv_ready, 1)
            for t in range(2):
                act.wait_ge(mkT_done, t + 1)
                act.activation(mkT[:, :, t * P:(t + 1) * P], banks[t][:, :].rearrange("p (k r) -> p k r", k=4),
                               ACT.Copy).then_inc(mkT_ready, 1)
            act.wait_ge(sk_zero, 1)
            for half in range(2):
                act.wait_ge(subT_done, half + 1)
                src = banks[4 + half][:, :].rearrange("p (k r) -> p k r", k=4)
                act.activation(skT[0:64, 4 * half:4 * half + 4, 0:P], src[0:64], ACT.Copy)
                act.activation(skT[64:P, 4 * half:4 * half + 4, P:2 * P], src[64:P], ACT.Copy).then_inc(subT_ready, 1)
            act.wait_ge(y_stored, 16 * 6)
            memory_queries(front, 1)
            for v in range(HM * len(front.tiles)):
                memory_unit(front, v)
            tile_norms(front, mo_added)
            expert_queries(front, 1)
            for t in front.tiles:
                key_scores_of(t)

            def background():
                act.wait_ge(s_rows_in, 16 * N_SROWS)
                act.activation(s_rows[0:64, S_T, :], s_rows[0:64, S_RG, :], ACT.Tanh, scale=0.5).then_inc(tanh_ready, 1)
                act.activation(gate[0:64, 0:3], col[0:64, 0:3], ACT.Tanh, scale=0.5).then_inc(tanh_ready, 1)
                act.wait_ge(sT_done, 1)
                act.activation(sqT[0:64, :], banks[0][0:64, 0:64], ACT.Copy, scale=0.125).then_inc(sT_ready, 1)
                yield 1
                yield 2
                act.wait_ge(s_max, 1)
                act.activation(cmp_p[0:64, :], s_scores[0:64, 0:256], ACT.Exp, bias=neg_max[0:64, 0:1],
                               accum_out=exp_sum[0:64, 0, 0:1]).then_inc(s_exp, 1)
                yield 3
                act.wait_ge(s_pT_done, 1)
                act.activation(cmp_pT, banks[2][:, 0:128].rearrange("p (x r) -> p x r", x=2), ACT.Copy).then_inc(s_pT_ready, 1)
                yield 4
                gi = 0
                for kind, nj in enumerate((8, 4)):
                    for i in range(BG * nj // 4):
                        act.wait_ge(s_keyT_done, gi + 1)
                        act.activation(keyT[0:HD, gi % 2, :], banks[gi % 2][0:HD, :], ACT.Copy).then_inc(s_keyT_ready, 1)
                        gi += 1
                    yield 5 + 3 * kind
                    act.wait_ge(s_max, 2 + kind)
                    N = nj * P + 1
                    act.activation(s_probs[0:64, 0:N], s_scores[0:64, 0:N], ACT.Exp, bias=neg_max[0:64, 1 + kind:2 + kind],
                                   accum_out=exp_sum[0:64, 0, 1 + kind:2 + kind]).then_inc(s_exp, 1)
                    act.wait_ge(s_pT_done, 2 + kind)
                    act.activation(s_probsT[:, 0:nj, :], banks[6][:, 0:nj * 64].rearrange("p (x r) -> p x r", x=nj),
                                   ACT.Copy).then_inc(s_pT_ready, 1)
                    yield 6 + 3 * kind
                    act.wait_ge(s_oT_done, 1 + kind)
                    act.activation(s_o[0:HD, 0, :], banks[7][0:HD, 0:64], ACT.Copy).then_inc(s_oT_ready, 1)
                    yield 7 + 3 * kind
                for step in (11, 12, 13):
                    yield step
                act.wait_ge(gn_var, PT + 1)
                act.activation(gn_r[0:64, 0:1], gn_v[0:64, 0:1], ACT.Sqrt, bias=eps_col[0:64, :]).then_inc(gn_std, 1)
                yield 14
                rows_transposed(back)
                yield 15
                tile_norms(back, out_added)
                yield 16
                memory_queries(back, 2)
                yield 17
                v0 = HM * back.tiles[0]
                for v in range(v0, v0 + HM):
                    memory_unit(back, v)
                    yield 18 + v - v0
                v = PT * HM
                for g in range(2 * DB):
                    act.wait_ge(m_keyT_done, g + 1)
                    act.activation(mkT_s[:, g % 2, :], banks[g % 2][:, :], ACT.Copy).then_inc(m_keyT_ready, 1)
                yield 22
                act.wait_ge(m_max, v + 1)
                act.activation(ms_probs[0:32, :], banks[2][0:32, 0:NMEM], ACT.Exp, bias=neg_max[0:32, 0:1],
                               accum_out=exp_sum[0:32, 0, 0:1]).then_inc(m_exp, 1)
                yield 23
                act.wait_ge(m_pT_done, v + 1)
                act.activation(ms_probsT, banks[3][:, 0:64].rearrange("p (x r) -> p x r", x=2), ACT.Copy
                               ).then_inc(m_pT_ready, 1)
                act.wait_ge(m_oT_done, v + 2)
                act.activation(back.oT_m[:, :, P:P + DB], banks[4][:, 0:32].rearrange("p (k r) -> p k r", k=HM), ACT.Copy
                               ).then_inc(m_oT_ready, 1)
                yield 24
                tile_norms(back, mo_added)
                yield 25
                expert_queries(back, 2)
                key_scores_of(3)
                yield 26

            steps = background()
            advance(steps, STEP_AT[SLOTS // RING - 1])
            expert_weights(0)
            act.wait_ge(routed, H)
            act.activation(s_all[:, 0, :], s_held, ACT.Copy).then_inc(scores_moved, 1)
            advance(steps, STEP_AT[(ROWS + SLOTS) // RING - 1])
            expert_weights(1)
            mean_square(h[:, 0, :], hn3[:, 0, :], row_used, ROWS)
            advance(steps, LAST_STEP)
            key_scores_of(SAMPLE)
            for t in (2, 3):
                expert_weights(t)
                mean_square(h[:, t - 1, :], hn3[:, t - 1, :], row_used, ROWS * t)
            expert_weights(SAMPLE)
            mean_square(h[:, PT - 1, :], hn3[:, PT - 1, :], row_used, ROWS * PT)
            mean_square(h[0:DB, SAMPLE, :], hn3[:, SAMPLE, :], x_done, 1)

        @block.vector
        def _(dve):
            order = Order(dve, vector_order)
            norms = [0]
            tt, ts, stt, red = dve.tensor_tensor, dve.tensor_scalar, dve.scalar_tensor_tensor, dve.tensor_reduce

            def normed(dst, x, g, s=None, v=None):
                n = norms[0]
                norms[0] += 1
                R = x.shape[0]
                r = rstd[0:R, n % 16:n % 16 + 1]
                dve.wait_ge(std_ready, n + 1)
                order(dve.reciprocal(r, r))
                if s is not None:
                    dve.wait_ge(s, v)
                return stt(out=dst[0:R, :], in0=x, scalar=r, in1=g[0:R, :], op0=ALU.mult, op1=ALU.mult)

            dve.wait_ge(consts_in, 16 * (3 + len(const_loads)))
            dve.memset(eps_col, EPS).then_inc(eps_set, 1)
            for t in range(NT):
                args = (hnT_done, 2 * (t - 1)) if t >= 2 else ()
                normed(hn_buf[:, t % 2, :], h[0:rows_of(t), t, :], gain[:, MIX, :], *args).then_inc(hn_ready, 1)
            order(dve.tensor_copy(page_f, page_i[:, :]))
            ts(blk_idx[:, :], page_f[:, 0:2], 4.0, row_add[:, 0:1], ALU.mult, ALU.add).then_inc(idx_ready, 1)
            for g in range(G):
                ins = ts(row_idx[:, g:BG:G], page_f[:, 2:10], 32.0, row_add[:, 1 + g:2 + g], ALU.mult, ALU.add)
            ins.then_inc(idx_ready, 1)

            def rotate(x1, x2, cos, sin, t4):
                tt(t4[0], x1, cos, ALU.mult)
                tt(t4[1], x2, sin, ALU.mult)
                tt(t4[2], x1, sin, ALU.mult)
                order(tt(t4[3], x2, cos, ALU.mult))
                tt(x1, t4[0], t4[1], ALU.subtract)
                return tt(x2, t4[2], t4[3], ALU.add)

            dve.wait_ge(proj_ready, NT * len(CHUNKS))
            for t in range(NT):
                R = rows_of(t)
                x = proj[t][0:R, 0:1024].rearrange("p (s h d) -> p s h d", s=2, h=H)
                tab = [rot_ret[0:R, t, i].unsqueeze(2).broadcast_to((R, 2, H, 32)) for i in range(2)]
                tv = [rot_t[0:R, i, :].rearrange("p (s h d) -> p s h d", s=2, h=H) for i in range(4)]
                order(rotate(x[:, :, :, 0:32], x[:, :, :, 32:64], tab[0], tab[1], tv))
                x = proj[t][0:R, C_NQ:C_NQ + 512].rearrange("p (h d) -> p h d", h=H)
                tab = [rot_nsa[0:R, t, i].unsqueeze(1).broadcast_to((R, H, 8)) for i in range(2)]
                tv = [rot_t[0:R, i, 0:64].rearrange("p (h d) -> p h d", h=H) for i in range(4)]
                order(rotate(x[:, :, 0:8], x[:, :, 8:16], tab[0], tab[1], tv))
                x = proj[t][0:R, C_CK:C_CK + 768].rearrange("p (y z g d) -> p y z g d", y=3, z=2, g=G)[:, :, 0]
                tab = [rot_nsa[0:R, t, i].unsqueeze(1).unsqueeze(1).broadcast_to((R, 3, G, 8)) for i in range(2)]
                tv = [rot_t[0:R, i, 0:48].rearrange("p (y g d) -> p y g d", y=3, g=G) for i in range(4)]
                rotate(x[:, :, :, 0:8], x[:, :, :, 8:16], tab[0], tab[1], tv).then_inc(rotated, 1)
                dve.wait_ge(rotated, t + 1)

            dve.memset(c_vblk[0:64, :], 0.0).then_inc(vblk_zero, 1)
            for unit in range(6):
                dve.wait_ge(cmp_done, unit + 1)
                bank = banks[4 + unit % 2]
                x = unit % 3
                if unit < 3:
                    R = P if x < 2 else BG
                    ins = ts(c_kT[0:HD, x * P:x * P + R], bank[0:HD, 0:R], cmp_bk[0:HD, :], None, ALU.add)
                elif x < 2:
                    ins = tt(c_v[:, x, :], bank[:, 0:HD], cmp_bv, ALU.add)
                else:
                    ins = tt(cv_out[0:BG, :], bank[0:BG, 0:HD], cmp_bv[0:BG, :], ALU.add)
                ins.then_inc(cmp_ready, 1)

            def wide(v, R, n=H, m=HD):
                return v.unsqueeze(2).broadcast_to((R, n, m))

            def heads(v, n=H):
                return v.rearrange("p (h d) -> p h d", h=n)

            def group_norm(o, sq, mean, R, n, t):
                order(red(mean, o, AX.X, ALU.add))
                order(ts(mean, mean, 1.0 / HD, None, ALU.mult))
                order(tt(o, o, wide(mean, R, n), ALU.subtract))
                order(tt(sq, o, o, ALU.mult))
                order(red(gn_v[0:R, 0:n], sq, AX.X, ALU.add))
                ts(gn_v[0:R, 0:n], gn_v[0:R, 0:n], 1.0 / HD, None, ALU.mult).then_inc(gn_var, 1)
                dve.wait_ge(gn_std, t + 1)
                order(dve.reciprocal(gn_r[0:R, 0:n], gn_r[0:R, 0:n]))
                order(tt(o, o, wide(gn_r[0:R, 0:n], R, n), ALU.mult))

            def branch_max(t, u):
                N = P * (t + 1)
                dve.wait_ge(sc_done, u + 1)
                red(neg_max[:, u % 16:u % 16 + 1], banks[u % 2][:, 0:N], AX.X, ALU.max, negate=True
                    ).then_inc(max_ready, 1)

            for t in range(PT):
                o, sq, x3, x4 = (heads(tmp[:, i, :]) for i in range(4))
                if t:
                    dve.wait_ge(ret_done, t)
                tt(vz, heads(proj[t][:, C_RV:C_RV + 512]), wide(zeta, P), ALU.mult).then_inc(vz_ready, 1)
                for m in range(2):
                    dve.wait_ge(att_done, 2 * t + m + 1)
                    tt(att[:, 4 * m:4 * m + 4, :], banks[2 + m][:, :].rearrange("p (k r) -> p k r", k=4),
                       decay[:, 4 * m:4 * m + 4, :], ALU.mult).then_inc(att_ready, 1)
                dve.wait_ge(cs_done, t + 1)
                cs3, cp3 = heads(cs_buf), heads(cp_buf)
                vis = cmp_vis[:, t, :].unsqueeze(1).broadcast_to((P, H, 8))
                neg = cmp_neg[:, t, :].unsqueeze(1).broadcast_to((P, H, 8))
                order(tt(cs3, heads(banks[7][:, 0:64]), neg, ALU.add))
                order(red(col[:, 0:8], cs3, AX.X, ALU.max))
                tt(cs3, cs3, wide(col[:, 0:8], P, H, 8), ALU.subtract).then_inc(cs_ready, 1)
                dve.wait_ge(cs_exp, t + 1)
                order(tt(cp3, cp3, vis, ALU.mult))
                order(red(col[:, 8:16], cp3, AX.X, ALU.add))
                order(ts(col[:, 8:16], col[:, 8:16], 1e-30, None, ALU.max))
                order(dve.reciprocal(col[:, 16:24], col[:, 8:16]))
                tt(cp3, cp3, wide(col[:, 16:24], P, H, 8), ALU.mult).then_inc(cp_ready, 1)
                dve.wait_ge(ret_done, t + 1)
                if t:
                    order(tt(o, heads(banks[4][:, :]), wide(xi, P), ALU.mult))
                    order(tt(o, o, heads(banks[5][:, :]), ALU.add))
                    order(tt(state[0:HD], state[0:HD], wide(g_chunk[0:HD], HD), ALU.mult))
                    tt(state[0:HD], state[0:HD], heads(banks[6][0:HD, :]), ALU.add).then_inc(state_ready, 1)
                else:
                    order(dve.tensor_copy(o, heads(banks[5][:, :])))
                    dve.tensor_copy(state[0:HD], heads(banks[6][0:HD, :])).then_inc(state_ready, 1)
                group_norm(o, sq, col[:, 24:32], P, H, t)
                order(tt(tmp[:, 0, :], tmp[:, 0, :], gn_gain, ALU.mult))
                dve.wait_ge(tanh_ready, 2 * t + 2)
                order(stt(out=tmp[:, 1, :], in0=tanh_rg, scalar=1.0, in1=proj[t][:, C_RG:C_RG + 512],
                          op0=ALU.add, op1=ALU.mult))
                stt(out=cat[:, t, 0:512], in0=tmp[:, 0, :], scalar=0.5, in1=tmp[:, 1, :], op0=ALU.mult, op1=ALU.mult)
                order(ts(gate, gate, 0.5, 0.5, ALU.mult, ALU.add))
                gate3 = gate.rearrange("p (h x) -> p h x", x=3)
                nsa = heads(cat[:, t, 512:1024])
                dve.wait_ge(co_done, t + 1)
                tt(nsa, heads(banks[2][:, :]), wide(gate3[:, :, 0], P), ALU.mult).then_inc(co_used, 1)
                dve.wait_ge(co_used, t + 1)
                u0 = 2 * H * t
                branch_max(t, u0)
                for u in range(u0, u0 + 2 * H):
                    if u + 1 < u0 + 2 * H:
                        branch_max(t, u + 1)
                    N = P * (t + 1)
                    dve.wait_ge(pT_done, u + 1)
                    dve.tensor_copy(probsT[:, u % 2, 0:N], banks[3 + u % 2][:, 0:N]).then_inc(pT_ready, 1)
                    if u % H == H - 1:
                        kind = u % 16 // H
                        dve.wait_ge(ao_done, 2 * t + kind + 1)
                        order(dve.reciprocal(gate_w, exp_sum[:, kind, :]))
                        order(tt(gate_w, gate_w, gate3[:, :, 1 + kind], ALU.mult))
                        tt(x3, heads(banks[5 + kind][:, :]), wide(gate_w, P), ALU.mult).then_inc(ao_used, 1)
                        dve.wait_ge(ao_used, 2 * t + kind + 1)
                        ins = tt(nsa, nsa, x3, ALU.add)
                        if kind:
                            ins.then_inc(cat_ready, 1)
                        else:
                            order(ins)

            def residual(grp, s, added, bank_of):
                for t in grp.tiles:
                    R = rows_of(t)
                    for half in range(2):
                        n = 2 * t + half
                        dve.wait_ge(s, n + 1)
                        hv = h[0:R, t, half * 512:(half + 1) * 512]
                        tt(hv, hv, banks[bank_of(n)][0:R, :], ALU.add).then_inc(added, 1)

            def tile_norms(grp, g):
                for t in grp.tiles:
                    normed(hn3[:, t, :], h[0:rows_of(t), t, :], gain[:, g, :]).then_inc(hn_ready, 1)

            def mem_max(v, R=P, b=None):
                dve.wait_ge(m_sc_done, v + 1)
                red(neg_max[0:R, v % 2:v % 2 + 1], banks[v % 2 if b is None else b][0:R, 0:NMEM], AX.X, ALU.max,
                    negate=True).then_inc(m_max, 1)

            def mem_norm(v, dst):
                R = dst.shape[0]
                dve.wait_ge(m_exp, v + 1)
                order(dve.reciprocal(col[0:R, 14:15], exp_sum[0:R, 0, v % 2:v % 2 + 1]))
                ts(dst, dst, col[0:R, 14:15], None, ALU.mult).then_inc(m_norm, 1)

            out_bank, mo_bank = (lambda n: 2 + n % 4), (lambda n: 2 + n % 2)
            dve.wait_ge(mem_in, 48)
            dve.memset(skT, 0.0).then_inc(sk_zero, 1)
            for t in range(2):
                normed(hn3[:, t, :], mem_x[:, t, :], memn_gain).then_inc(hn_ready, 1)
            residual(front, out_done, out_added, out_bank)
            dve.wait_ge(hnT_done, 2 * (NT + 2))
            tile_norms(front, MEM)
            mem_max(0)
            for v in range(HM * len(front.tiles)):
                if v + 1 < HM * len(front.tiles):
                    mem_max(v + 1)
                mem_norm(v, front.m_probs[:, v % 2, :])
            residual(front, mo_done, mo_added, mo_bank)
            tile_norms(front, FFN)

            def background():
                row = lambda i: s_rows[0:64, i, :]
                dve.wait_ge(sT_ready, 1)
                dve.wait_ge(own_q_in, 16)
                tt(q_mask[0:64], own_q[0:64], sqT[0:64, :].unsqueeze(1).broadcast_to((64, BG, 64)), ALU.mult
                   ).then_inc(qmask_ready, 1)
                yield 1
                dve.wait_ge(s_sc_done, 1)
                order(tt(s_scores[0:64, 0:256], banks[1][0:64, 0:256], own_neg[0:64, :], ALU.add))
                red(neg_max[0:64, 0:1], s_scores[0:64, 0:256], AX.X, ALU.max, negate=True).then_inc(s_max, 1)
                yield 2
                dve.wait_ge(s_exp, 1)
                order(dve.reciprocal(col[0:64, 10:11], exp_sum[0:64, 0, 0:1]))
                order(ts(cmp_p[0:64, :], cmp_p[0:64, :], col[0:64, 10:11], None, ALU.mult))
                order(red(s_small[0:64, 0:32], cmp_p[0:64, :].rearrange("p (x y) -> p y x", x=8), AX.X, ALU.add))
                red(s_small[0:64, 32:48].rearrange("p (i k) -> p i k", k=2),
                    s_small[0:64, 0:32].rearrange("p (i g k) -> p i k g", g=G, k=2), AX.X, ALU.add).then_inc(s_imp, 1)
                dve.wait_ge(tanh_ready, 2 * PT + 2)
                order(ts(gate[0:64, 0:3], gate[0:64, 0:3], 0.5, 0.5, ALU.mult, ALU.add))
                yield 3
                dve.wait_ge(s_o_done, 1)
                order(ts(s_o[0:64, 3, :], banks[3][0:64, 0:64], gate[0:64, 0:1], None, ALU.mult))
                imp, eq, key = (s_small[0:64, x:x + 16] for x in (48, 64, 80))
                tt(imp, banks[3][0:64, 64:80], blk_excl[0:64, :], ALU.add).then_inc(s_branch, 1)
                dve.wait_ge(s_branch, 1)
                order(red(col[0:64, 11:12], imp, AX.X, ALU.min))
                order(ts(eq, imp, col[0:64, 11:12], None, ALU.is_equal))
                order(tt(key, eq, blk_rank[0:64, :], ALU.mult))
                order(red(col[0:64, 12:13], key, AX.X, ALU.max))
                order(ts(drop_neg[0:64, :], key, col[0:64, 12:13], NEG, ALU.is_equal, ALU.mult))
                yield 4
                for kind, nj in enumerate((8, 4)):
                    N = nj * P
                    yield 5 + 3 * kind
                    dve.wait_ge(s_sc_done, 2 + kind)
                    for cc in range(nj // 4):
                        if kind == 0:
                            v = "p (j y x) -> p j y x"
                            ins = tt(s_scores[0:64, cc * 512:(cc + 1) * 512].rearrange(v, j=4, y=16),
                                     banks[4 + cc][0:64, :].rearrange(v, j=4, y=16),
                                     drop_neg[0:64, :].unsqueeze(1).unsqueeze(3).broadcast_to((64, 4, 16, 8)), ALU.add)
                        else:
                            ins = dve.tensor_copy(s_scores[0:64, 0:512], banks[4][0:64, :])
                    order(ins)
                    if kind == 1:
                        order(ts(s_scores[0:64, 0:1], s_scores[0:64, 0:1], NEG, None, ALU.add))
                    order(dve.tensor_tensor_reduce(out=row(S_U), in0=row(S_NQ), in1=row((S_SK, S_WK)[kind]), scale=0.125,
                                                   scalar=0.0, op0=ALU.mult, op1=ALU.add,
                                                   accum_out=s_scores[0:64, N:N + 1]))
                    red(neg_max[0:64, 1 + kind:2 + kind], s_scores[0:64, 0:N + 1], AX.X, ALU.max, negate=True
                        ).then_inc(s_max, 1)
                    yield 6 + 3 * kind
                    dve.wait_ge(s_exp, 2 + kind)
                    order(dve.reciprocal(col[0:64, 13:14], exp_sum[0:64, 0, 1 + kind:2 + kind]))
                    order(tt(col[0:64, 13:14], col[0:64, 13:14], gate[0:64, 1 + kind:2 + kind], ALU.mult))
                    dve.wait_ge(s_o_done, 2 + kind)
                    order(stt(out=s_o[0:64, 1, :], in0=row((S_SV, S_WV)[kind]), scalar=s_probs[0:64, N:N + 1],
                              in1=banks[3][0:64, 0:64], op0=ALU.mult, op1=ALU.add))
                    stt(out=s_o[0:64, 3, :], in0=s_o[0:64, 1, :], scalar=col[0:64, 13:14], in1=s_o[0:64, 3, :],
                        op0=ALU.mult, op1=ALU.add).then_inc(s_branch, 1)
                    dve.wait_ge(s_branch, 2 + kind)
                    yield 7 + 3 * kind
                q_d = row(S_RQ).unsqueeze(2).broadcast_to((64, HD, HD))
                k_d = row(S_RK).unsqueeze(2).broadcast_to((64, HD, HD))
                v_e = row(S_RV).unsqueeze(1).broadcast_to((64, HD, HD))
                dve.wait_ge(s_state_in, 16)
                order(tt(s_prod[0:64], s_state[0:64], q_d, ALU.mult))
                yield 11
                order(red(row(S_Y), s_prod[0:64].rearrange("p d e -> p e d"), AX.X, ALU.add))
                order(ts(row(S_Y), row(S_Y), gamma1[0:64, :], None, ALU.mult))
                order(dve.tensor_tensor_reduce(out=row(S_U), in0=row(S_RQ), in1=row(S_RK), scale=1.0, scalar=0.0,
                                               op0=ALU.mult, op1=ALU.add, accum_out=col[0:64, 8:9]))
                order(stt(out=row(S_Y), in0=row(S_RV), scalar=col[0:64, 8:9], in1=row(S_Y), op0=ALU.mult, op1=ALU.add))
                yield 12
                order(tt(s_prod[0:64], k_d, v_e, ALU.mult))
                yield 13
                stt(out=s_state[0:64].rearrange("p d e -> p (d e)"), in0=s_state[0:64].rearrange("p d e -> p (d e)"),
                    scalar=gamma1[0:64, :], in1=s_prod[0:64].rearrange("p d e -> p (d e)"),
                    op0=ALU.mult, op1=ALU.add).then_inc(s_branch, 1)
                y3 = row(S_Y).unsqueeze(1)
                group_norm(y3, row(S_U).unsqueeze(1), col[0:64, 9:10], 64, 1, PT)
                order(tt(row(S_Y), row(S_Y), gn_rows[0:64, :], ALU.mult))
                order(stt(out=row(S_U), in0=row(S_T), scalar=1.0, in1=row(S_RG), op0=ALU.add, op1=ALU.mult))
                stt(out=row(S_Y), in0=row(S_Y), scalar=0.5, in1=row(S_U), op0=ALU.mult, op1=ALU.mult
                    ).then_inc(s_cat_ready, 1)
                yield 14
                residual(back, out_done, out_added, out_bank)
                yield 15
                tile_norms(back, MEM)
                yield 16
                v0 = HM * back.tiles[0]
                mem_max(v0)
                yield 17
                for v in range(v0, v0 + HM):
                    if v + 1 < v0 + HM:
                        mem_max(v + 1)
                    mem_norm(v, back.m_probs[:, v % 2, :])
                    if v == v0:
                        dve.wait_ge(qm_ready, 2 * HM)
                        dve.wait_ge(own_m_in, 16)
                        tt(qm_mask.rearrange("p c (h b) -> p c h b", h=HM), own_m.rearrange("p c (h b) -> p c h b", h=HM),
                           back.qT_m[:, :, P:P + DB].unsqueeze(1).broadcast_to((P, 32, HM, DB)), ALU.mult
                           ).then_inc(m_qmask, 1)
                    yield 18 + v - v0
                mem_max(PT * HM, 32, 2)
                yield 22
                mem_norm(PT * HM, ms_probs[0:32, :])
                yield 23
                residual(back, mo_done, mo_added, mo_bank)
                yield 24
                tile_norms(back, FFN)
                yield 25
                yield 26

            def route_head(t, head, rows_before):
                R = rows_of(t)

                def best16(vals, idx, src):
                    n = src.shape[1]
                    rows_before(True)
                    for x in range(n):
                        ins = dve.max(vals[0:R, x, 0:8], src[0:R, x, :])
                    yield ins
                    rows_before(True)
                    for x in range(n):
                        dve.max_index(idx[0:R, x, 0:8], vals[0:R, x, 0:8], src[0:R, x, :])
                        ins = dve.match_replace(src[0:R, x, :], vals[0:R, x, 0:8], src[0:R, x, :], -3.0e38)
                    yield ins
                    rows_before(True)
                    for x in range(n):
                        ins = dve.max(vals[0:R, x, 8:16], src[0:R, x, :])
                    yield ins
                    rows_before(True)
                    for x in range(n):
                        ins = dve.max_index(idx[0:R, x, 8:16], vals[0:R, x, 8:16], src[0:R, x, :])
                    yield ins

                yield dve.tensor_copy(s_head[0:R].rearrange("p x n -> p (x n)"), s_all[0:R, t % 2, bass.ds(head * 256, 256)])
                yield from best16(top_v, top_i, s_head)
                rows_before()
                dve.tensor_copy(top_f[0:R], top_i[0:R])
                yield tt(cand[0:R, :].rearrange("p (i j) -> p i j", i=TOPK),
                         top_v[0:R, 0, :].unsqueeze(2).broadcast_to((R, TOPK, TOPK)),
                         top_v[0:R, 1, :].unsqueeze(1).broadcast_to((R, TOPK, TOPK)), ALU.add)
                yield from best16(head_v.unsqueeze(1), head_i[:, :].unsqueeze(1), cand.unsqueeze(1))
                rows_before()
                ts(ab_i[0:R, 0, :], head_i[0:R, :], 4, None, ALU.logical_shift_right)
                yield ts(ab_i[0:R, 1, :], head_i[0:R, :], 15, None, ALU.bitwise_and)
                rows_before()
                yield dve.tensor_copy(ab_f[0:R], ab_i[0:R])
                rows_before()
                for x in range(2):
                    ins = tt(onehot[0:R, x], ab_f[0:R, x, :].unsqueeze(2).broadcast_to((R, TOPK, TOPK)),
                             iota16[0:R].unsqueeze(1).broadcast_to((R, TOPK, TOPK)), ALU.is_equal)
                yield ins
                rows_before()
                for x in range(2):
                    ins = tt(onehot[0:R, x], onehot[0:R, x], top_f[0:R, x, :].unsqueeze(1).broadcast_to((R, TOPK, TOPK)),
                             ALU.mult)
                yield ins
                rows_before()
                yield red(pick[0:R], onehot[0:R], AX.X, ALU.add)
                rows_before()
                yield stt(out=pick[0:R, 0, :], in0=pick[0:R, 0, :], scalar=float(NKEY), in1=pick[0:R, 1, :],
                          op0=ALU.mult, op1=ALU.add)
                rows_before()
                dve.tensor_copy(best_v[0:R, t % 2, bass.ds(head * TOPK, TOPK)], head_v[0:R, :])
                experts = expert[:, t, :] if t < PT else expert_f
                dve.tensor_copy(experts[0:R, bass.ds(head * TOPK, TOPK)], pick[0:R, 0, :]).then_inc(routed, 1)
                yield None

            def gates_shifted(t):
                R = rows_of(t)
                b3 = best_v[0:R, t % 2, :].rearrange("p (h k) -> p h k", h=H)
                tt(heads(best_e[0:R, :]), b3, b3[:, :, 0:1].broadcast_to((R, H, TOPK)), ALU.subtract
                   ).then_inc(best_shift, 1)

            def gates_of(t):
                R = rows_of(t)
                dve.wait_ge(best_exp, t + 1)
                order(red(col[0:R, 16:24], heads(best_e[0:R, :]), AX.X, ALU.add))
                order(dve.reciprocal(col[0:R, 24:32], col[0:R, 16:24]))
                return tt(heads(gate_t[0:R, :]), heads(best_e[0:R, :]), wide(col[0:R, 24:32], R, H, TOPK), ALU.mult)

            def gelu_argument(x, n):
                w = gtmp[:, 0, 0:n]
                order(tt(w, x, x, ALU.mult))
                order(ts(w, w, GELU_A, 1.0, ALU.mult, ALU.add))
                tt(w, w, x, ALU.mult).then_inc(gelu_in, 1)

            def weights(c_out, x, g, n, t):
                dve.wait_ge(gelu_tanh, t + 1)
                order(stt(out=gtmp[:, 1, 0:n], in0=gtmp[:, 0, 0:n], scalar=1.0, in1=x, op0=ALU.add, op1=ALU.mult))
                return stt(out=c_out, in0=gtmp[:, 1, 0:n], scalar=0.5, in1=g, op0=ALU.mult, op1=ALU.mult)

            def final_norm(t):
                R = rows_of(t)
                normed(hn3[:, t, :], h[0:R, t, :], gain[:, 0, :]).then_inc(y_ready, 1)

            def u_row(t, k, turn, cell):
                dve.wait_ge(row_in[k], turn * 16)
                dve.tensor_tensor_reduce(out=ring[:, k, :], in0=ring[:, k, :], in1=hn3[:, t, :], scale=1.0,
                                         scalar=0.0, op0=ALU.mult, op1=ALU.add, accum_out=cell).then_inc(row_used, 1)

            def v_row(t, k, turn, used, slot):
                dve.wait_ge(row_in[k], turn * 16)
                dve.wait_ge(row_used, used)
                stt(out=h[:, t, :], in0=ring[:, k, :], scalar=coef[:, bass.ds(slot, 1)],
                    in1=h[:, t, :], op0=ALU.mult, op1=ALU.add).then_inc(row_used, 1)

            def between_tables(t):
                gates_shifted(t)
                dve.wait_ge(row_used, ROWS * t + SLOTS)
                if t >= 2:
                    dve.wait_ge(act_kept, 4 * (t - 1))
                gelu_argument(act_p, SLOTS)
                order(gates_of(t))
                order(weights(coef, act_p, gate_t, SLOTS, t))
                if t:
                    if t == 1:
                        dve.wait_ge(fin_gain_in, 16)
                    final_norm(t - 1)

            dve.wait_ge(ps_ready, 4)
            for ins in route_head(0, 0, lambda top=False: None):
                if ins is not None:
                    order(ins)
            steps = background()
            n = 0
            for t in (0, 1):
                for table in range(2):
                    if table:
                        between_tables(t)
                    for r in range(SLOTS):
                        if t == 0:
                            every, head, whose = 16, (r // 16 + 1 if table == 0 else r // 16), table
                        else:
                            every, head, whose = 32, 4 * table + r // 32, 2
                        if r % every == 0:
                            if r == 0:
                                dve.wait_ge(ps_ready, 4 * (whose + 1))
                                if whose == 2:
                                    dve.wait_ge(scores_moved, 1)
                            route = route_head(whose, head, lambda top=False: dve.wait_ge(row_used, n)) if head < H else iter(())
                        if table:
                            v_row(t, n % RING, n // RING + 1, n, r)
                        else:
                            u_row(t, n % RING, n // RING + 1, act_p[:, r:r + 1])
                        n += 1
                        ins = next(route, None)
                        if r % every == every - 1 and ins is not None:
                            order(ins)
                            next(route, None)
                        if n % RING == 0:
                            advance(steps, STEP_AT[n // RING - 1])
            for t in (2, 3):
                for table in range(2):
                    if table:
                        between_tables(t)
                    base_row = ROWS * t + SLOTS * table
                    dve.wait_ge(ps_ready, 4 * (t + 2))
                    with dve.Fori(0, 4) as i:
                        done = 0

                        def rows_before(top=False):
                            dve.wait_ge(row_used, i * 32 + (base_row + done))
                            if top:
                                dve.tensor_copy(waited, eps_col)

                        route = route_head(t + 1, i + 4 * table, rows_before)
                        for r in range(32):
                            turn = i * 4 + (base_row // RING + r // RING + 1)
                            if table:
                                v_row(t, r % RING, turn, i * 32 + (base_row + r), i * 32 + r)
                            else:
                                u_row(t, r % RING, turn, act_part[:, r:r + 1])
                            done = r + 1
                            next(route, None)
                        if table == 0:
                            dve.wait_ge(row_used, i * 32 + (base_row + 32))
                            dve.tensor_copy(act_p[:, bass.ds(i * 32, 32)], act_part).then_inc(act_kept, 1)
                            dve.wait_ge(act_kept, i + (4 * (t - 2) + 1))
            gates_shifted(SAMPLE)
            gates_of(SAMPLE).then_inc(gates_ready, 1)
            dve.wait_ge(rt_done, 1)
            dve.tensor_copy(gate_s, banks[0][:, DB:2 * DB])
            dve.tensor_copy(expert_s[:, :], banks[0][:, 0:DB]).then_inc(samples_routed, 1)
            dve.wait_ge(hns_in, 16)
            for b in range(DB):
                dve.wait_ge(row_in[b], 16 * (ROWS * PT // RING + 1))
                dve.tensor_tensor_reduce(out=ring[:, b, :], in0=ring[:, b, :], in1=hn_s[:, b, :], scale=1.0,
                                         scalar=0.0, op0=ALU.mult, op1=ALU.add,
                                         accum_out=act_p[:, b:b + 1]).then_inc(row_used, 1)
            dve.wait_ge(row_used, ROWS * PT + DB)
            gelu_argument(act_p[:, 0:DB], DB)
            order(weights(coef[:, 0:DB], act_p[:, 0:DB], gate_s, DB, PT))
            tt(coef_m, eye8, coef[:, 0:DB].unsqueeze(1).broadcast_to((P, DB, DB)), ALU.mult).then_inc(coefm_ready, 1)
            final_norm(PT - 1)
            dve.wait_ge(se_done, 1)
            for half in range(2):
                hv = h[0:DB, SAMPLE, half * 512:(half + 1) * 512]
                ins = tt(hv, hv, banks[6 + half][0:DB, :], ALU.add)
            ins.then_inc(x_done, 1)
            final_norm(SAMPLE)


def shape_constants():
    import numpy as np
    f = np.float32
    c = {}
    c["ident"] = np.eye(P, dtype=f)
    q, k = np.arange(P)[:, None], np.arange(P)[None, :]
    c["tri"] = np.where(k <= q, 0.0, NEG).astype(f)
    lg = np.log(f(1.0) - f(2.0) ** (-5.0 - np.arange(H, dtype=f))).astype(f)
    lg = lg.astype(np.float64)
    diff = (k - q).astype(np.float64)
    c["decay"] = np.where(diff[:, None, :] >= 0, np.exp(lg[None, :, None] * np.maximum(diff, 0)[:, None, :]), 0.0).astype(f)
    i = np.arange(P, dtype=np.float64)[:, None]
    c["xi"] = np.exp(lg[None, :] * (i + 1)).astype(f)
    c["zeta"] = np.exp(lg[None, :] * (P - 1 - i)).astype(f)
    c["g_chunk"] = np.broadcast_to(np.exp(lg * P)[None, :], (P, H)).astype(f)
    c["gamma1"] = np.tile(np.exp(lg), DB)[:, None].astype(f)
    tok = np.arange(SEQ).reshape(PT, P)
    blk_end = np.arange(8) * CMP + CMP - 1
    vis = (blk_end[None, None, :] <= tok[:, :, None]).transpose(1, 0, 2)
    c["cmp_vis"] = vis.astype(f)
    c["cmp_neg"] = np.where(vis, 0.0, NEG).astype(f)
    pos = np.concatenate([tok, np.full((1, P), PAST)]).astype(f).T

    def table(half, theta):
        inv = (f(theta) ** (-np.arange(half, dtype=f) / f(half))).astype(f)
        ang = (pos[:, :, None] * inv).astype(f).astype(np.float64)
        return np.cos(ang), np.sin(ang)
    cos, sin = table(32, 10000.0)
    scale = np.array([1.0, HD ** -0.5])[None, None, :, None]
    c["rot_ret"] = np.stack([cos[:, :, None] * scale, sin[:, :, None] * scale], 2).astype(f)
    cos, sin = table(8, 500000.0)
    c["rot_nsa"] = np.stack([cos, sin], 2).astype(f)
    qs = np.arange(64)
    blk = np.arange(256)
    own = (qs[:, None] // H == blk[None, :] // 32) & (qs[:, None] // R4 % G == blk[None, :] // 2 % G)
    c["own_neg"] = np.where(own, 0.0, NEG).astype(f)
    c["group"] = (qs[:, None] // R4 == qs[None, :] // R4).astype(f)
    c["blk_excl"] = np.broadcast_to(np.where(np.arange(16) == 0, 1e4, 0.0), (64, 16)).astype(f)
    c["blk_rank"] = np.broadcast_to(np.arange(1.0, 17.0), (64, 16)).astype(f)
    p = np.arange(P)
    c["row_add"] = np.stack([p % 4, p % 16, p % 16 + 16], 1).astype(f)
    c["iota16"] = np.broadcast_to(np.arange(16), (P, 16)).astype(f)
    c["eye8"] = np.broadcast_to(np.eye(DB), (P, DB, DB)).astype(f)
    c["own_q"] = np.broadcast_to((np.arange(BG)[:, None] == qs[None, :] // R4)[None], (64, BG, 64)).astype(f)
    c["own_m"] = np.broadcast_to(np.eye(32), (P, 32, 32)).astype(f)
    return {k: np.ascontiguousarray(v) for k, v in c.items()}


_DIRECT = ["x_prompt", "x_sample", "mem_prompt", "state_ret", "cache_cmp_k", "cache_cmp_v", "cache_slc_k",
           "cache_slc_v", "cache_win_k", "cache_win_v", "cache_mem_k", "cache_mem_v", "cmp_w", "peer_subkeys",
           "peer_u", "peer_v", "norm_final_g"]
_LAYER = ["norm_mix_g", "w_in", "w_out", "norm_mem_g", "mem_norm_g", "w_mq", "w_mk", "w_mv", "w_mo", "norm_ffn_g",
          "peer_wq"]
_OUTS = [("y_prompt", (1, SEQ, D)), ("y_sample", (DB, 1, D)), ("p_state", (1, 1, H, HD, HD)),
         ("p_cmp_k", (1, 1, PT, G, P, HD)), ("p_cmp_v", (1, 1, PT, G, P, HD)),
         ("p_slc_k", (1, 1, PT, G, P, HD)), ("p_slc_v", (1, 1, PT, G, P, HD)),
         ("p_win_k", (1, 1, G, 512, HD)), ("p_win_v", (1, 1, G, 512, HD)),
         ("p_mem_k", (1, 1, NMEM, HM, HDM)), ("p_mem_v", (1, 1, NMEM, HM, HDM)),
         ("s_state", (1, DB, H, HD, HD)),
         ("s_cmp_k", (1, DB, G, 1, HD)), ("s_cmp_v", (1, DB, G, 1, HD)),
         ("s_slc_k", (1, DB, G, 1, HD)), ("s_slc_v", (1, DB, G, 1, HD)),
         ("s_win_k", (1, DB, G, 512, HD)), ("s_win_v", (1, DB, G, 512, HD))]


def kernel(**inputs):
    import numpy as np
    import concourse.bacc as bacc
    from concourse.bass_utils import run_bass_kernel_spmd

    arrays = {}
    for name in _DIRECT:
        arrays[name] = np.ascontiguousarray(inputs[name])
    for name in _LAYER:
        arrays[name] = np.ascontiguousarray(inputs[name])[0]
    table = np.asarray(inputs["page_table"]).astype(np.int32)
    arrays["page_rows"] = np.concatenate([np.repeat(table.reshape(2, 32), 4, axis=1).T,
                                          np.repeat(table.T, 16, axis=0)], axis=1)
    gn = np.asarray(inputs["ret_gn_g"])[0]
    consts = shape_constants()
    consts["gn_gain"] = np.broadcast_to(gn[None, :], (P, 512))
    consts["gn_rows"] = np.tile(gn.reshape(H, HD), (DB, 1))
    consts["cmp_bv"] = np.broadcast_to(np.asarray(inputs["cmp_b"])[0, 1][None, :], (P, HD))
    consts["cmp_bk"] = np.asarray(inputs["cmp_b"])[0, 0][:, None]

    nc = bacc.Bacc("TRN2", target_bir_lowering=False, num_devices=1)

    def declare(group, prefix):
        aps = {}
        for name, value in group.items():
            value = np.ascontiguousarray(value)
            feed[prefix + name] = value
            aps[name] = nc.dram_tensor(prefix + name, value.shape, mybir.dt.from_np(value.dtype),
                                       kind="ExternalInput").ap()
        return aps

    feed = {}
    a = declare(arrays, "in_")
    c = declare(consts, "const_")
    out = {name: nc.dram_tensor("out_" + name, shape, F32, kind="ExternalOutput").ap() for name, shape in _OUTS}
    trunk_kernel(nc, a, c, out)
    r = run_bass_kernel_spmd(nc, [feed], core_ids=[0])
    return tuple(r.results[0]["out_" + name] for name, _ in _OUTS)
```

```python
from contextlib import ExitStack

import concourse.bass as bass
from concourse import mybir

ALU = mybir.AluOpType
ACT = mybir.ActivationFunctionType
AX = mybir.AxisListType
F32 = mybir.dt.float32
U32 = mybir.dt.uint32

P = 128
D = 1024
KC = D // P
SEQ = 512
PT = SEQ // P
DB = 8
NT = PT + 1
SAMPLE = PT
H = 8
HD = 64
G = 2
R4 = H // G
CMP = 64
PAST = 1024
PAGES = PAST // P
BG = DB * G
NMEM = 256
HM = 4
HDM = 128
NKEY = 128
TOPK = 16
SLOTS = H * TOPK
D_IN = 4 * 512 + 512 + 6 * P + 3 * H
C_RQ, C_RK, C_RV, C_RG, C_NQ, C_CK, C_CV, C_SK, C_SV, C_WK, C_WV, C_NG = (
    0, 512, 1024, 1536, 2048, 2560, 2688, 2816, 2944, 3072, 3200, 3328)
CHUNKS = [(c, min(512, D_IN - c)) for c in range(0, D_IN, 512)]
EPS = 1e-6
NEG = -1.0e30
RING = 8
TURNS = SLOTS // RING
ROWS = 2 * SLOTS
PE_SLOTS = (1, 4, 7)
V_TURN = [(2 * t + 1) * TURNS for t in range(PT)]
SCORE_BANKS = (0, 1, 7)
ROUTE_STEPS = 16
VALUES_AT = 5
STEP_TURNS = ((1, 1), (2, 2), (3, 3), (4, 4), (5, 5), (6, 8), (7, 13), (8, 15), (9, 19), (10, 20), (11, 23),
              (12, 24), (13, 25), (14, 26), (15, 31), (16, 34), (17, 35), (18, 38), (19, 40), (20, 41), (21, 42),
              (22, 43), (23, 44), (24, 45), (25, 50), (26, 51), (27, 52), (28, 57), (29, 58), (30, 61), (31, 69),
              (32, 70))
STEPS_DONE = 99
GELU_A = 0.044715
GELU_B = 0.7978845608028654


def rows_of(t):
    return P if t < PT else DB


class Arena:

    def __init__(self, tensor, at, end):
        self.tensor, self.at, self.end = tensor, at, end

    def take(self, *shape):
        n = 1
        for s in shape:
            n *= s
        a = self.at
        self.at += n
        assert self.at <= self.end, (self.at, self.end)
        v = self.tensor[:, a:a + n]
        names = "abcd"[:len(shape)]
        if len(shape) > 1:
            v = v.rearrange(f"p ({' '.join(names)}) -> p {' '.join(names)}", **dict(zip(names, shape)))
        return v

    def part(self, off, size):
        return Arena(self.tensor, self.at + off, self.at + off + size)


def trunk_kernel(nc, a, c, out):
    with ExitStack() as ctx:
        def sb(name, shape, dt=F32):
            return ctx.enter_context(nc.sbuf_tensor(name, shape, dt))

        def sem(name):
            return ctx.enter_context(nc.semaphore(name))

        def scratch(name, shape):
            return nc.dram_tensor(name, shape, F32, kind="Internal").ap()

        banks = [ctx.enter_context(nc.psum_tensor(f"bank{i}", [P, 512], F32)) for i in range(8)]

        sc_heads = scratch("sc_heads", (5, DB, 512))
        sc_gates = scratch("sc_gates", (DB, 3 * H))
        sc_cv = scratch("sc_cv", (BG, HD))
        sc_cat = scratch("sc_cat", (2, DB, 512))
        sc_hn = scratch("sc_hn", (DB, D))

        words = 51900
        arena = sb("arena", [P, words])
        base = Arena(arena, 0, words)
        h = base.take(NT, D)
        gain = base.take(3, D)
        MIX, MEM, FFN = range(3)
        eps_col = base.take(1)
        waited = base.take(1)
        gn_rows = base.take(HD)
        cmp_bv = base.take(HD)
        cmp_bk = base.take(1)
        ident = base.take(P)
        xi = base.take(H)
        zeta = base.take(H)
        g_chunk = base.take(H)
        gamma1 = base.take(1)
        cmp_vis = base.take(PT, H)
        cmp_neg = base.take(PT, H)
        own_neg = base.take(256)
        group = base.take(64)
        blk_excl = base.take(16)
        blk_rank = base.take(16)
        page_f = base.take(10)
        row_add = base.take(3)
        iota16 = base.take(16)
        eye8 = base.take(DB, DB)
        mean_sq = base.take(16)
        rstd = base.take(16)
        gn_v = base.take(H)
        gn_r = base.take(H)
        neg_max = base.take(16)
        exp_sum = base.take(2, H)
        gate = base.take(3 * H)
        gate_w = base.take(H)
        drop_neg = base.take(16)
        c_kT = base.take(272)
        c_v = base.take(2, HD)
        col = base.take(160)
        blk_idx = sb("blk_idx", [P, 2], U32)
        row_idx = sb("row_idx", [P, BG], U32)
        page_i = sb("page_i", [P, 10], mybir.dt.int32)
        x0 = base.at
        XW = words - x0

        proj = [base.part(t * D_IN, D_IN).take(D_IN) for t in range(NT)]
        cat = base.part(NT * D_IN, NT * D).take(NT, D)
        r2 = NT * D_IN + NT * D
        MIXC = 512 + P + H * P + NT * 128 + NT * 16 + 512
        R2W = XW - r2 - MIXC
        ar = base.part(XW - MIXC, MIXC)
        gn_gain = ar.take(512)
        tri = ar.take(P)
        decay = ar.take(H, P)
        rot_ret = ar.take(NT, 2, 2, 32)
        rot_nsa = ar.take(NT, 2, 8)
        c_vblk = ar.take(512)
        ar = base.part(r2, R2W)
        hnT = ar.take(KC, 520)
        hn_buf = ar.take(2, D)
        w_buf = ar.take(2, KC, 512)
        sq_junk = cat[:, 0, :]
        ar = base.part(r2, R2W)
        blk_buf = ar.take(2, CMP * HD)
        cmp_w = ar.take(2, 32, HD)
        blkT = ar.take(2, 4, P)
        cv_out = ar.take(HD)
        ar = base.part(r2, R2W)
        rqT = ar.take(H, P)
        rkT = ar.take(H, P)
        nqT = ar.take(H, P)
        kT = ar.take(2, G, SEQ)
        att = ar.take(H, P)
        probs = ar.take(3, SEQ)
        probsT = ar.take(2, SEQ)
        state = ar.take(H, HD)
        vz = ar.take(H, HD)
        tmp = ar.take(4, 512)
        rot_t = tmp
        tanh_rg = ar.take(512)
        cs_buf = ar.take(64)
        cp_buf = ar.take(64)
        cpT = ar.take(P)
        W_BANK, RING_AT, AREA2 = 0, KC * D, 2 * KC * D
        AREA2W = r2 - 2 * D - AREA2
        ar = base.part(r2, XW - r2)
        hn3 = ar.take(NT, D)
        s_all = ar.take(2, H * 256)
        s_held = hn3[:, 3:NT, :].rearrange("p t n -> p (t n)")
        skT = ar.take(H, 256)
        mv = ar.take(2, 512)
        mkT = ar.take(HM, NMEM)
        act_p = ar.take(SLOTS)
        act_part = ar.take(16)
        diag = ar.take(len(PE_SLOTS), P)
        coef = ar.take(SLOTS)
        gate_t = ar.take(SLOTS)
        gtmp = ar.take(2, SLOTS)
        gate_s = ar.take(DB)
        coef_m = ar.take(DB, DB)
        s_head = ar.take(2, NKEY)
        cand = ar.take(256)
        onehot = ar.take(2, TOPK, 16)
        top_v = ar.take(2, TOPK)
        top_f = ar.take(2, TOPK)
        head_v = ar.take(TOPK)
        best_v = ar.take(2, SLOTS)
        best_e = ar.take(SLOTS)
        ab_f = ar.take(2, TOPK)
        pick = ar.take(2, TOPK)
        expert_f = ar.take(SLOTS)
        AREA1, AREA1W = ar.at - x0, XW - (ar.at - x0)
        top_i = sb("top_i", [P, 2, TOPK], U32)
        head_i = sb("head_i", [P, TOPK], U32)
        ab_i = sb("ab_i", [P, 2, TOPK], U32)
        expert = sb("expert", [P, PT, SLOTS], U32)
        expert_s = sb("expert_s", [P, DB], U32)
        cursor = sb("cursor", [P, 2, RING], U32)
        ring = base.part(RING_AT, RING * D).take(RING, D)
        hn_s = base.part(W_BANK, DB * D).take(DB, D)

        ar = base.part(W_BANK, BG * 512)
        key_rows = ar.take(BG, 512)
        val_rows = key_rows
        ar = base.part(W_BANK, BG * 512)
        win_keys = ar.take(BG, 256)
        win_vals = ar.take(BG, 256)
        ar = base.part(W_BANK, BG * 512)
        s_state = ar.take(HD, HD)
        s_prod = ar.take(HD, HD)
        ar = base.part(AREA2, AREA2W)
        q_mask = ar.take(BG, 64)
        own_q = ar.take(BG, 64)
        keyT = ar.take(2, 512)
        cmp_p = ar.take(256)
        ar = base.part(AREA1, AREA1W)
        s_scores = ar.take(1028)
        s_probs = s_scores
        s_probsT = ar.take(8, 64)
        s_rows = ar.take(12, HD)
        cmp_pT = ar.take(2, 64)
        s_small = ar.take(96)
        s_o = ar.take(4, HD)
        sqT = ar.take(64)
        ar = base.part(W_BANK, KC * D)
        w_mk = ar.take(KC, 512)
        w_mv = ar.take(KC, 512)
        mem_x = s_all[:, 0, :].rearrange("p (t n) -> p t n", t=2)
        memn_gain = hn3[:, 3, :]
        sub_k = hn3[:, SAMPLE, :].rearrange("p (h n) -> p h n", h=H)
        ar = base.part(AREA1, AREA1W)
        mT = ar.take(KC, NMEM)
        mk = ar.take(2, 512)
        ar = base.part(W_BANK, KC * D)
        w_mq2 = ar.take(KC, 512)
        w_mo = ar.take(HM, D)
        w_mq1 = base.part(RING_AT, KC * 512).take(KC, 512)
        mem_piece = base.part(W_BANK, 4 * D).take(4, D)

        class Group:
            pass

        front, back = Group(), Group()
        front.tiles, back.tiles = (0, 1, 2), (3, SAMPLE)
        front.width, back.width = 3 * P, P + DB
        front.at, back.at = {0: 0, 1: P, 2: 2 * P}, {3: 0, SAMPLE: P}
        front.w_out = front.wq = base.part(RING_AT, KC * D).take(KC, D)
        back.w_out = back.wq = base.part(W_BANK, KC * D).take(KC, D)
        front.w_mq, back.w_mq = w_mq1, w_mq2
        front.hnT = base.part(AREA1, AREA1W).take(KC, front.width)
        catT2 = s_all[:, 1, :].rearrange("p (b k r) -> p b k r", b=2, k=KC)
        front.catT = {t: catT2[:, t % 2] for t in front.tiles}
        ar = base.part(NT * D_IN, 3 * D)
        front.qT_m = ar.take(HM, front.width)
        front.oT_m = ar.take(HM, front.width)
        front.qT_p = base.part(NT * D_IN, 3 * D).take(H, front.width)
        probs_at = s_all[:, 0, :].rearrange("p (x b n) -> p x b n", x=4, b=2)
        front.m_probs, front.m_probsT = probs_at[:, 0], probs_at[:, 1]
        ar = base.part(AREA1, AREA1W)
        back.hnT = ar.take(KC, back.width)
        back.catT = {t: back.hnT[:, :, back.at[t]:back.at[t] + rows_of(t)] for t in back.tiles}
        back.qT_p = Arena(arena, ar.at, ar.end).take(H, back.width)
        back.qT_m = ar.take(HM, back.width)
        back.oT_m = ar.take(HM, back.width)
        back.m_probs = ar.take(2, NMEM)
        back.m_probsT = ar.take(2, NMEM)
        ar = base.part(AREA2, AREA2W)
        qm_mask = ar.take(32, 32)
        own_m = ar.take(32, 32)
        mkT_s = ar.take(2, 512)
        ms_probs = ar.take(NMEM)
        ms_probsT = ar.take(2, 32)

        x_in = sem("x_in")
        consts_in = sem("consts_in")
        eps_set = sem("eps_set")
        mean_ready = sem("mean_ready")
        std_ready = sem("std_ready")
        hn_ready = sem("hn_ready")
        hnT_done = sem("hnT_done")
        hnT_ready = sem("hnT_ready")
        w_in_loaded = [sem("w_in_even"), sem("w_in_odd")]
        proj_done = sem("proj_done")
        proj_ready = sem("proj_ready")
        rotated = sem("rotated")
        rows_stored = sem("rows_stored")
        idx_ready = sem("idx_ready")
        blk_in = [sem("blk_even"), sem("blk_odd")]
        own_blk_in = sem("own_blk_in")
        cmpw_in = sem("cmpw_in")
        blkT_done = sem("blkT_done")
        blkT_ready = sem("blkT_ready")
        cmp_done = sem("cmp_done")
        cmp_ready = sem("cmp_ready")
        vblk_in = sem("vblk_in")
        vblk_zero = sem("vblk_zero")
        headT_done = sem("headT_done")
        headT_ready = sem("headT_ready")
        att_done = sem("att_done")
        att_ready = sem("att_ready")
        vz_ready = sem("vz_ready")
        ret_done = sem("ret_done")
        state_ready = sem("state_ready")
        cs_done = sem("cs_done")
        cs_ready = sem("cs_ready")
        cs_exp = sem("cs_exp")
        cp_ready = sem("cp_ready")
        cpT_done = sem("cpT_done")
        cpT_ready = sem("cpT_ready")
        co_done = sem("co_done")
        co_used = sem("co_used")
        sc_done = sem("sc_done")
        max_ready = sem("max_ready")
        exp_ready = sem("exp_ready")
        pT_done = sem("pT_done")
        pT_ready = sem("pT_ready")
        ao_done = sem("ao_done")
        ao_used = sem("ao_used")
        tanh_ready = sem("tanh_ready")
        cat_ready = sem("cat_ready")
        state_stored = sem("state_stored")
        s_rows_in = sem("s_rows_in")
        s_state_in = sem("s_state_in")
        s_stored = sem("s_stored")
        s_cat_in = sem("s_cat_in")
        scratch_stored = sem("scratch_stored")
        sT_done = sem("sT_done")
        sT_ready = sem("sT_ready")
        qmask_ready = sem("qmask_ready")
        key_in = [sem("page_keys_in"), sem("window_keys_in")]
        val_in = [sem("page_values_in"), sem("window_values_in")]
        gn_var = sem("gn_var")
        gn_std = sem("gn_std")
        s_keyT_done = sem("s_keyT_done")
        s_keyT_ready = sem("s_keyT_ready")
        s_sc_done = sem("s_sc_done")
        s_max = sem("s_max")
        s_exp = sem("s_exp")
        s_pT_done = sem("s_pT_done")
        s_pT_ready = sem("s_pT_ready")
        s_oT_done = sem("s_oT_done")
        s_oT_ready = sem("s_oT_ready")
        s_o_done = sem("s_o_done")
        s_imp = sem("s_imp")
        s_branch = sem("s_branch")
        w_out_in = sem("w_out_in")
        catT_done = sem("catT_done")
        catT_ready = sem("catT_ready")
        out_done = sem("out_done")
        out_added = sem("out_added")
        memw_in = sem("memw_in")
        mem_in = sem("mem_in")
        mkv_done = sem("mkv_done")
        mkv_ready = sem("mkv_ready")
        mkT_done = sem("mkT_done")
        mkT_ready = sem("mkT_ready")
        mq_in = sem("mq_in")
        qm_done = sem("qm_done")
        qm_ready = sem("qm_ready")
        m_sc_done = sem("m_sc_done")
        m_max = sem("m_max")
        m_exp = sem("m_exp")
        m_norm = sem("m_norm")
        m_pT_done = sem("m_pT_done")
        m_pT_ready = sem("m_pT_ready")
        m_oT_done = sem("m_oT_done")
        m_oT_ready = sem("m_oT_ready")
        memkv_in = sem("memkv_in")
        mo_in = sem("mo_in")
        m_keyT_done = sem("m_keyT_done")
        m_keyT_ready = sem("m_keyT_ready")
        mo_done = sem("mo_done")
        mo_added = sem("mo_added")
        wq_in = sem("wq_in")
        sub_in = sem("sub_in")
        subT_done = sem("subT_done")
        subT_ready = sem("subT_ready")
        qp_done = sem("qp_done")
        qp_ready = sem("qp_ready")
        ps_done = sem("ps_done")
        ps_ready = sem("ps_ready")
        scores_moved = sem("scores_moved")
        best_shift = sem("best_shift")
        best_exp = sem("best_exp")
        routed = sem("routed")
        gates_ready = sem("gates_ready")
        rt_done = sem("rt_done")
        hns_in = sem("hns_in")
        cursor_ready = sem("cursor_ready")
        row_in = [sem(f"row_in{k}") for k in range(RING)]
        row_free = [sem(f"row_free{k}") for k in range(RING)]
        diag_ready = sem("diag_ready")
        coef_ready = sem("coef_ready")
        sum_added = sem("sum_added")
        route_step = sem("route_step")
        act_kept = sem("act_kept")
        gelu_in = sem("gelu_in")
        gelu_tanh = sem("gelu_tanh")
        se_done = sem("se_done")
        sk_zero = sem("sk_zero")
        x_done = sem("x_done")
        y_ready = sem("y_ready")
        y_stored = sem("y_stored")
        fin_gain_in = sem("fin_gain_in")
        own_in = sem("own_in")
        s_cat_ready = sem("s_cat_ready")
        vector_order = sem("vector_order")
        scalar_order = sem("scalar_order")

        class Order:

            def __init__(self, eng, s):
                self.eng, self.sem, self.n = eng, s, 0

            def __call__(self, ins):
                ins.then_inc(self.sem, 1)
                self.n += 1
                self.eng.wait_ge(self.sem, self.n)

        const_loads = [
            (gn_gain, c["gn_gain"]), (gn_rows[0:64, :], c["gn_rows"]), (cmp_bv, c["cmp_bv"]),
            (cmp_bk[0:64, :], c["cmp_bk"]), (ident, c["ident"]), (tri, c["tri"]), (decay, c["decay"]),
            (xi, c["xi"]), (zeta, c["zeta"]), (g_chunk, c["g_chunk"]), (gamma1[0:64, :], c["gamma1"]),
            (cmp_vis, c["cmp_vis"]), (cmp_neg, c["cmp_neg"]), (rot_ret, c["rot_ret"]), (rot_nsa, c["rot_nsa"]),
            (own_neg[0:64, :], c["own_neg"]), (group[0:64, :], c["group"]), (blk_excl[0:64, :], c["blk_excl"]),
            (blk_rank[0:64, :], c["blk_rank"]), (row_add, c["row_add"]), (iota16, c["iota16"]),
            (eye8, c["eye8"]), (page_i, a["page_rows"]),
        ]
        heads64 = sc_heads.rearrange("x b (h d) -> x (b h) d", d=HD)
        S_RQ, S_RK, S_RV, S_RG, S_NQ, S_SK, S_SV, S_WK, S_WV, S_Y, S_T, S_U = range(12)
        N_SROWS = 5 + 4 + 1

        def progress(turn):
            for (step, begin), (_, end) in zip(STEP_TURNS, STEP_TURNS[1:]):
                if begin <= turn < end:
                    return step + (turn - begin + 1) / (end - begin + 1)
            return 0 if turn < STEP_TURNS[0][1] else STEP_TURNS[-1][0]

        def advance(steps, last):
            while upcoming.setdefault(steps, 0) <= last:
                upcoming[steps] = next(steps)

        upcoming = {}
        block = ctx.enter_context(nc.Block())

        @block.sync
        def _(sp):
            for t in range(NT):
                src = a["x_prompt"][0, t * P:(t + 1) * P, :] if t < PT else a["x_sample"][:, 0, :]
                sp.dma_start(h[0:rows_of(t), t, :], src).then_inc(x_in, 16)
            for i, name in enumerate(("norm_mix_g", "norm_mem_g", "norm_ffn_g")):
                sp.dma_start(gain[:, i, :], a[name].partition_broadcast(P)).then_inc(consts_in, 16)
            for dst, src in const_loads:
                sp.dma_start(dst[:], src).then_inc(consts_in, 16)
            w_in = a["w_in"].rearrange("(k p) n -> p k n", p=P)
            for i, (c0, n) in enumerate(CHUNKS):
                if i >= 2:
                    sp.wait_ge(proj_done, NT * (i - 1))
                sp.dma_start(w_buf[:, i % 2, :, 0:n], w_in[:, :, c0:c0 + n]).then_inc(w_in_loaded[i % 2], 16)
            for t in range(NT):
                sp.wait_ge(rotated, t + 1)
                R = rows_of(t)
                if t < PT:
                    for name, c0 in (("p_cmp_k", C_CK), ("p_cmp_v", C_CV), ("p_slc_k", C_SK), ("p_slc_v", C_SV)):
                        sp.dma_start(out[name][0, 0, t].rearrange("g k d -> k g d"),
                                     proj[t][:, c0:c0 + P].rearrange("p (g d) -> p g d", g=G)
                                     ).then_inc(rows_stored, 16)
                    for name, c0 in (("p_win_k", C_WK), ("p_win_v", C_WV)):
                        sp.dma_start(out[name][0, 0, :, t * P:(t + 1) * P].rearrange("g k d -> k g d"),
                                     proj[t][:, c0:c0 + P].rearrange("p (g d) -> p g d", g=G)
                                     ).then_inc(rows_stored, 16)
                else:
                    for name, c0 in (("s_cmp_k", C_CK), ("s_cmp_v", C_CV), ("s_slc_k", C_SK), ("s_slc_v", C_SV)):
                        sp.dma_start(out[name][0].rearrange("b g x d -> b (g x d)"),
                                     proj[t][0:R, c0:c0 + P]).then_inc(rows_stored, 16)
                    for name, c0 in (("s_win_k", C_WK), ("s_win_v", C_WV)):
                        sp.dma_start(out[name][0, :, :, 511, :], proj[t][0:R, c0:c0 + P].rearrange(
                            "p (g d) -> p g d", g=G)).then_inc(rows_stored, 16)
                    sp.dma_start(sc_heads.rearrange("x b n -> b x n"), proj[t][0:R, 0:5 * 512].rearrange(
                        "p (x n) -> p x n", x=5)).then_inc(rows_stored, 16)
                    sp.dma_start(sc_gates, proj[t][0:R, C_NG:C_NG + 3 * H]).then_inc(rows_stored, 16)
            ROWS_STORED = 16 * (PT * 6 + 8)
            for name, src in (("s_win_k", "cache_win_k"), ("s_win_v", "cache_win_v")):
                sp.dma_start(out[name][0, :, :, 0:511, :], a[src][0, :, :, 1:512, :]).then_inc(y_stored, 16)
            sp.wait_ge(proj_done, NT * len(CHUNKS))
            for i in range(2):
                sp.dma_start(cmp_w[:, i, :, :], a["cmp_w"][0, i].rearrange("j d e -> (j d) e").rearrange(
                    "(m q) e -> q m e", q=P)).then_inc(cmpw_in, 16)
            sp.wait_ge(rows_stored, ROWS_STORED)
            for i, name in enumerate(("p_cmp_k", "p_cmp_v")):
                n = 3 * i + 2
                if n >= 2:
                    sp.wait_ge(blkT_done, 8 * (n - 1))
                sp.dma_start(blk_buf[0:BG, n % 2, :], out[name][0, 0].rearrange(
                    "n g (k j) d -> (n g k) (j d)", k=2)).then_inc(own_blk_in, 16)
            sp.wait_ge(cmp_ready, 6)
            sp.dma_start(sc_cv, cv_out[0:BG, :]).then_inc(scratch_stored, 16)
            sp.wait_ge(scratch_stored, 16)
            sp.wait_ge(vblk_zero, 1)
            cvr = sc_cv.rearrange("(n g k) d -> g n k d", g=G, k=2)
            for hh in range(H):
                sp.dma_start(c_vblk[hh * 8:hh * 8 + 8, hh * HD:(hh + 1) * HD], cvr[hh // R4]).then_inc(vblk_in, 16)
            sp.wait_ge(state_ready, PT)
            sp.dma_start(out["p_state"][0, 0].rearrange("h d e -> d h e"), state[0:HD, :, :]).then_inc(state_stored, 16)
            sp.wait_ge(cat_ready, PT)
            sp.wait_ge(state_stored, 16)
            for t in range(2):
                sp.dma_start(mem_x[:, t, :], a["mem_prompt"][0, t * P:(t + 1) * P, :]).then_inc(mem_in, 16)
            sp.dma_start(memn_gain, a["mem_norm_g"].partition_broadcast(P)).then_inc(mem_in, 16)
            w_out = a["w_out"].rearrange("(k p) n -> p k n", p=P)
            sp.dma_start(front.w_out, w_out).then_inc(w_out_in, 16)
            for dst, name in ((w_mk, "w_mk"), (w_mv, "w_mv")):
                sp.dma_start(dst, a[name].rearrange("(k p) n -> p k n", p=P)).then_inc(memw_in, 16)
            sp.dma_start(sub_k.rearrange("p h (x d) -> p h x d", x=2),
                         a["peer_subkeys"][0].rearrange("h x k d -> k h x d")).then_inc(sub_in, 16)
            sp.dma_start(gain[:, MIX, :], a["norm_final_g"].partition_broadcast(P)).then_inc(fin_gain_in, 16)

            w_mq, w_mo_rows = (a[name].rearrange("(k p) n -> p k n", p=P) for name in ("w_mq", "w_mo"))
            wq = a["peer_wq"].rearrange("(k p) n -> p k n", p=P)
            sp.wait_ge(out_done, 2 * len(front.tiles))
            sp.dma_start(front.w_mq, w_mq).then_inc(mq_in, 16)
            sp.dma_start(front.wq[:, 4:8, :], wq[:, 4:8, :]).then_inc(wq_in, 16)
            sp.wait_ge(mkv_done, 4)
            sp.dma_start(w_mo, w_mo_rows).then_inc(mo_in, 16)
            for n in range(4):
                sp.wait_ge(mkv_ready, n + 1)
                buf, name, t = (mk, "p_mem_k", n) if n < 2 else (mv, "p_mem_v", n - 2)
                sp.dma_start(out[name][0, 0, t * P:(t + 1) * P].rearrange("m h d -> m (h d)"),
                             buf[:, t, :]).then_inc(y_stored, 16)
            sp.wait_ge(qm_done, HM)
            sp.dma_start(front.wq[:, 0:4, :], wq[:, 0:4, :]).then_inc(wq_in, 16)
            sp.wait_ge(qp_done, H)
            for i in range(5):
                sp.dma_start(s_rows[0:64, i, :], heads64[i]).then_inc(s_rows_in, 16)
            for i, name in ((S_SK, "s_slc_k"), (S_SV, "s_slc_v")):
                src = out[name][0].rearrange("b g x d -> (b g) x d")
                sp.dma_start(s_rows[0:64, i, :], src.broadcast_to((BG, R4, HD))).then_inc(s_rows_in, 16)
            for i, name in ((S_WK, "s_win_k"), (S_WV, "s_win_v")):
                src = out[name][0].rearrange("b g k d -> (b g) k d")[:, 511:512, :]
                sp.dma_start(s_rows[0:64, i, :], src.broadcast_to((BG, R4, HD))).then_inc(s_rows_in, 16)
            sp.dma_start(col[0:64, 0:3], sc_gates.rearrange("b (h x) -> (b h) x", x=3)).then_inc(s_rows_in, 16)
            sp.wait_ge(ps_done, 4 * len(front.tiles))
            sp.dma_start(own_q[0:64, :, :], c["own_q"]).then_inc(own_in, 16)
            sp.wait_ge(s_oT_done, 1)
            for dst, name, s in ((win_keys, "cache_win_k", key_in[1]), (win_vals, "cache_win_v", val_in[1])):
                sp.dma_start(dst, a[name][0].rearrange("b g (p j) d -> p (b g) (j d)", p=P)).then_inc(s, 16)
            sp.wait_ge(s_oT_done, 2)
            sp.dma_start(s_state[0:64, :, :], a["state_ret"][0].rearrange("b h d e -> (b h) d e")).then_inc(s_state_in, 16)
            sp.wait_ge(s_branch, 4)
            sp.dma_start(out["s_state"][0].rearrange("b h d e -> (b h) d e"), s_state[0:64, :, :]).then_inc(s_stored, 16)
            sp.wait_ge(s_cat_ready, 1)
            sp.dma_start(sc_cat[0].rearrange("b (h d) -> (b h) d", d=HD), s_rows[0:64, S_Y, :]).then_inc(scratch_stored, 16)
            sp.dma_start(sc_cat[1].rearrange("b (h d) -> (b h) d", d=HD), s_o[0:64, 3, :]).then_inc(scratch_stored, 16)
            sp.wait_ge(scratch_stored, 48)
            sp.dma_start(cat[0:DB, SAMPLE, :].rearrange("p (x n) -> p x n", x=2),
                         sc_cat.rearrange("x b n -> b x n")).then_inc(s_cat_in, 16)
            sp.wait_ge(s_stored, 16)
            sp.dma_start(back.w_out, w_out).then_inc(w_out_in, 16)
            sp.dma_start(own_m, c["own_m"]).then_inc(own_in, 16)
            sp.wait_ge(out_done, 2 * NT)
            sp.dma_start(back.w_mq, w_mq).then_inc(mq_in, 16)
            sp.dma_start(w_mo, w_mo_rows).then_inc(mo_in, 16)
            for piece, (s, v) in enumerate(((qm_done, 2 * HM), (m_keyT_done, DB), (m_keyT_done, 2 * DB),
                                            (m_oT_done, PT * HM + 1))):
                name, b0 = ("cache_mem_k", "cache_mem_v")[piece // 2], 4 * (piece % 2)
                sp.wait_ge(s, v)
                sp.dma_start(mem_piece, a[name][0].rearrange("b (p m) h d -> p b (m h d)", m=2)[:, b0:b0 + 4, :]
                             ).then_inc(memkv_in, 16)
            sp.wait_ge(mo_done, 2 * NT)
            sp.dma_start(back.wq, wq).then_inc(wq_in, 16)
            sp.wait_ge(hn_ready, 3 * NT + 2)
            sp.dma_start(sc_hn, hn3[0:DB, SAMPLE, :]).then_inc(scratch_stored, 16)
            sp.wait_ge(scratch_stored, 64)
            sp.wait_ge(qp_done, 2 * H)
            sp.dma_start(hn_s.rearrange("p b d -> p (b d)"), sc_hn.rearrange("b d -> (b d)").partition_broadcast(P)).then_inc(hns_in, 16)
            for t in range(NT):
                R = rows_of(t)
                sp.wait_ge(y_ready, t + 1)
                dst = out["y_prompt"][0, t * P:(t + 1) * P, :] if t < PT else out["y_sample"][:, 0, :]
                sp.dma_start(dst, hn3[0:R, t, :]).then_inc(y_stored, 16)
            sp.wait_ge(rows_stored, ROWS_STORED)
            sp.wait_ge(state_stored, 16)
            sp.wait_ge(s_stored, 16)
            sp.wait_ge(scratch_stored, 64)
            sp.wait_ge(y_stored, 16 * (2 + 4 + NT))

        @block.gpsimd
        def _(pool):
            pool.wait_ge(idx_ready, 2)
            pool.wait_ge(proj_done, NT * len(CHUNKS))
            for i, name in enumerate(("cache_cmp_k", "cache_cmp_v")):
                src = a[name][0].rearrange("n g (k j) d -> (n g k) (j d)", k=2)
                for x in range(2):
                    n = 3 * i + x
                    if n >= 2:
                        pool.wait_ge(blkT_done, 8 * (n - 1))
                    pool.indirect_dma_start(
                        out=blk_buf[:, n % 2, :], out_offset=None, in_=src,
                        in_offset=bass.IndirectOffsetOnAxis(ap=blk_idx[:, x:x + 1], axis=0)
                    ).then_inc(blk_in[n % 2], 16)

            def gather_pages(dst, name, s):
                src = a[name][0].rearrange("n g (q j) d -> (n g q) (j d)", q=16)
                for bg in range(BG):
                    pool.indirect_dma_start(
                        out=dst[:, bg, :], out_offset=None, in_=src,
                        in_offset=bass.IndirectOffsetOnAxis(ap=row_idx[:, bg:bg + 1], axis=0)).then_inc(s, 16)

            pool.wait_ge(mo_done, 2 * len(front.tiles))
            gather_pages(key_rows, "cache_slc_k", key_in[0])

            def gather(name, idx, k):
                pool.indirect_dma_start(
                    out=ring[:, k, :], out_offset=None, in_=a[name][0],
                    in_offset=bass.IndirectOffsetOnAxis(ap=idx, axis=0)).then_inc(row_in[k], 16)

            def gather_turn(name, t, slot, turn, x, heads_known):
                pool.wait_ge(row_free[0], turn)
                pool.tensor_copy(cursor[:, x, :], expert[:, t, bass.ds(slot, RING)]).then_inc(cursor_ready, 1)
                for k in range(RING):
                    pool.wait_ge(routed, heads_known)
                    if k:
                        pool.wait_ge(row_free[k], turn)
                    else:
                        pool.wait_ge(cursor_ready, turn)
                    gather(name, cursor[:, x, k:k + 1], k)

            pool.wait_ge(routed, 1)
            for k in range(RING):
                gather("peer_u", expert[:, 0, k:k + 1], k)
            gather_turn("peer_u", 0, RING, 1, 1, 1)
            for begin, end in ((1, VALUES_AT), (VALUES_AT, H)):
                with pool.Fori(begin, end) as i:
                    pool.wait_ge(routed, i + 1)
                    for x in range(2):
                        gather_turn("peer_u", 0, i * TOPK + x * RING, i * 2 + x, x, 1)
                if begin == 1:
                    pool.wait_ge(s_sc_done, 2)
                    gather_pages(val_rows, "cache_slc_v", val_in[0])
            for t in range(PT):
                for table, name in enumerate(("peer_u", "peer_v")):
                    if t == 0 and table == 0:
                        continue
                    turn0 = (ROWS * t + SLOTS * table) // RING
                    pool.wait_ge(routed, H * (t + 1))
                    with pool.Fori(0, TURNS // 2) as i:
                        for x in range(2):
                            gather_turn(name, t, i * TOPK + x * RING, i * 2 + (turn0 + x), x, H * (t + 1))
            pool.wait_ge(routed, H * NT + 1)
            for x, name in enumerate(("peer_u", "peer_v")):
                for b in range(DB):
                    pool.wait_ge(row_free[b], ROWS * PT // RING + x)
                    gather(name, expert_s[:, b:b + 1], b)

        @block.tensor
        def _(pe):
            freed = {}
            norms = [0]

            def claim(b):
                if b in freed:
                    pe.wait_ge(*freed.pop(b))
                return banks[b]

            def transpose_rows(src, R):
                n = norms[0]
                norms[0] += 1
                pe.wait_ge(hn_ready, n + 1)
                for half in range(2):
                    bank = claim(half)
                    for q in range(4):
                        k = 4 * half + q
                        ins = pe.transpose(bank[:, q * P:q * P + R], src[0:R, k * P:(k + 1) * P], ident[0:R, 0:R])
                    ins.then_inc(hnT_done, 1)
                    freed[half] = (hnT_ready, 2 * n + half + 1)

            pe.wait_ge(consts_in, 16 * (3 + len(const_loads)))
            for t in range(NT):
                transpose_rows(hn_buf[:, t % 2, :], rows_of(t))
            n = 0
            for i, (c0, w) in enumerate(CHUNKS):
                pe.wait_ge(w_in_loaded[i % 2], 16 * (i // 2 + 1))
                for t in range(NT):
                    if i == 0:
                        pe.wait_ge(hnT_ready, 2 * (t + 1))
                    R = rows_of(t)
                    b = 2 + n % 4
                    bank = claim(b)
                    for k in range(KC):
                        ins = pe.matmul(bank[0:R, 0:w], hnT[:, k, t * P:t * P + R], w_buf[:, i % 2, k, 0:w],
                                        start=(k == 0), stop=(k == KC - 1))
                    ins.then_inc(proj_done, 1)
                    n += 1
                    freed[b] = (proj_ready, n)

            def cmp_products(unit, m):
                kind, x = divmod(unit, 3)
                R = P if x < 2 else BG
                pe.wait_ge(blkT_ready, 8 * unit + m + 1)
                acc_bank = banks[4 + unit % 2]
                for q in range(4):
                    j = 4 * m + q
                    rows, w = blkT[:, m % 2, q, 0:R], cmp_w[:, kind, j, :]
                    if kind == 0:
                        ins = pe.matmul(acc_bank[0:HD, 0:R], w, rows, start=(j == 0), stop=(j == 31))
                    else:
                        ins = pe.matmul(acc_bank[0:R, 0:HD], rows, w, start=(j == 0), stop=(j == 31))
                if m == 7:
                    ins.then_inc(cmp_done, 1)
                    freed[4 + unit % 2] = (cmp_ready, unit + 1)

            for unit in range(6):
                R = P if unit % 3 < 2 else BG
                if unit % 3 == 2:
                    pe.wait_ge(own_blk_in, 16 * (unit // 3 + 1))
                else:
                    pe.wait_ge(blk_in[unit % 2], 16 * (1 + (unit >= 3)))
                if unit == 0:
                    pe.wait_ge(cmpw_in, 32)
                claim(4 + unit % 2)
                for m in range(8):
                    bank = claim(m % 2)
                    for q in range(4):
                        j = 4 * m + q
                        ins = pe.transpose(bank[:, q * P:q * P + R], blk_buf[0:R, unit % 2, j * P:(j + 1) * P],
                                           ident[0:R, 0:R])
                    ins.then_inc(blkT_done, 1)
                    freed[m % 2] = (blkT_ready, 8 * unit + m + 1)
                    if m:
                        cmp_products(unit, m - 1)
                cmp_products(unit, 7)

            def att_scores(t, u):
                kind, hh = divmod(u % 16, H)
                b, N = SCORE_BANKS[u % 3], P * (t + 1)
                bank = claim(b)
                pe.matmul(bank[:, 0:N], nqT[0:HD, hh, :], kT[0:HD, kind, hh // R4, 0:N], start=True, stop=False)
                pe.matmul(bank[:, N - P:N], ident, tri, start=False, stop=True).then_inc(sc_done, 1)
                freed[b] = (exp_ready, u + 1)

            def att_probsT(t, u):
                b = 3 + u % 2
                bank = claim(b)
                pe.wait_ge(exp_ready, u + 1)
                for j in range(t + 1):
                    ins = pe.transpose(bank[:, j * P:(j + 1) * P], probs[:, u % 3, j * P:(j + 1) * P], ident)
                ins.then_inc(pT_done, 1)
                freed[b] = (pT_ready, u + 1)

            def att_values(t, u):
                kind, hh = divmod(u % 16, H)
                b = 5 + kind
                if hh == 0:
                    claim(b)
                c0 = (C_SV, C_WV)[kind] + hh // R4 * HD
                pe.wait_ge(pT_ready, u + 1)
                for j in range(t + 1):
                    ins = pe.matmul(banks[b][:, hh * HD:(hh + 1) * HD], probsT[:, u % 2, j * P:(j + 1) * P],
                                    proj[j][:, c0:c0 + HD], start=(j == 0), stop=(j == t))
                if hh == H - 1:
                    ins.then_inc(ao_done, 1)
                    freed[b] = (ao_used, 2 * t + kind + 1)

            for t in range(PT):
                pe.wait_ge(rotated, t + 1)
                heads = [C_RQ + HD * x for x in range(H)] + [C_RK + HD * x for x in range(H)] + \
                        [C_NQ + HD * x for x in range(H)] + [C_SK, C_SK + HD, C_WK, C_WK + HD]
                for m in range(7):
                    bank = claim(m % 2)
                    for q in range(4):
                        c0 = heads[4 * m + q]
                        ins = pe.transpose(bank[0:HD, q * P:(q + 1) * P], proj[t][:, c0:c0 + HD], ident)
                    ins.then_inc(headT_done, 1)
                    freed[m % 2] = (headT_ready, 7 * t + m + 1)
                pe.wait_ge(headT_ready, 7 * t + 4)
                for m in range(2):
                    bank = claim(2 + m)
                    for q in range(4):
                        ins = pe.matmul(bank[:, q * P:(q + 1) * P], rkT[0:HD, 4 * m + q, :], rqT[0:HD, 4 * m + q, :],
                                        start=True, stop=True)
                    ins.then_inc(att_done, 1)
                    freed[2 + m] = (att_ready, 2 * t + m + 1)
                if t == 0:
                    pe.wait_ge(cmp_ready, 6)
                pe.wait_ge(headT_ready, 7 * t + 6)
                bank = claim(7)
                for hh in range(H):
                    keys = c_kT[0:HD, 256:272].rearrange("p (n g k) -> p n g k", g=G, k=2)[:, :, hh // R4, :]
                    ins = pe.matmul(bank[:, hh * 8:(hh + 1) * 8], nqT[0:HD, hh, :], keys, start=True, stop=True)
                ins.then_inc(cs_done, 1)
                freed[7] = (cs_ready, t + 1)
                for b in (4, 5, 6):
                    claim(b)
                if t:
                    pe.wait_ge(state_ready, t)
                    for hh in range(H):
                        pe.matmul(banks[4][:, hh * HD:(hh + 1) * HD], rqT[0:HD, hh, :], state[0:HD, hh, :],
                                  start=True, stop=True)
                pe.wait_ge(vz_ready, t + 1)
                for hh in range(H):
                    pe.matmul(banks[6][0:HD, hh * HD:(hh + 1) * HD], proj[t][:, C_RK + hh * HD:C_RK + (hh + 1) * HD],
                              vz[:, hh, :], start=True, stop=True)
                pe.wait_ge(att_ready, 2 * t + 2)
                for hh in range(H):
                    ins = pe.matmul(banks[5][:, hh * HD:(hh + 1) * HD], att[:, hh, :],
                                    proj[t][:, C_RV + hh * HD:C_RV + (hh + 1) * HD], start=True, stop=True)
                ins.then_inc(ret_done, 1)
                for b in (4, 5, 6):
                    freed[b] = (state_ready, t + 1)
                bank = claim(7)
                pe.wait_ge(cp_ready, t + 1)
                pe.transpose(bank[0:64, 0:P], cp_buf, ident).then_inc(cpT_done, 1)
                freed[7] = (cpT_ready, t + 1)
                bank = claim(2)
                if t == 0:
                    pe.wait_ge(vblk_in, 16 * H)
                pe.wait_ge(cpT_ready, t + 1)
                pe.matmul(bank[:, 0:512], cpT[0:64, :], c_vblk[0:64, :], start=True, stop=True).then_inc(co_done, 1)
                freed[2] = (co_used, t + 1)
                pe.wait_ge(headT_ready, 7 * t + 7)
                u0 = 2 * H * t
                att_scores(t, u0)
                att_scores(t, u0 + 1)
                for u in range(u0, u0 + 2 * H):
                    if u + 2 < u0 + 2 * H:
                        att_scores(t, u + 2)
                    att_probsT(t, u)
                    if u > u0:
                        att_values(t, u - 1)
                att_values(t, u)

            def output_projection(grp, nth):
                for t in grp.tiles:
                    R = rows_of(t)
                    if t == SAMPLE:
                        pe.wait_ge(s_cat_in, 16)
                    for half in range(2):
                        bank = claim(half)
                        for q in range(4):
                            k = 4 * half + q
                            ins = pe.transpose(bank[:, q * P:q * P + R], cat[0:R, t, k * P:(k + 1) * P], ident[0:R, 0:R])
                        ins.then_inc(catT_done, 1)
                        freed[half] = (catT_ready, 2 * t + half + 1)
                    pe.wait_ge(w_out_in, 16 * nth)
                    pe.wait_ge(catT_ready, 2 * t + 2)
                    for half in range(2):
                        n = 2 * t + half
                        b = 2 + n % 4
                        bank = claim(b)
                        for k in range(KC):
                            ins = pe.matmul(bank[0:R, :], grp.catT[t][:, k, 0:R],
                                            grp.w_out[:, k, half * 512:(half + 1) * 512],
                                            start=(k == 0), stop=(k == KC - 1))
                        ins.then_inc(out_done, 1)
                        freed[b] = (out_added, n + 1)

            def memory_queries(grp, nth):
                for t in grp.tiles:
                    transpose_rows(hn3[:, t, :], rows_of(t))
                pe.wait_ge(mq_in, 16 * nth)
                pe.wait_ge(hnT_ready, 2 * norms[0])
                for hh in range(HM):
                    n = HM * (nth - 1) + hh
                    b = 2 + n % 4
                    bank = claim(b)
                    for k in range(KC):
                        ins = pe.matmul(bank[:, 0:grp.width], grp.w_mq[:, k, hh * P:(hh + 1) * P], grp.hnT[:, k, :],
                                        start=(k == 0), stop=(k == KC - 1))
                    ins.then_inc(qm_done, 1)
                    freed[b] = (qm_ready, n + 1)
                pe.wait_ge(qm_ready, HM * nth)

            def mem_scores(grp, v):
                t, hh = divmod(v, HM)
                at = grp.at[t]
                bank = claim(v % 2)
                pe.matmul(bank[:, 0:NMEM], grp.qT_m[:, hh, at:at + P], mkT[:, hh, :],
                          start=True, stop=True).then_inc(m_sc_done, 1)
                freed[v % 2] = (m_exp, v + 1)

            def memory_unit(grp, v, last):
                hh = v % HM
                if not last:
                    mem_scores(grp, v + 1)
                b = 2 + v % 2
                bank = claim(b)
                pe.wait_ge(m_norm, v + 1)
                for x in range(2):
                    ins = pe.transpose(bank[:, x * P:(x + 1) * P], grp.m_probs[:, v % 2, x * P:(x + 1) * P], ident)
                ins.then_inc(m_pT_done, 1)
                freed[b] = (m_pT_ready, v + 1)
                b = 4 + v % 2
                bank = claim(b)
                pe.wait_ge(m_pT_ready, v + 1)
                for x in range(2):
                    ins = pe.matmul(bank[:, 0:P], mv[:, x, hh * P:(hh + 1) * P],
                                    grp.m_probsT[:, v % 2, x * P:(x + 1) * P], start=(x == 0), stop=(x == 1))
                ins.then_inc(m_oT_done, 1)
                freed[b] = (m_oT_ready, v + 1)

            def memory_output(grp, nth):
                pe.wait_ge(mo_in, 16 * nth)
                for t in grp.tiles:
                    R, at = rows_of(t), grp.at[t]
                    for half in range(2):
                        n = 2 * t + half
                        b = 2 + n % 2
                        bank = claim(b)
                        for hh in range(HM):
                            ins = pe.matmul(bank[0:R, :], grp.oT_m[:, hh, at:at + R],
                                            w_mo[:, hh, half * 512:(half + 1) * 512],
                                            start=(hh == 0), stop=(hh == HM - 1))
                        ins.then_inc(mo_done, 1)
                        freed[b] = (mo_added, n + 1)

            def normed_rowsT(grp):
                for t in grp.tiles:
                    transpose_rows(hn3[:, t, :], rows_of(t))

            def expert_query(grp, nth, hh):
                n = H * (nth - 1) + hh
                b = 2 + n % 4
                bank = claim(b)
                if hh == 0:
                    pe.wait_ge(wq_in, 16 * (nth + 1))
                    pe.wait_ge(hnT_ready, 2 * norms[0])
                for k in range(KC):
                    ins = pe.matmul(bank[:, 0:grp.width], grp.wq[:, k, hh * P:(hh + 1) * P], grp.hnT[:, k, :],
                                    start=(k == 0), stop=(k == KC - 1))
                ins.then_inc(qp_done, 1)
                freed[b] = (qp_ready, n + 1)

            def key_scores_of(grp, t):
                R, at = rows_of(t), grp.at[t]
                for m in range(4):
                    b = 2 + m
                    bank = claim(b)
                    for x in range(2):
                        hh = 2 * m + x
                        ins = pe.matmul(bank[0:R, x * 256:(x + 1) * 256], grp.qT_p[:, hh, at:at + R], skT[:, hh, :],
                                        start=True, stop=True)
                    ins.then_inc(ps_done, 1)
                    freed[b] = (ps_ready, 4 * t + m + 1)

            pe.wait_ge(cat_ready, PT)
            output_projection(front, 1)
            for t in range(2):
                transpose_rows(hn3[:, t, :], P)
            pe.wait_ge(hnT_ready, 2 * (NT + 2))
            pe.wait_ge(memw_in, 32)
            for n in range(4):
                w, t = divmod(n, 2)
                b = (6, 7, 2, 3)[n]
                bank = claim(b)
                for k in range(KC):
                    ins = pe.matmul(bank[:, :], mT[:, k, t * P:(t + 1) * P], (w_mk, w_mv)[w][:, k, :],
                                    start=(k == 0), stop=(k == KC - 1))
                ins.then_inc(mkv_done, 1)
                freed[b] = (mkv_ready, n + 1)
            pe.wait_ge(mkv_ready, 2)
            for t in range(2):
                bank = claim(t)
                for hh in range(HM):
                    ins = pe.transpose(bank[:, hh * P:(hh + 1) * P], mk[:, t, hh * P:(hh + 1) * P], ident)
                ins.then_inc(mkT_done, 1)
                freed[t] = (mkT_ready, t + 1)
            pe.wait_ge(sub_in, 16)
            for half in range(2):
                bank = claim(4 + half)
                for q in range(4):
                    ins = pe.transpose(bank[:, q * P:(q + 1) * P], sub_k[:, 4 * half + q, :], ident)
                ins.then_inc(subT_done, 1)
                freed[4 + half] = (subT_ready, half + 1)
            memory_queries(front, 1)
            pe.wait_ge(mkT_ready, 2)
            mem_scores(front, 0)
            units = HM * len(front.tiles)
            for v in range(units):
                memory_unit(front, v, v == units - 1)
            pe.wait_ge(m_oT_ready, units)
            memory_output(front, 1)
            normed_rowsT(front)
            for hh in range(H):
                expert_query(front, 1, hh)
            pe.wait_ge(qp_ready, H)
            pe.wait_ge(subT_ready, 2)
            for t in front.tiles:
                key_scores_of(front, t)

            def background():
                yield 1
                pe.wait_ge(s_rows_in, 16 * N_SROWS)
                bank = claim(0)
                pe.transpose(bank[0:64, 0:64], s_rows[0:64, S_NQ, :], ident[0:64, 0:64]).then_inc(sT_done, 1)
                freed[0] = (sT_ready, 1)
                pe.wait_ge(sT_ready, 1)
                bank = claim(1)
                pe.matmul(bank[0:64, 0:256], sqT[0:64, :], c_kT[0:HD, 0:256], start=True, stop=True).then_inc(s_sc_done, 1)
                freed[1] = (s_max, 1)
                yield 4
                pe.wait_ge(s_imp, 1)
                bank = claim(2)
                for x in range(2):
                    ins = pe.transpose(bank[:, x * 64:(x + 1) * 64], cmp_p[0:64, x * P:(x + 1) * P], ident[0:64, 0:64])
                ins.then_inc(s_pT_done, 1)
                freed[2] = (s_pT_ready, 1)
                pe.wait_ge(s_pT_ready, 1)
                bank = claim(3)
                pe.matmul(bank[0:64, 64:80], group[0:64, :], s_small[0:64, 32:48], start=True, stop=True)
                for x in range(2):
                    ins = pe.matmul(bank[0:64, 0:64], cmp_pT[:, x, :], c_v[:, x, :], start=(x == 0), stop=(x == 1))
                ins.then_inc(s_o_done, 1)
                freed[3] = (s_branch, 1)
                yield 5
                pe.wait_ge(qmask_ready, 1)
                gi = 0
                for kind, nj in enumerate((8, 4)):
                    nc_ = nj // 4
                    keys, vals = ((key_rows, val_rows), (win_keys, win_vals))[kind]
                    pe.wait_ge(key_in[kind], (16 * BG, 16)[kind])
                    for cc in range(nc_):
                        claim(4 + cc)

                    def key_scores(i, gi):
                        bg, cc = divmod(i, nc_)
                        pe.wait_ge(s_keyT_ready, gi + 1)
                        ins = pe.matmul(banks[4 + cc][0:64, :], q_mask[0:HD, bg, :], keyT[0:HD, gi % 2, :],
                                        start=(bg == 0), stop=(bg == BG - 1))
                        return ins

                    for i in range(BG * nc_):
                        bg, cc = divmod(i, nc_)
                        if i and i % 4 == 0:
                            yield 5 + 3 * kind + i / (BG * nc_)
                        bank = claim(gi % 2)
                        for q in range(4):
                            j = 4 * cc + q
                            ins = pe.transpose(bank[0:HD, q * P:(q + 1) * P], keys[:, bg, j * HD:(j + 1) * HD], ident)
                        ins.then_inc(s_keyT_done, 1)
                        freed[gi % 2] = (s_keyT_ready, gi + 1)
                        if i:
                            key_scores(i - 1, gi - 1)
                        gi += 1
                    key_scores(BG * nc_ - 1, gi - 1).then_inc(s_sc_done, 1)
                    yield 6 + 3 * kind
                    for cc in range(nc_):
                        freed[4 + cc] = (s_max, 2 + kind)
                    bank = claim(2)
                    pe.wait_ge(s_exp, 2 + kind)
                    for j in range(nj):
                        ins = pe.transpose(bank[:, j * 64:(j + 1) * 64], s_probs[0:64, j * P:(j + 1) * P],
                                           ident[0:64, 0:64])
                    ins.then_inc(s_pT_done, 1)
                    freed[2] = (s_pT_ready, 2 + kind)
                    yield 7 + 3 * kind
                    pe.wait_ge(val_in[kind], (16 * BG, 16)[kind])
                    pe.wait_ge(s_pT_ready, 2 + kind)
                    bank = claim(5)
                    for bg in range(BG):
                        for j in range(nj):
                            ins = pe.matmul(bank[0:HD, bg * R4:(bg + 1) * R4], vals[:, bg, j * HD:(j + 1) * HD],
                                            s_probsT[:, j, bg * R4:(bg + 1) * R4], start=(j == 0), stop=(j == nj - 1))
                    ins.then_inc(s_oT_done, 1)
                    freed[5] = (s_oT_ready, 1 + kind)
                    pe.wait_ge(s_oT_ready, 1 + kind)
                    bank = claim(3)
                    pe.transpose(bank[0:64, 0:64], s_o[0:HD, 0, :], ident[0:64, 0:64]).then_inc(s_o_done, 1)
                    freed[3] = (s_branch, 2 + kind)
                    yield 8 + 3 * kind

                yield 15
                output_projection(back, 2)
                yield 18
                memory_queries(back, 2)
                v0 = HM * back.tiles[0]
                mem_scores(back, v0)
                for v in range(v0, v0 + HM):
                    yield 20 + v - v0
                    memory_unit(back, v, v == v0 + HM - 1)
                yield 24
                V = PT * HM
                pe.wait_ge(qmask_ready, 2)
                claim(2)

                def mem_key_scores(g):
                    b, pair = divmod(g, 2)
                    pe.wait_ge(m_keyT_ready, g + 1)
                    for x in range(2):
                        cc = (2 * pair + x) * DB + b
                        ins = pe.matmul(banks[2][0:32, 0:NMEM], qm_mask[:, cc, :], mkT_s[:, g % 2, x * NMEM:(x + 1) * NMEM],
                                        start=(g == 0 and x == 0), stop=(g == 2 * DB - 1 and x == 1))
                    return ins

                for g in range(2 * DB):
                    b, pair = divmod(g, 2)
                    if g:
                        yield 24 + g / (2 * DB)
                    if g % DB == 0:
                        pe.wait_ge(memkv_in, 16 * (g // DB + 1))
                    bank = claim(g % 2)
                    for x in range(2):
                        for m in range(2):
                            c0 = m * 512 + (2 * pair + x) * P
                            ins = pe.transpose(bank[:, x * NMEM + m * P:x * NMEM + (m + 1) * P],
                                               mem_piece[:, b % 4, c0:c0 + P], ident)
                    ins.then_inc(m_keyT_done, 1)
                    freed[g % 2] = (m_keyT_ready, g + 1)
                    if g:
                        mem_key_scores(g - 1)
                mem_key_scores(2 * DB - 1).then_inc(m_sc_done, 1)
                freed[2] = (m_exp, V + 1)
                yield 27
                bank = claim(3)
                pe.wait_ge(m_norm, V + 1)
                for m in range(2):
                    ins = pe.transpose(bank[:, m * 32:(m + 1) * 32], ms_probs[0:32, m * P:(m + 1) * P], ident[0:32, 0:32])
                ins.then_inc(m_pT_done, 1)
                freed[3] = (m_pT_ready, V + 1)
                bank = claim(4)
                pe.wait_ge(m_pT_ready, V + 1)
                for b in range(DB):
                    if b == 4:
                        yield 27.5
                    if b % 4 == 0:
                        pe.wait_ge(memkv_in, 16 * (3 + b // 4))
                    for hh in range(HM):
                        cc = hh * DB + b
                        for m in range(2):
                            c0 = m * 512 + hh * P
                            ins = pe.matmul(bank[:, cc:cc + 1], mem_piece[:, b % 4, c0:c0 + P], ms_probsT[:, m, cc:cc + 1],
                                            start=(m == 0), stop=(m == 1))
                    if b % 4 == 3:
                        ins.then_inc(m_oT_done, 1)
                freed[4] = (m_oT_ready, V + 1)
                yield 27.9
                pe.wait_ge(m_oT_ready, V + 1)
                memory_output(back, 2)
                yield 30
                normed_rowsT(back)
                for hh in range(H):
                    yield 30 + (hh + 1) / 10
                    expert_query(back, 2, hh)
                yield 31
                pe.wait_ge(qp_ready, 2 * H)
                key_scores_of(back, 3)
                yield STEPS_DONE

            def v_rows(t, turn):
                first = V_TURN[t]
                for j, k in enumerate(PE_SLOTS):
                    pe.wait_ge(row_in[k], 16 * (turn + 1))
                    pe.wait_ge(diag_ready, (TURNS * t + turn - first) * len(PE_SLOTS) + j + 1)
                    for half in range(2):
                        ins = pe.matmul(banks[6 + half][:, :], diag[:, j, :], ring[:, k, half * 512:(half + 1) * 512],
                                        start=(turn == first and j == 0),
                                        stop=(turn == first + TURNS - 1 and j == len(PE_SLOTS) - 1))
                    ins.then_inc(row_free[k], 1)

            def v_banks(t):
                for half in range(2):
                    claim(6 + half)
                if t:
                    pe.wait_ge(sum_added, 2 * t)

            steps = background()
            for t in range(PT):
                advance(steps, progress(V_TURN[t] - 1))
                if t == 2:
                    key_scores_of(back, SAMPLE)
                v_banks(t)
                for turn in range(V_TURN[t], V_TURN[t] + TURNS):
                    v_rows(t, turn)
                    advance(steps, progress(turn))

            bank = claim(0)
            pe.wait_ge(gates_ready, 1)
            pe.transpose(bank[:, 0:DB], expert_f[0:DB, :], ident[0:DB, 0:DB])
            pe.transpose(bank[:, DB:2 * DB], gate_t[0:DB, :], ident[0:DB, 0:DB]).then_inc(rt_done, 1)

            pe.wait_ge(sum_added, 2 * PT)
            pe.wait_ge(coef_ready, PT + 1)
            for b in range(DB):
                pe.wait_ge(row_in[b], 16 * (ROWS * PT // RING + 2))
                for half in range(2):
                    ins = pe.matmul(banks[6 + half][0:DB, :], coef_m[:, b, :], ring[:, b, half * 512:(half + 1) * 512],
                                    start=(b == 0), stop=(b == DB - 1))
            ins.then_inc(se_done, 1)

        @block.scalar
        def _(act):
            norms = [0]
            order = Order(act, scalar_order)

            def mean_square(x, junk, s=None, v=None):
                n = norms[0]
                norms[0] += 1
                R = x.shape[0]
                if s is not None:
                    act.wait_ge(s, v)
                act.activation(junk[0:R, :], x, ACT.Square, scale=1.0 / 32,
                               accum_out=mean_sq[0:R, n % 16:n % 16 + 1]).then_inc(mean_ready, 1)
                act.wait_ge(mean_ready, n + 1)
                act.activation(rstd[0:R, n % 16:n % 16 + 1], mean_sq[0:R, n % 16:n % 16 + 1], ACT.Sqrt,
                               bias=eps_col[0:R, :]).then_inc(std_ready, 1)

            copied = [0]

            def copy_rowsT(dst, c0, R):
                n = copied[0]
                copied[0] += 1
                for half in range(2):
                    act.wait_ge(hnT_done, 2 * n + half + 1)
                    act.activation(dst[:, 4 * half:4 * half + 4, c0:c0 + R],
                                   banks[half][:, :].rearrange("p (k r) -> p k r", k=4)[:, :, 0:R],
                                   ACT.Copy).then_inc(hnT_ready, 1)

            act.wait_ge(x_in, 16 * NT)
            act.wait_ge(eps_set, 1)
            for t in range(NT):
                mean_square(h[0:rows_of(t), t, :], sq_junk)
            for t in range(NT):
                copy_rowsT(hnT, t * P, rows_of(t))
            n = 0
            for c0, w in CHUNKS:
                for t in range(NT):
                    R = rows_of(t)
                    act.wait_ge(proj_done, n + 1)
                    act.activation(proj[t][0:R, c0:c0 + w], banks[2 + n % 4][0:R, 0:w], ACT.Copy).then_inc(proj_ready, 1)
                    n += 1
            for unit in range(6):
                R = P if unit % 3 < 2 else BG
                for m in range(8):
                    act.wait_ge(blkT_done, 8 * unit + m + 1)
                    act.activation(blkT[:, m % 2, :, 0:R], banks[m % 2][:, :].rearrange("p (k r) -> p k r", k=4)[:, :, 0:R],
                                   ACT.Copy).then_inc(blkT_ready, 1)
            for t in range(PT):
                for m in range(7):
                    act.wait_ge(headT_done, 7 * t + m + 1)
                    src = banks[m % 2][0:HD, :].rearrange("p (k r) -> p k r", k=4)
                    if m < 6:
                        dst = (rqT, rkT, nqT)[m // 2][0:HD, 4 * (m % 2):4 * (m % 2) + 4, :]
                    else:
                        dst = kT[0:HD, :, :, t * P:(t + 1) * P].rearrange("p x g r -> p (x g) r")
                    act.activation(dst, src, ACT.Copy, scale=0.125 if m in (4, 5) else 1.0).then_inc(headT_ready, 1)
                if t:
                    act.wait_ge(cat_ready, t)
                act.activation(tanh_rg, proj[t][:, C_RG:C_RG + 512], ACT.Tanh, scale=0.5).then_inc(tanh_ready, 1)
                act.activation(gate, proj[t][:, C_NG:C_NG + 3 * H], ACT.Tanh, scale=0.5).then_inc(tanh_ready, 1)
                act.wait_ge(cs_ready, t + 1)
                act.activation(cp_buf, cs_buf, ACT.Exp).then_inc(cs_exp, 1)
                act.wait_ge(cpT_done, t + 1)
                act.activation(cpT[0:64, :], banks[7][0:64, 0:P], ACT.Copy).then_inc(cpT_ready, 1)
                act.wait_ge(gn_var, t + 1)
                act.activation(gn_r[:, 0:H], gn_v[:, 0:H], ACT.Sqrt, bias=eps_col).then_inc(gn_std, 1)
                for u in range(2 * H * t, 2 * H * (t + 1)):
                    kind, hh = divmod(u % 16, H)
                    N = P * (t + 1)
                    act.wait_ge(max_ready, u + 1)
                    if u >= 3:
                        act.wait_ge(pT_done, u - 2)
                    act.activation(probs[:, u % 3, 0:N], banks[SCORE_BANKS[u % 3]][:, 0:N], ACT.Exp,
                                   bias=neg_max[:, u % 16:u % 16 + 1],
                                   accum_out=exp_sum[:, kind, hh:hh + 1]).then_inc(exp_ready, 1)
            def rows_transposed(grp):
                for t in grp.tiles:
                    R = rows_of(t)
                    for half in range(2):
                        act.wait_ge(catT_done, 2 * t + half + 1)
                        act.activation(grp.catT[t][:, 4 * half:4 * half + 4, 0:R],
                                       banks[half][:, :].rearrange("p (k r) -> p k r", k=4)[:, :, 0:R],
                                       ACT.Copy).then_inc(catT_ready, 1)

            def tile_norms(grp, s):
                for t in grp.tiles:
                    mean_square(h[0:rows_of(t), t, :], hn3[:, t, :], s, 2 * (t + 1))

            def memory_queries(grp, nth):
                for t in grp.tiles:
                    copy_rowsT(grp.hnT, grp.at[t], rows_of(t))
                for hh in range(HM):
                    n = HM * (nth - 1) + hh
                    act.wait_ge(qm_done, n + 1)
                    act.activation(grp.qT_m[:, hh, :], banks[2 + n % 4][:, 0:grp.width], ACT.Copy,
                                   scale=HDM ** -0.5).then_inc(qm_ready, 1)

            def memory_unit(grp, v):
                t, hh = divmod(v, HM)
                at = grp.at[t]
                act.wait_ge(m_max, v + 1)
                act.activation(grp.m_probs[:, v % 2, :], banks[v % 2][:, 0:NMEM], ACT.Exp,
                               bias=neg_max[:, v % 2:v % 2 + 1],
                               accum_out=exp_sum[:, 0, v % 2:v % 2 + 1]).then_inc(m_exp, 1)
                act.wait_ge(m_pT_done, v + 1)
                act.activation(grp.m_probsT[:, v % 2, :], banks[2 + v % 2][:, 0:NMEM], ACT.Copy).then_inc(m_pT_ready, 1)
                act.wait_ge(m_oT_done, v + 1)
                act.activation(grp.oT_m[:, hh, at:at + P], banks[4 + v % 2][:, 0:P], ACT.Copy).then_inc(m_oT_ready, 1)

            def normed_rowsT(grp):
                for t in grp.tiles:
                    copy_rowsT(grp.hnT, grp.at[t], rows_of(t))

            def expert_query(grp, nth, hh):
                n = H * (nth - 1) + hh
                act.wait_ge(qp_done, n + 1)
                act.activation(grp.qT_p[:, hh, :], banks[2 + n % 4][:, 0:grp.width], ACT.Copy).then_inc(qp_ready, 1)

            def key_scores_of(t):
                R = rows_of(t)
                if t > 2:
                    act.wait_ge(routed, H * (t - 1))
                dst = s_held if t == 2 else s_all[:, t % 2, :]
                for m in range(4):
                    act.wait_ge(ps_done, 4 * t + m + 1)
                    act.activation(dst[0:R, m * 512:(m + 1) * 512], banks[2 + m][0:R, :], ACT.Copy
                                   ).then_inc(ps_ready, 1)

            def expert_weights(t):
                R, n = (P, SLOTS) if t < PT else (DB, DB)
                act.wait_ge(best_shift, t + 1)
                act.activation(best_e[0:R, :], best_e[0:R, :], ACT.Exp).then_inc(best_exp, 1)
                act.wait_ge(gelu_in, t + 1)
                act.activation(gtmp[:, 0, 0:n], gtmp[:, 0, 0:n], ACT.Tanh, scale=GELU_B).then_inc(gelu_tanh, 1)

            act.wait_ge(cat_ready, PT)
            act.wait_ge(state_stored, 16)
            act.wait_ge(mem_in, 48)
            for t in range(2):
                mean_square(mem_x[:, t, :], hn3[:, t, :])
            rows_transposed(front)
            for t in range(2):
                copy_rowsT(mT, t * P, P)
            tile_norms(front, out_added)
            for n in range(4):
                act.wait_ge(mkv_done, n + 1)
                act.activation((mk, mv)[n // 2][:, n % 2, :], banks[(6, 7, 2, 3)[n]][:, :], ACT.Copy).then_inc(mkv_ready, 1)
            for t in range(2):
                act.wait_ge(mkT_done, t + 1)
                act.activation(mkT[:, :, t * P:(t + 1) * P], banks[t][:, :].rearrange("p (k r) -> p k r", k=4),
                               ACT.Copy).then_inc(mkT_ready, 1)
            act.wait_ge(sk_zero, 1)
            for half in range(2):
                act.wait_ge(subT_done, half + 1)
                src = banks[4 + half][:, :].rearrange("p (k r) -> p k r", k=4)
                act.activation(skT[0:64, 4 * half:4 * half + 4, 0:P], src[0:64], ACT.Copy)
                act.activation(skT[64:P, 4 * half:4 * half + 4, P:2 * P], src[64:P], ACT.Copy).then_inc(subT_ready, 1)
            act.wait_ge(y_stored, 16 * 6)
            memory_queries(front, 1)
            for v in range(HM * len(front.tiles)):
                memory_unit(front, v)
            tile_norms(front, mo_added)
            normed_rowsT(front)
            for hh in range(H):
                expert_query(front, 1, hh)
            for t in front.tiles:
                key_scores_of(t)

            def background():
                yield 1
                act.wait_ge(s_rows_in, 16 * N_SROWS)
                act.activation(s_rows[0:64, S_T, :], s_rows[0:64, S_RG, :], ACT.Tanh, scale=0.5).then_inc(tanh_ready, 1)
                act.activation(gate[0:64, 0:3], col[0:64, 0:3], ACT.Tanh, scale=0.5).then_inc(tanh_ready, 1)
                act.wait_ge(sT_done, 1)
                act.activation(sqT[0:64, :], banks[0][0:64, 0:64], ACT.Copy, scale=0.125).then_inc(sT_ready, 1)
                yield 3
                act.wait_ge(s_max, 1)
                act.activation(cmp_p[0:64, :], s_scores[0:64, 0:256], ACT.Exp, bias=neg_max[0:64, 0:1],
                               accum_out=exp_sum[0:64, 0, 0:1]).then_inc(s_exp, 1)
                yield 4
                act.wait_ge(s_pT_done, 1)
                act.activation(cmp_pT, banks[2][:, 0:128].rearrange("p (x r) -> p x r", x=2), ACT.Copy).then_inc(s_pT_ready, 1)
                yield 5
                gi = 0
                for kind, nj in enumerate((8, 4)):
                    for i in range(BG * nj // 4):
                        if i and i % 4 == 0:
                            yield 5 + 3 * kind + i / (BG * nj // 4)
                        act.wait_ge(s_keyT_done, gi + 1)
                        act.activation(keyT[0:HD, gi % 2, :], banks[gi % 2][0:HD, :], ACT.Copy).then_inc(s_keyT_ready, 1)
                        gi += 1
                    yield 6 + 3 * kind
                    act.wait_ge(s_max, 2 + kind)
                    N = nj * P + 1
                    act.activation(s_probs[0:64, 0:N], s_scores[0:64, 0:N], ACT.Exp, bias=neg_max[0:64, 1 + kind:2 + kind],
                                   accum_out=exp_sum[0:64, 0, 1 + kind:2 + kind]).then_inc(s_exp, 1)
                    act.wait_ge(s_pT_done, 2 + kind)
                    act.activation(s_probsT[:, 0:nj, :], banks[2][:, 0:nj * 64].rearrange("p (x r) -> p x r", x=nj),
                                   ACT.Copy).then_inc(s_pT_ready, 1)
                    yield 7 + 3 * kind
                    act.wait_ge(s_oT_done, 1 + kind)
                    act.activation(s_o[0:HD, 0, :], banks[5][0:HD, 0:64], ACT.Copy).then_inc(s_oT_ready, 1)
                    yield 8 + 3 * kind
                yield 14
                act.wait_ge(gn_var, PT + 1)
                act.activation(gn_r[0:64, 0:1], gn_v[0:64, 0:1], ACT.Sqrt, bias=eps_col[0:64, :]).then_inc(gn_std, 1)
                yield 15
                rows_transposed(back)
                yield 16
                tile_norms(back, out_added)
                yield 18
                memory_queries(back, 2)
                v0 = HM * back.tiles[0]
                for v in range(v0, v0 + HM):
                    yield 20 + v - v0
                    memory_unit(back, v)
                v = PT * HM
                yield 24
                for g in range(2 * DB):
                    if g:
                        yield 24 + g / (2 * DB)
                    act.wait_ge(m_keyT_done, g + 1)
                    act.activation(mkT_s[:, g % 2, :], banks[g % 2][:, :], ACT.Copy).then_inc(m_keyT_ready, 1)
                yield 25
                act.wait_ge(m_max, v + 1)
                act.activation(ms_probs[0:32, :], banks[2][0:32, 0:NMEM], ACT.Exp, bias=neg_max[0:32, 0:1],
                               accum_out=exp_sum[0:32, 0, 0:1]).then_inc(m_exp, 1)
                yield 27
                act.wait_ge(m_pT_done, v + 1)
                act.activation(ms_probsT, banks[3][:, 0:64].rearrange("p (x r) -> p x r", x=2), ACT.Copy
                               ).then_inc(m_pT_ready, 1)
                yield 27.9
                act.wait_ge(m_oT_done, v + 2)
                act.activation(back.oT_m[:, :, P:P + DB], banks[4][:, 0:32].rearrange("p (k r) -> p k r", k=HM), ACT.Copy
                               ).then_inc(m_oT_ready, 1)
                yield 28
                tile_norms(back, mo_added)
                yield 30
                normed_rowsT(back)
                for hh in range(H):
                    yield 30 + (hh + 1) / 10
                    expert_query(back, 2, hh)
                yield 31
                key_scores_of(3)
                yield STEPS_DONE

            def v_weights(t, turn):
                for j, k in enumerate(PE_SLOTS):
                    slot = (turn - V_TURN[t]) * RING + k
                    act.wait_ge(row_free[k], turn)
                    act.activation(diag[:, j, :], ident, ACT.Copy, scale=coef[:, slot:slot + 1]).then_inc(diag_ready, 1)

            steps = background()
            for t in range(PT):
                advance(steps, progress(V_TURN[t] - 1))
                expert_weights(t)
                if t == 0:
                    act.wait_ge(routed, H)
                    act.activation(s_all[:, 0, :], s_held, ACT.Copy).then_inc(scores_moved, 1)
                if t == 2:
                    key_scores_of(SAMPLE)
                act.wait_ge(coef_ready, t + 1)
                for turn in range(V_TURN[t], V_TURN[t] + TURNS):
                    v_weights(t, turn)
                    advance(steps, progress(turn))
                if t:
                    mean_square(h[:, t - 1, :], hn3[:, t - 1, :], sum_added, 2 * t)
            expert_weights(SAMPLE)
            mean_square(h[:, PT - 1, :], hn3[:, PT - 1, :], sum_added, 2 * PT)
            mean_square(h[0:DB, SAMPLE, :], hn3[:, SAMPLE, :], x_done, 1)

        @block.vector
        def _(dve):
            order = Order(dve, vector_order)
            norms = [0]
            tt, ts, stt, red = dve.tensor_tensor, dve.tensor_scalar, dve.scalar_tensor_tensor, dve.tensor_reduce

            def normed(dst, x, g, s=None, v=None):
                n = norms[0]
                norms[0] += 1
                R = x.shape[0]
                r = rstd[0:R, n % 16:n % 16 + 1]
                dve.wait_ge(std_ready, n + 1)
                order(dve.reciprocal(r, r))
                if s is not None:
                    dve.wait_ge(s, v)
                return stt(out=dst[0:R, :], in0=x, scalar=r, in1=g[0:R, :], op0=ALU.mult, op1=ALU.mult)

            dve.wait_ge(consts_in, 16 * (3 + len(const_loads)))
            dve.memset(eps_col, EPS).then_inc(eps_set, 1)
            for t in range(NT):
                args = (hnT_done, 2 * (t - 1)) if t >= 2 else ()
                normed(hn_buf[:, t % 2, :], h[0:rows_of(t), t, :], gain[:, MIX, :], *args).then_inc(hn_ready, 1)
            order(dve.tensor_copy(page_f, page_i[:, :]))
            ts(blk_idx[:, :], page_f[:, 0:2], 4.0, row_add[:, 0:1], ALU.mult, ALU.add).then_inc(idx_ready, 1)
            for g in range(G):
                ins = ts(row_idx[:, g:BG:G], page_f[:, 2:10], 32.0, row_add[:, 1 + g:2 + g], ALU.mult, ALU.add)
            ins.then_inc(idx_ready, 1)

            def rotate(x1, x2, cos, sin, t4):
                tt(t4[0], x1, cos, ALU.mult)
                tt(t4[1], x2, sin, ALU.mult)
                tt(t4[2], x1, sin, ALU.mult)
                order(tt(t4[3], x2, cos, ALU.mult))
                tt(x1, t4[0], t4[1], ALU.subtract)
                return tt(x2, t4[2], t4[3], ALU.add)

            dve.wait_ge(proj_ready, NT * len(CHUNKS))
            for t in range(NT):
                R = rows_of(t)
                x = proj[t][0:R, 0:1024].rearrange("p (s h d) -> p s h d", s=2, h=H)
                tab = [rot_ret[0:R, t, i].unsqueeze(2).broadcast_to((R, 2, H, 32)) for i in range(2)]
                tv = [rot_t[0:R, i, :].rearrange("p (s h d) -> p s h d", s=2, h=H) for i in range(4)]
                order(rotate(x[:, :, :, 0:32], x[:, :, :, 32:64], tab[0], tab[1], tv))
                x = proj[t][0:R, C_NQ:C_NQ + 512].rearrange("p (h d) -> p h d", h=H)
                tab = [rot_nsa[0:R, t, i].unsqueeze(1).broadcast_to((R, H, 8)) for i in range(2)]
                tv = [rot_t[0:R, i, 0:64].rearrange("p (h d) -> p h d", h=H) for i in range(4)]
                order(rotate(x[:, :, 0:8], x[:, :, 8:16], tab[0], tab[1], tv))
                x = proj[t][0:R, C_CK:C_CK + 768].rearrange("p (y z g d) -> p y z g d", y=3, z=2, g=G)[:, :, 0]
                tab = [rot_nsa[0:R, t, i].unsqueeze(1).unsqueeze(1).broadcast_to((R, 3, G, 8)) for i in range(2)]
                tv = [rot_t[0:R, i, 0:48].rearrange("p (y g d) -> p y g d", y=3, g=G) for i in range(4)]
                rotate(x[:, :, :, 0:8], x[:, :, :, 8:16], tab[0], tab[1], tv).then_inc(rotated, 1)
                dve.wait_ge(rotated, t + 1)

            dve.memset(c_vblk[0:64, :], 0.0).then_inc(vblk_zero, 1)
            for unit in range(6):
                dve.wait_ge(cmp_done, unit + 1)
                bank = banks[4 + unit % 2]
                x = unit % 3
                if unit < 3:
                    R = P if x < 2 else BG
                    ins = ts(c_kT[0:HD, x * P:x * P + R], bank[0:HD, 0:R], cmp_bk[0:HD, :], None, ALU.add)
                elif x < 2:
                    ins = tt(c_v[:, x, :], bank[:, 0:HD], cmp_bv, ALU.add)
                else:
                    ins = tt(cv_out[0:BG, :], bank[0:BG, 0:HD], cmp_bv[0:BG, :], ALU.add)
                ins.then_inc(cmp_ready, 1)

            def wide(v, R, n=H, m=HD):
                return v.unsqueeze(2).broadcast_to((R, n, m))

            def heads(v, n=H):
                return v.rearrange("p (h d) -> p h d", h=n)

            def group_norm(o, sq, mean, R, n, t):
                order(red(mean, o, AX.X, ALU.add))
                order(ts(mean, mean, 1.0 / HD, None, ALU.mult))
                order(tt(o, o, wide(mean, R, n), ALU.subtract))
                order(tt(sq, o, o, ALU.mult))
                order(red(gn_v[0:R, 0:n], sq, AX.X, ALU.add))
                ts(gn_v[0:R, 0:n], gn_v[0:R, 0:n], 1.0 / HD, None, ALU.mult).then_inc(gn_var, 1)
                dve.wait_ge(gn_std, t + 1)
                order(dve.reciprocal(gn_r[0:R, 0:n], gn_r[0:R, 0:n]))
                order(tt(o, o, wide(gn_r[0:R, 0:n], R, n), ALU.mult))

            def branch_max(t, u):
                N = P * (t + 1)
                dve.wait_ge(sc_done, u + 1)
                red(neg_max[:, u % 16:u % 16 + 1], banks[SCORE_BANKS[u % 3]][:, 0:N], AX.X, ALU.max, negate=True
                    ).then_inc(max_ready, 1)

            for t in range(PT):
                o, sq, x3, x4 = (heads(tmp[:, i, :]) for i in range(4))
                if t:
                    dve.wait_ge(ret_done, t)
                tt(vz, heads(proj[t][:, C_RV:C_RV + 512]), wide(zeta, P), ALU.mult).then_inc(vz_ready, 1)
                for m in range(2):
                    dve.wait_ge(att_done, 2 * t + m + 1)
                    tt(att[:, 4 * m:4 * m + 4, :], banks[2 + m][:, :].rearrange("p (k r) -> p k r", k=4),
                       decay[:, 4 * m:4 * m + 4, :], ALU.mult).then_inc(att_ready, 1)
                dve.wait_ge(cs_done, t + 1)
                cs3, cp3 = heads(cs_buf), heads(cp_buf)
                vis = cmp_vis[:, t, :].unsqueeze(1).broadcast_to((P, H, 8))
                neg = cmp_neg[:, t, :].unsqueeze(1).broadcast_to((P, H, 8))
                order(tt(cs3, heads(banks[7][:, 0:64]), neg, ALU.add))
                order(red(col[:, 0:8], cs3, AX.X, ALU.max))
                tt(cs3, cs3, wide(col[:, 0:8], P, H, 8), ALU.subtract).then_inc(cs_ready, 1)
                dve.wait_ge(cs_exp, t + 1)
                order(tt(cp3, cp3, vis, ALU.mult))
                order(red(col[:, 8:16], cp3, AX.X, ALU.add))
                order(ts(col[:, 8:16], col[:, 8:16], 1e-30, None, ALU.max))
                order(dve.reciprocal(col[:, 16:24], col[:, 8:16]))
                tt(cp3, cp3, wide(col[:, 16:24], P, H, 8), ALU.mult).then_inc(cp_ready, 1)
                dve.wait_ge(ret_done, t + 1)
                if t:
                    order(tt(o, heads(banks[4][:, :]), wide(xi, P), ALU.mult))
                    order(tt(o, o, heads(banks[5][:, :]), ALU.add))
                    order(tt(state[0:HD], state[0:HD], wide(g_chunk[0:HD], HD), ALU.mult))
                    tt(state[0:HD], state[0:HD], heads(banks[6][0:HD, :]), ALU.add).then_inc(state_ready, 1)
                else:
                    order(dve.tensor_copy(o, heads(banks[5][:, :])))
                    dve.tensor_copy(state[0:HD], heads(banks[6][0:HD, :])).then_inc(state_ready, 1)
                group_norm(o, sq, col[:, 24:32], P, H, t)
                order(tt(tmp[:, 0, :], tmp[:, 0, :], gn_gain, ALU.mult))
                dve.wait_ge(tanh_ready, 2 * t + 2)
                order(stt(out=tmp[:, 1, :], in0=tanh_rg, scalar=1.0, in1=proj[t][:, C_RG:C_RG + 512],
                          op0=ALU.add, op1=ALU.mult))
                stt(out=cat[:, t, 0:512], in0=tmp[:, 0, :], scalar=0.5, in1=tmp[:, 1, :], op0=ALU.mult, op1=ALU.mult)
                order(ts(gate, gate, 0.5, 0.5, ALU.mult, ALU.add))
                gate3 = gate.rearrange("p (h x) -> p h x", x=3)
                nsa = heads(cat[:, t, 512:1024])
                dve.wait_ge(co_done, t + 1)
                tt(nsa, heads(banks[2][:, :]), wide(gate3[:, :, 0], P), ALU.mult).then_inc(co_used, 1)
                dve.wait_ge(co_used, t + 1)
                u0 = 2 * H * t
                branch_max(t, u0)
                branch_max(t, u0 + 1)

                def gated(kind):
                    dve.wait_ge(ao_done, 2 * t + kind + 1)
                    order(dve.reciprocal(gate_w, exp_sum[:, kind, :]))
                    order(tt(gate_w, gate_w, gate3[:, :, 1 + kind], ALU.mult))
                    tt(x3, heads(banks[5 + kind][:, :]), wide(gate_w, P), ALU.mult).then_inc(ao_used, 1)
                    dve.wait_ge(ao_used, 2 * t + kind + 1)
                    return tt(nsa, nsa, x3, ALU.add)

                for u in range(u0, u0 + 2 * H):
                    if u + 2 < u0 + 2 * H:
                        branch_max(t, u + 2)
                    N = P * (t + 1)
                    dve.wait_ge(pT_done, u + 1)
                    dve.tensor_copy(probsT[:, u % 2, 0:N], banks[3 + u % 2][:, 0:N]).then_inc(pT_ready, 1)
                    if u == u0 + H:
                        order(gated(0))
                gated(1).then_inc(cat_ready, 1)

            def residual(grp, s, added, bank_of):
                for t in grp.tiles:
                    R = rows_of(t)
                    for half in range(2):
                        n = 2 * t + half
                        dve.wait_ge(s, n + 1)
                        hv = h[0:R, t, half * 512:(half + 1) * 512]
                        tt(hv, hv, banks[bank_of(n)][0:R, :], ALU.add).then_inc(added, 1)

            def tile_norms(grp, g):
                for t in grp.tiles:
                    normed(hn3[:, t, :], h[0:rows_of(t), t, :], gain[:, g, :]).then_inc(hn_ready, 1)

            def mem_max(v, R=P, b=None):
                dve.wait_ge(m_sc_done, v + 1)
                red(neg_max[0:R, v % 2:v % 2 + 1], banks[v % 2 if b is None else b][0:R, 0:NMEM], AX.X, ALU.max,
                    negate=True).then_inc(m_max, 1)

            def mem_norm(v, dst):
                R = dst.shape[0]
                dve.wait_ge(m_exp, v + 1)
                order(dve.reciprocal(col[0:R, 14:15], exp_sum[0:R, 0, v % 2:v % 2 + 1]))
                ts(dst, dst, col[0:R, 14:15], None, ALU.mult).then_inc(m_norm, 1)

            out_bank, mo_bank = (lambda n: 2 + n % 4), (lambda n: 2 + n % 2)
            dve.wait_ge(mem_in, 48)
            dve.memset(skT, 0.0).then_inc(sk_zero, 1)
            for t in range(2):
                normed(hn3[:, t, :], mem_x[:, t, :], memn_gain).then_inc(hn_ready, 1)
            residual(front, out_done, out_added, out_bank)
            dve.wait_ge(hnT_done, 2 * (NT + 2))
            tile_norms(front, MEM)
            mem_max(0)
            for v in range(HM * len(front.tiles)):
                if v + 1 < HM * len(front.tiles):
                    mem_max(v + 1)
                mem_norm(v, front.m_probs[:, v % 2, :])
            residual(front, mo_done, mo_added, mo_bank)
            tile_norms(front, FFN)

            def background():
                yield 1
                row = lambda i: s_rows[0:64, i, :]
                dve.wait_ge(sT_ready, 1)
                dve.wait_ge(own_in, 16)
                tt(q_mask[0:64], own_q[0:64], sqT[0:64, :].unsqueeze(1).broadcast_to((64, BG, 64)), ALU.mult
                   ).then_inc(qmask_ready, 1)
                yield 2
                dve.wait_ge(s_sc_done, 1)
                order(tt(s_scores[0:64, 0:256], banks[1][0:64, 0:256], own_neg[0:64, :], ALU.add))
                red(neg_max[0:64, 0:1], s_scores[0:64, 0:256], AX.X, ALU.max, negate=True).then_inc(s_max, 1)
                yield 3
                dve.wait_ge(s_exp, 1)
                order(dve.reciprocal(col[0:64, 10:11], exp_sum[0:64, 0, 0:1]))
                order(ts(cmp_p[0:64, :], cmp_p[0:64, :], col[0:64, 10:11], None, ALU.mult))
                order(red(s_small[0:64, 0:32], cmp_p[0:64, :].rearrange("p (x y) -> p y x", x=8), AX.X, ALU.add))
                red(s_small[0:64, 32:48].rearrange("p (i k) -> p i k", k=2),
                    s_small[0:64, 0:32].rearrange("p (i g k) -> p i k g", g=G, k=2), AX.X, ALU.add).then_inc(s_imp, 1)
                dve.wait_ge(tanh_ready, 2 * PT + 2)
                order(ts(gate[0:64, 0:3], gate[0:64, 0:3], 0.5, 0.5, ALU.mult, ALU.add))
                yield 4
                dve.wait_ge(s_o_done, 1)
                order(ts(s_o[0:64, 3, :], banks[3][0:64, 0:64], gate[0:64, 0:1], None, ALU.mult))
                imp, eq, key = (s_small[0:64, x:x + 16] for x in (48, 64, 80))
                tt(imp, banks[3][0:64, 64:80], blk_excl[0:64, :], ALU.add).then_inc(s_branch, 1)
                dve.wait_ge(s_branch, 1)
                order(red(col[0:64, 11:12], imp, AX.X, ALU.min))
                order(ts(eq, imp, col[0:64, 11:12], None, ALU.is_equal))
                order(tt(key, eq, blk_rank[0:64, :], ALU.mult))
                order(red(col[0:64, 12:13], key, AX.X, ALU.max))
                order(ts(drop_neg[0:64, :], key, col[0:64, 12:13], NEG, ALU.is_equal, ALU.mult))
                yield 5
                for kind, nj in enumerate((8, 4)):
                    N = nj * P
                    yield 6 + 3 * kind
                    dve.wait_ge(s_sc_done, 2 + kind)
                    for cc in range(nj // 4):
                        if kind == 0:
                            v = "p (j y x) -> p j y x"
                            ins = tt(s_scores[0:64, cc * 512:(cc + 1) * 512].rearrange(v, j=4, y=16),
                                     banks[4 + cc][0:64, :].rearrange(v, j=4, y=16),
                                     drop_neg[0:64, :].unsqueeze(1).unsqueeze(3).broadcast_to((64, 4, 16, 8)), ALU.add)
                        else:
                            ins = dve.tensor_copy(s_scores[0:64, 0:512], banks[4][0:64, :])
                    order(ins)
                    if kind == 1:
                        order(ts(s_scores[0:64, 0:1], s_scores[0:64, 0:1], NEG, None, ALU.add))
                    order(dve.tensor_tensor_reduce(out=row(S_U), in0=row(S_NQ), in1=row((S_SK, S_WK)[kind]), scale=0.125,
                                                   scalar=0.0, op0=ALU.mult, op1=ALU.add,
                                                   accum_out=s_scores[0:64, N:N + 1]))
                    red(neg_max[0:64, 1 + kind:2 + kind], s_scores[0:64, 0:N + 1], AX.X, ALU.max, negate=True
                        ).then_inc(s_max, 1)
                    yield 7 + 3 * kind
                    dve.wait_ge(s_exp, 2 + kind)
                    order(dve.reciprocal(col[0:64, 13:14], exp_sum[0:64, 0, 1 + kind:2 + kind]))
                    order(tt(col[0:64, 13:14], col[0:64, 13:14], gate[0:64, 1 + kind:2 + kind], ALU.mult))
                    dve.wait_ge(s_o_done, 2 + kind)
                    order(stt(out=s_o[0:64, 1, :], in0=row((S_SV, S_WV)[kind]), scalar=s_probs[0:64, N:N + 1],
                              in1=banks[3][0:64, 0:64], op0=ALU.mult, op1=ALU.add))
                    stt(out=s_o[0:64, 3, :], in0=s_o[0:64, 1, :], scalar=col[0:64, 13:14], in1=s_o[0:64, 3, :],
                        op0=ALU.mult, op1=ALU.add).then_inc(s_branch, 1)
                    dve.wait_ge(s_branch, 2 + kind)
                    yield 8 + 3 * kind
                q_d = row(S_RQ).unsqueeze(2).broadcast_to((64, HD, HD))
                k_d = row(S_RK).unsqueeze(2).broadcast_to((64, HD, HD))
                v_e = row(S_RV).unsqueeze(1).broadcast_to((64, HD, HD))
                dve.wait_ge(s_state_in, 16)
                order(tt(s_prod[0:64], s_state[0:64], q_d, ALU.mult))
                yield 12
                order(red(row(S_Y), s_prod[0:64].rearrange("p d e -> p e d"), AX.X, ALU.add))
                order(ts(row(S_Y), row(S_Y), gamma1[0:64, :], None, ALU.mult))
                order(dve.tensor_tensor_reduce(out=row(S_U), in0=row(S_RQ), in1=row(S_RK), scale=1.0, scalar=0.0,
                                               op0=ALU.mult, op1=ALU.add, accum_out=col[0:64, 8:9]))
                order(stt(out=row(S_Y), in0=row(S_RV), scalar=col[0:64, 8:9], in1=row(S_Y), op0=ALU.mult, op1=ALU.add))
                yield 13
                order(tt(s_prod[0:64], k_d, v_e, ALU.mult))
                yield 14
                stt(out=s_state[0:64].rearrange("p d e -> p (d e)"), in0=s_state[0:64].rearrange("p d e -> p (d e)"),
                    scalar=gamma1[0:64, :], in1=s_prod[0:64].rearrange("p d e -> p (d e)"),
                    op0=ALU.mult, op1=ALU.add).then_inc(s_branch, 1)
                y3 = row(S_Y).unsqueeze(1)
                group_norm(y3, row(S_U).unsqueeze(1), col[0:64, 9:10], 64, 1, PT)
                order(tt(row(S_Y), row(S_Y), gn_rows[0:64, :], ALU.mult))
                order(stt(out=row(S_U), in0=row(S_T), scalar=1.0, in1=row(S_RG), op0=ALU.add, op1=ALU.mult))
                stt(out=row(S_Y), in0=row(S_Y), scalar=0.5, in1=row(S_U), op0=ALU.mult, op1=ALU.mult
                    ).then_inc(s_cat_ready, 1)
                yield 16
                residual(back, out_done, out_added, out_bank)
                yield 17
                tile_norms(back, MEM)
                yield 19
                v0 = HM * back.tiles[0]
                mem_max(v0)
                for v in range(v0, v0 + HM):
                    yield 20 + v - v0
                    if v + 1 < v0 + HM:
                        mem_max(v + 1)
                    mem_norm(v, back.m_probs[:, v % 2, :])
                    if v == v0:
                        dve.wait_ge(qm_ready, 2 * HM)
                        dve.wait_ge(own_in, 32)
                        tt(qm_mask.rearrange("p c (h b) -> p c h b", h=HM), own_m.rearrange("p c (h b) -> p c h b", h=HM),
                           back.qT_m[:, :, P:P + DB].unsqueeze(1).broadcast_to((P, 32, HM, DB)), ALU.mult
                           ).then_inc(qmask_ready, 1)
                yield 25
                mem_max(PT * HM, 32, 2)
                yield 26
                mem_norm(PT * HM, ms_probs[0:32, :])
                yield 28
                residual(back, mo_done, mo_added, mo_bank)
                yield 29
                tile_norms(back, FFN)
                yield STEPS_DONE

            def route_head(t, head):
                R = rows_of(t)
                made = [0]

                def step(ins):
                    ins.then_inc(route_step, 1)
                    made[0] += 1

                def step_before(top=False):
                    count = head * ROUTE_STEPS + (ROUTE_STEPS * H * t + made[0])
                    dve.wait_ge(route_step, count)
                    if top and not isinstance(head, int):
                        dve.tensor_copy(waited, eps_col)

                def best16(vals, idx, src):
                    n = src.shape[1]
                    step_before(True)
                    for x in range(n):
                        ins = dve.max(vals[0:R, x, 0:8], src[0:R, x, :])
                    step(ins)
                    yield
                    step_before(True)
                    for x in range(n):
                        dve.max_index(idx[0:R, x, 0:8], vals[0:R, x, 0:8], src[0:R, x, :])
                        ins = dve.match_replace(src[0:R, x, :], vals[0:R, x, 0:8], src[0:R, x, :], -3.0e38)
                    step(ins)
                    yield
                    step_before(True)
                    for x in range(n):
                        ins = dve.max(vals[0:R, x, 8:16], src[0:R, x, :])
                    step(ins)
                    yield
                    step_before(True)
                    for x in range(n):
                        ins = dve.max_index(idx[0:R, x, 8:16], vals[0:R, x, 8:16], src[0:R, x, :])
                    step(ins)
                    yield

                step(dve.tensor_copy(s_head[0:R].rearrange("p x n -> p (x n)"),
                                     s_all[0:R, t % 2, bass.ds(head * 256, 256)]))
                yield
                yield from best16(top_v, top_i, s_head)
                step_before()
                dve.tensor_copy(top_f[0:R], top_i[0:R])
                step(tt(cand[0:R, :].rearrange("p (i j) -> p i j", i=TOPK),
                        top_v[0:R, 0, :].unsqueeze(2).broadcast_to((R, TOPK, TOPK)),
                        top_v[0:R, 1, :].unsqueeze(1).broadcast_to((R, TOPK, TOPK)), ALU.add))
                yield
                yield from best16(head_v.unsqueeze(1), head_i[:, :].unsqueeze(1), cand.unsqueeze(1))
                step_before()
                ts(ab_i[0:R, 0, :], head_i[0:R, :], 4, None, ALU.logical_shift_right)
                step(ts(ab_i[0:R, 1, :], head_i[0:R, :], 15, None, ALU.bitwise_and))
                yield
                step_before()
                step(dve.tensor_copy(ab_f[0:R], ab_i[0:R]))
                yield
                step_before()
                for x in range(2):
                    ins = tt(onehot[0:R, x], ab_f[0:R, x, :].unsqueeze(2).broadcast_to((R, TOPK, TOPK)),
                             iota16[0:R].unsqueeze(1).broadcast_to((R, TOPK, TOPK)), ALU.is_equal)
                step(ins)
                yield
                step_before()
                for x in range(2):
                    ins = tt(onehot[0:R, x], onehot[0:R, x], top_f[0:R, x, :].unsqueeze(1).broadcast_to((R, TOPK, TOPK)),
                             ALU.mult)
                step(ins)
                yield
                step_before()
                step(red(pick[0:R], onehot[0:R], AX.X, ALU.add))
                yield
                step_before()
                step(stt(out=pick[0:R, 0, :], in0=pick[0:R, 0, :], scalar=float(NKEY), in1=pick[0:R, 1, :],
                         op0=ALU.mult, op1=ALU.add))
                assert made[0] == ROUTE_STEPS
                yield
                step_before()
                dve.tensor_copy(best_v[0:R, t % 2, bass.ds(head * TOPK, TOPK)], head_v[0:R, :])
                experts = expert[:, t, :] if t < PT else expert_f
                dve.tensor_copy(experts[0:R, bass.ds(head * TOPK, TOPK)], pick[0:R, 0, :]).then_inc(routed, 1)

            def gates_shifted(t):
                R = rows_of(t)
                b3 = best_v[0:R, t % 2, :].rearrange("p (h k) -> p h k", h=H)
                tt(heads(best_e[0:R, :]), b3, b3[:, :, 0:1].broadcast_to((R, H, TOPK)), ALU.subtract
                   ).then_inc(best_shift, 1)

            def gates_of(t):
                R = rows_of(t)
                dve.wait_ge(best_exp, t + 1)
                order(red(col[0:R, 16:24], heads(best_e[0:R, :]), AX.X, ALU.add))
                order(dve.reciprocal(col[0:R, 24:32], col[0:R, 16:24]))
                return tt(heads(gate_t[0:R, :]), heads(best_e[0:R, :]), wide(col[0:R, 24:32], R, H, TOPK), ALU.mult)

            def gelu_argument(x, n):
                w = gtmp[:, 0, 0:n]
                order(tt(w, x, x, ALU.mult))
                order(ts(w, w, GELU_A, 1.0, ALU.mult, ALU.add))
                tt(w, w, x, ALU.mult).then_inc(gelu_in, 1)

            def weights(c_out, x, g, n, t):
                dve.wait_ge(gelu_tanh, t + 1)
                order(stt(out=gtmp[:, 1, 0:n], in0=gtmp[:, 0, 0:n], scalar=1.0, in1=x, op0=ALU.add, op1=ALU.mult))
                return stt(out=c_out, in0=gtmp[:, 1, 0:n], scalar=0.5, in1=g, op0=ALU.mult, op1=ALU.mult)

            def final_norm(t):
                R = rows_of(t)
                normed(hn3[:, t, :], h[0:R, t, :], gain[:, 0, :]).then_inc(y_ready, 1)

            V_SLOTS = [k for k in range(RING) if k not in PE_SLOTS]

            def rows16(t, table, i, route=None, steps=None):
                turn0 = (ROWS * t + SLOTS * table) // RING
                mine = [(x, k) for x in range(2) for k in (V_SLOTS if table else range(RING))]
                parts = 0
                for j, (x, k) in enumerate(mine):
                    turn = i * 2 + (turn0 + x + 1)
                    dve.wait_ge(row_in[k], turn * 16)
                    if table:
                        before = mine[j - 1]
                        dve.wait_ge(row_free[before[1]], i * 2 + (turn0 + before[0] + 1 - (2 if j == 0 else 0)))
                        stt(out=h[:, t, :], in0=ring[:, k, :], scalar=coef[:, bass.ds(i * 16 + (x * RING + k), 1)],
                            in1=h[:, t, :], op0=ALU.mult, op1=ALU.add).then_inc(row_free[k], 1)
                    else:
                        r = x * RING + k
                        dve.tensor_tensor_reduce(out=ring[:, k, :], in0=ring[:, k, :], in1=hn3[:, t, :], scale=1.0,
                                                 scalar=0.0, op0=ALU.mult, op1=ALU.add,
                                                 accum_out=act_part[:, r:r + 1]).then_inc(row_free[k], 1)
                    while route is not None and parts * len(mine) < (j + 1) * (ROUTE_STEPS + 1):
                        next(route, None)
                        parts += 1
                    if steps is not None and (j + 1 == len(mine) or mine[j + 1][0] > x):
                        advance(steps, progress(turn - 1))
                if not table:
                    dve.wait_ge(row_free[RING - 1], i * 2 + (turn0 + 2))
                    dve.tensor_copy(act_p[:, bass.ds(i * 16, 16)], act_part).then_inc(act_kept, 1)
                    dve.wait_ge(act_kept, i + (8 * t + 1))

            def add_sum(t):
                dve.wait_ge(row_free[RING - 1], ROWS * (t + 1) // RING)
                dve.wait_ge(row_free[V_SLOTS[-1]], ROWS * (t + 1) // RING)
                for half in range(2):
                    hv = h[:, t, half * 512:(half + 1) * 512]
                    tt(hv, hv, banks[6 + half][:, :], ALU.add).then_inc(sum_added, 1)

            def between_tables(t):
                gates_shifted(t)
                gelu_argument(act_p, SLOTS)
                if t:
                    add_sum(t - 1)
                order(gates_of(t))
                weights(coef, act_p, gate_t, SLOTS, t).then_inc(coef_ready, 1)
                dve.wait_ge(coef_ready, t + 1)

            dve.wait_ge(ps_ready, 4)
            for _ in route_head(0, 0):
                pass
            steps = background()
            for t in (0, 1):
                for i in range(8):
                    rows16(t, 0, i, route_head(0, i + 1) if t == 0 and i < H - 1 else None, steps)
                between_tables(t)
                dve.wait_ge(ps_ready, 4 * (t + 2))
                if t == 1:
                    dve.wait_ge(scores_moved, 1)
                for i in range(8):
                    rows16(t, 1, i, route_head(t + 1, i), steps)
            dve.wait_ge(fin_gain_in, 16)
            final_norm(0)
            for t in (2, 3):
                with dve.Fori(0, 8) as i:
                    rows16(t, 0, i)
                between_tables(t)
                dve.wait_ge(ps_ready, 4 * (t + 2))
                with dve.Fori(0, 8) as i:
                    rows16(t, 1, i, route_head(t + 1, i))
                final_norm(t - 1)
            add_sum(PT - 1)
            gates_shifted(SAMPLE)
            gates_of(SAMPLE).then_inc(gates_ready, 1)
            dve.wait_ge(rt_done, 1)
            dve.tensor_copy(gate_s, banks[0][:, DB:2 * DB])
            dve.tensor_copy(expert_s[:, :], banks[0][:, 0:DB]).then_inc(routed, 1)
            dve.wait_ge(hns_in, 16)
            for b in range(DB):
                dve.wait_ge(row_in[b], 16 * (ROWS * PT // RING + 1))
                dve.tensor_tensor_reduce(out=ring[:, b, :], in0=ring[:, b, :], in1=hn_s[:, b, :], scale=1.0,
                                         scalar=0.0, op0=ALU.mult, op1=ALU.add,
                                         accum_out=act_p[:, b:b + 1]).then_inc(row_free[b], 1)
            dve.wait_ge(row_free[DB - 1], ROWS * PT // RING + 1)
            gelu_argument(act_p[:, 0:DB], DB)
            order(weights(coef[:, 0:DB], act_p[:, 0:DB], gate_s, DB, PT))
            tt(coef_m, eye8, coef[:, 0:DB].unsqueeze(1).broadcast_to((P, DB, DB)), ALU.mult).then_inc(coef_ready, 1)
            final_norm(PT - 1)
            dve.wait_ge(se_done, 1)
            for half in range(2):
                hv = h[0:DB, SAMPLE, half * 512:(half + 1) * 512]
                ins = tt(hv, hv, banks[6 + half][0:DB, :], ALU.add)
            ins.then_inc(x_done, 1)
            final_norm(SAMPLE)


def shape_constants():
    import numpy as np
    f = np.float32
    c = {}
    c["ident"] = np.eye(P, dtype=f)
    q, k = np.arange(P)[:, None], np.arange(P)[None, :]
    c["tri"] = np.where(k <= q, 0.0, NEG).astype(f)
    lg = np.log(f(1.0) - f(2.0) ** (-5.0 - np.arange(H, dtype=f))).astype(f)
    lg = lg.astype(np.float64)
    diff = (k - q).astype(np.float64)
    c["decay"] = np.where(diff[:, None, :] >= 0, np.exp(lg[None, :, None] * np.maximum(diff, 0)[:, None, :]), 0.0).astype(f)
    i = np.arange(P, dtype=np.float64)[:, None]
    c["xi"] = np.exp(lg[None, :] * (i + 1)).astype(f)
    c["zeta"] = np.exp(lg[None, :] * (P - 1 - i)).astype(f)
    c["g_chunk"] = np.broadcast_to(np.exp(lg * P)[None, :], (P, H)).astype(f)
    c["gamma1"] = np.tile(np.exp(lg), DB)[:, None].astype(f)
    tok = np.arange(SEQ).reshape(PT, P)
    blk_end = np.arange(8) * CMP + CMP - 1
    vis = (blk_end[None, None, :] <= tok[:, :, None]).transpose(1, 0, 2)
    c["cmp_vis"] = vis.astype(f)
    c["cmp_neg"] = np.where(vis, 0.0, NEG).astype(f)
    pos = np.concatenate([tok, np.full((1, P), PAST)]).astype(f).T

    def table(half, theta):
        inv = (f(theta) ** (-np.arange(half, dtype=f) / f(half))).astype(f)
        ang = (pos[:, :, None] * inv).astype(f).astype(np.float64)
        return np.cos(ang), np.sin(ang)
    cos, sin = table(32, 10000.0)
    scale = np.array([1.0, HD ** -0.5])[None, None, :, None]
    c["rot_ret"] = np.stack([cos[:, :, None] * scale, sin[:, :, None] * scale], 2).astype(f)
    cos, sin = table(8, 500000.0)
    c["rot_nsa"] = np.stack([cos, sin], 2).astype(f)
    qs = np.arange(64)
    blk = np.arange(256)
    own = (qs[:, None] // H == blk[None, :] // 32) & (qs[:, None] // R4 % G == blk[None, :] // 2 % G)
    c["own_neg"] = np.where(own, 0.0, NEG).astype(f)
    c["group"] = (qs[:, None] // R4 == qs[None, :] // R4).astype(f)
    c["blk_excl"] = np.broadcast_to(np.where(np.arange(16) == 0, 1e4, 0.0), (64, 16)).astype(f)
    c["blk_rank"] = np.broadcast_to(np.arange(1.0, 17.0), (64, 16)).astype(f)
    p = np.arange(P)
    c["row_add"] = np.stack([p % 4, p % 16, p % 16 + 16], 1).astype(f)
    c["iota16"] = np.broadcast_to(np.arange(16), (P, 16)).astype(f)
    c["eye8"] = np.broadcast_to(np.eye(DB), (P, DB, DB)).astype(f)
    c["own_q"] = np.broadcast_to((np.arange(BG)[:, None] == qs[None, :] // R4)[None], (64, BG, 64)).astype(f)
    c["own_m"] = np.broadcast_to(np.eye(32), (P, 32, 32)).astype(f)
    return {k: np.ascontiguousarray(v) for k, v in c.items()}


_DIRECT = ["x_prompt", "x_sample", "mem_prompt", "state_ret", "cache_cmp_k", "cache_cmp_v", "cache_slc_k",
           "cache_slc_v", "cache_win_k", "cache_win_v", "cache_mem_k", "cache_mem_v", "cmp_w", "peer_subkeys",
           "peer_u", "peer_v", "norm_final_g"]
_LAYER = ["norm_mix_g", "w_in", "w_out", "norm_mem_g", "mem_norm_g", "w_mq", "w_mk", "w_mv", "w_mo", "norm_ffn_g",
          "peer_wq"]
_OUTS = [("y_prompt", (1, SEQ, D)), ("y_sample", (DB, 1, D)), ("p_state", (1, 1, H, HD, HD)),
         ("p_cmp_k", (1, 1, PT, G, P, HD)), ("p_cmp_v", (1, 1, PT, G, P, HD)),
         ("p_slc_k", (1, 1, PT, G, P, HD)), ("p_slc_v", (1, 1, PT, G, P, HD)),
         ("p_win_k", (1, 1, G, 512, HD)), ("p_win_v", (1, 1, G, 512, HD)),
         ("p_mem_k", (1, 1, NMEM, HM, HDM)), ("p_mem_v", (1, 1, NMEM, HM, HDM)),
         ("s_state", (1, DB, H, HD, HD)),
         ("s_cmp_k", (1, DB, G, 1, HD)), ("s_cmp_v", (1, DB, G, 1, HD)),
         ("s_slc_k", (1, DB, G, 1, HD)), ("s_slc_v", (1, DB, G, 1, HD)),
         ("s_win_k", (1, DB, G, 512, HD)), ("s_win_v", (1, DB, G, 512, HD))]


def kernel(**inputs):
    import numpy as np
    import concourse.bacc as bacc
    from concourse.bass_utils import run_bass_kernel_spmd

    arrays = {}
    for name in _DIRECT:
        arrays[name] = np.ascontiguousarray(inputs[name])
    for name in _LAYER:
        arrays[name] = np.ascontiguousarray(inputs[name])[0]
    table = np.asarray(inputs["page_table"]).astype(np.int32)
    arrays["page_rows"] = np.concatenate([np.repeat(table.reshape(2, 32), 4, axis=1).T,
                                          np.repeat(table.T, 16, axis=0)], axis=1)
    gn = np.asarray(inputs["ret_gn_g"])[0]
    consts = shape_constants()
    consts["gn_gain"] = np.broadcast_to(gn[None, :], (P, 512))
    consts["gn_rows"] = np.tile(gn.reshape(H, HD), (DB, 1))
    consts["cmp_bv"] = np.broadcast_to(np.asarray(inputs["cmp_b"])[0, 1][None, :], (P, HD))
    consts["cmp_bk"] = np.asarray(inputs["cmp_b"])[0, 0][:, None]

    nc = bacc.Bacc("TRN2", target_bir_lowering=False, num_devices=1)

    def declare(group, prefix):
        aps = {}
        for name, value in group.items():
            value = np.ascontiguousarray(value)
            feed[prefix + name] = value
            aps[name] = nc.dram_tensor(prefix + name, value.shape, mybir.dt.from_np(value.dtype),
                                       kind="ExternalInput").ap()
        return aps

    feed = {}
    a = declare(arrays, "in_")
    c = declare(consts, "const_")
    out = {name: nc.dram_tensor("out_" + name, shape, F32, kind="ExternalOutput").ap() for name, shape in _OUTS}
    trunk_kernel(nc, a, c, out)
    r = run_bass_kernel_spmd(nc, [feed], core_ids=[0])
    return tuple(r.results[0]["out_" + name] for name, _ in _OUTS)
```
